# Optimizing a Trainium2 kernel written in Bass

```python
import math
import jax
import jax.numpy as jnp
from jax import lax
import numpy as np

D_MODEL = 1024
BATCH = 1
SEQ = 512
DEPTH = 2

N_A_LAYERS = DEPTH // 2
N_B_LAYERS = DEPTH - N_A_LAYERS
NORM_EPS = 1e-6

RWKV_HEAD = 64
RWKV_HEADS = D_MODEL // RWKV_HEAD
DECAY_LORA = max(32, int(round(1.8 * (D_MODEL ** 0.5) / 32)) * 32)
AAA_LORA = max(32, int(round(1.8 * (D_MODEL ** 0.5) / 32)) * 32)
GATE_LORA = max(32, int(round(0.6 * (D_MODEL ** 0.8) / 32)) * 32)
GN_EPS = RWKV_HEAD * 1e-5
N_SHIFT_MIX = 6

DIL_PATTERNS = ((128, 1), (512, 4), (2048, 16))
N_DIL_GROUPS = len(DIL_PATTERNS)
DIL_HEADS = 8
DIL_HEAD_DIM = 64
Q_WIDTH = N_DIL_GROUPS * DIL_HEADS * DIL_HEAD_DIM
ATTN_OUT_WIDTH = DIL_HEADS * DIL_HEAD_DIM

N_EXPERT_GROUPS = 4
EXPERTS_PER_GROUP = 4
N_EXPERTS = N_EXPERT_GROUPS * EXPERTS_PER_GROUP
TOP_K_INNER = 2
EXPERT_HIDDEN = D_MODEL // 2

kernel_name = "yoco_rwkv7_dilated_hmoe"

def rmsnorm(x, g):
    xf = x.astype(jnp.float32)
    y = xf * lax.rsqrt(jnp.mean(xf * xf, axis=-1, keepdims=True) + NORM_EPS)
    return y.astype(x.dtype) * g

def rwkv7_time_mix(x, mu, w_r, w_k, w_v, w0, w1, w2, a0, a1, a2, g1, g2,
                   k_k, k_a, r_k, ln_w, ln_b, w_o):
    bsz, seq, d = x.shape
    f32 = jnp.float32
    xx = jnp.pad(x, ((0, 0), (1, 0), (0, 0)))[:, :-1] - x
    xr, xw, xk, xv, xa, xg = [x + xx * mu[i] for i in range(N_SHIFT_MIX)]
    r = xr @ w_r
    k = xk @ w_k
    v = xv @ w_v
    w_log = -jax.nn.softplus(-(w0 + jnp.tanh(xw @ w1) @ w2)) - 0.5
    a = jax.nn.sigmoid(a0 + (xa @ a1) @ a2)
    g = jax.nn.sigmoid(xg @ g1) @ g2

    def heads(t):
        return t.astype(f32).reshape(bsz, seq, RWKV_HEADS, RWKV_HEAD)

    r, k, v, a, w_log = heads(r), heads(k), heads(v), heads(a), heads(w_log)
    k_k_h = k_k.astype(f32).reshape(RWKV_HEADS, RWKV_HEAD)
    k_a_h = k_a.astype(f32).reshape(RWKV_HEADS, RWKV_HEAD)
    kk = k * k_k_h
    kk = kk / jnp.maximum(jnp.sqrt(jnp.sum(kk * kk, axis=-1, keepdims=True)), 1e-12)
    k = k * (1.0 + (a - 1.0) * k_a_h)
    decay = jnp.exp(-jnp.exp(w_log))
    b = kk * a

    def step(state, inp):
        r_t, dec_t, k_t, v_t, kk_t, b_t = inp
        sa = jnp.einsum("bhvk,bhk->bhv", state, kk_t)
        state = (state * dec_t[:, :, None, :]
                 - sa[..., None] * b_t[:, :, None, :]
                 + v_t[..., None] * k_t[:, :, None, :])
        y_t = jnp.einsum("bhvk,bhk->bhv", state, r_t)
        return state, y_t

    tm = lambda t: jnp.moveaxis(t, 1, 0)
    state0 = jnp.zeros((bsz, RWKV_HEADS, RWKV_HEAD, RWKV_HEAD), f32)
    _, y = lax.scan(step, state0, (tm(r), tm(decay), tm(k), tm(v), tm(kk), tm(b)))
    y = jnp.moveaxis(y, 0, 1)
    mean = jnp.mean(y, axis=-1, keepdims=True)
    var = jnp.mean(jnp.square(y - mean), axis=-1, keepdims=True)
    y = ((y - mean) * lax.rsqrt(var + GN_EPS)).reshape(bsz, seq, d)
    y = y * ln_w.astype(f32) + ln_b.astype(f32)
    bonus = jnp.sum(r * k * r_k.astype(f32), axis=-1, keepdims=True) * v
    y = y + bonus.reshape(bsz, seq, d)
    return (y * g.astype(f32)).astype(x.dtype) @ w_o

def dilated_window_group(q, k, v, window, dilation):
    bsz, seq, nh, hd = q.shape
    n_keys = window // dilation
    span = dilation * n_keys
    s_pad = -(-seq // span) * span
    sub_len = s_pad // dilation
    n_blk = sub_len // n_keys
    scale = 1.0 / math.sqrt(hd)

    def to_sub(t):
        t = jnp.pad(t, ((0, 0), (0, s_pad - seq), (0, 0), (0, 0)))
        t = jnp.moveaxis(t.reshape(bsz, sub_len, dilation, nh, hd), 2, 1)
        return t.reshape(bsz, dilation, n_blk, n_keys, nh, hd)

    def with_prev(t):
        prev = jnp.pad(t, ((0, 0), (0, 0), (1, 0), (0, 0), (0, 0), (0, 0)))[:, :, :-1]
        return jnp.concatenate([prev, t], axis=3)

    qb = to_sub(q)
    kc = with_prev(to_sub(k))
    vc = with_prev(to_sub(v))
    s = jnp.einsum("brnqhd,brnkhd->brnhqk", qb, kc,
                   preferred_element_type=jnp.float32) * scale
    q_loc = jnp.arange(n_keys)[:, None]
    k_loc = jnp.arange(2 * n_keys)[None, :]
    band = (k_loc >= q_loc) & (k_loc <= q_loc + n_keys)
    not_before_start = (jnp.arange(n_blk)[:, None] > 0) | (jnp.arange(2 * n_keys)[None, :] >= n_keys)
    mask = band[None, :, :] & not_before_start[:, None, :]
    s = jnp.where(mask[None, None, :, None, :, :], s, jnp.finfo(jnp.float32).min)
    m = jnp.max(s, axis=-1, keepdims=True)
    p = jnp.exp(s - m)
    l = jnp.sum(p, axis=-1, keepdims=True)
    o = jnp.einsum("brnhqk,brnkhd->brnqhd", p / l, vc.astype(jnp.float32))
    lse = (m + jnp.log(l))[..., 0]
    o = jnp.moveaxis(o.reshape(bsz, dilation, sub_len, nh, hd), 1, 2)
    o = o.reshape(bsz, s_pad, nh, hd)[:, :seq]
    lse = jnp.transpose(lse, (0, 1, 2, 4, 3)).reshape(bsz, dilation, sub_len, nh)
    lse = jnp.moveaxis(lse, 1, 2).reshape(bsz, s_pad, nh)[:, :seq]
    return o, lse

def dilated_attention(xn, k_sh, v_sh, w_q, w_o):
    bsz, seq, _ = xn.shape
    q = (xn @ w_q).reshape(bsz, seq, N_DIL_GROUPS, DIL_HEADS, DIL_HEAD_DIM)
    outs, lses = [], []
    for gi, (window, dilation) in enumerate(DIL_PATTERNS):
        o, lse = dilated_window_group(q[:, :, gi], k_sh[:, :, gi], v_sh[:, :, gi], window, dilation)
        outs.append(o)
        lses.append(lse)
    alpha = jax.nn.softmax(jnp.stack(lses, axis=0), axis=0)
    o = jnp.sum(alpha[..., None] * jnp.stack(outs, axis=0), axis=0)
    return o.reshape(bsz, seq, ATTN_OUT_WIDTH).astype(xn.dtype) @ w_o

def hier_moe(x, w_grp, b_grp, w_exp, b_exp, w_gate, w_up, w_down):
    f32 = jnp.float32
    bsz, seq, d = x.shape
    t = x.reshape(bsz * seq, d)
    n_tok = t.shape[0]
    grp_logits = (t @ w_grp).astype(f32) + b_grp.astype(f32)
    grp_prob = jax.nn.softmax(grp_logits, axis=-1)
    grp = jnp.argmax(grp_logits, axis=-1)
    p_grp = jnp.take_along_axis(grp_prob, grp[:, None], axis=-1)
    exp_logits = ((t @ w_exp).astype(f32) + b_exp.astype(f32)).reshape(
        n_tok, N_EXPERT_GROUPS, EXPERTS_PER_GROUP)
    sel = jnp.take_along_axis(exp_logits, grp[:, None, None], axis=1)[:, 0]
    top_v, top_i = lax.top_k(sel, TOP_K_INNER)
    top_w = jax.nn.softmax(top_v, axis=-1)
    within = jnp.sum(jax.nn.one_hot(top_i, EXPERTS_PER_GROUP, dtype=f32) * top_w[..., None], axis=1)
    gate = (jax.nn.one_hot(grp, N_EXPERT_GROUPS, dtype=f32)[:, :, None]
            * within[:, None, :] * p_grp[:, :, None]).reshape(n_tok, N_EXPERTS).astype(x.dtype)
    y = jnp.zeros_like(t)
    for e in range(N_EXPERTS):
        hdn = jax.nn.silu(t @ w_gate[e]) * (t @ w_up[e])
        y = y + gate[:, e:e + 1] * (hdn @ w_down[e])
    return y.reshape(bsz, seq, d)

def setup_inputs(seed: int = 0) -> dict:
    key = jax.random.key(seed)
    ks = iter(jax.random.split(key, 64))
    f32 = jnp.float32
    D = D_MODEL

    def nrm(shape, scale):
        return jax.random.normal(next(ks), shape, f32) * scale

    def unif(shape, lo, hi):
        return jax.random.uniform(next(ks), shape, f32, minval=lo, maxval=hi)

    NA, NB = N_A_LAYERS, N_B_LAYERS
    F = EXPERT_HIDDEN
    return {
        "x": nrm((BATCH, SEQ, D), 1.0),
        "norm_mix_g": 1.0 + nrm((DEPTH, D), 0.02),
        "norm_ffn_g": 1.0 + nrm((DEPTH, D), 0.02),
        "rwkv_mu": unif((NA, N_SHIFT_MIX, D), 0.0, 1.0),
        "rwkv_w_r": nrm((NA, D, D), D ** -0.5),
        "rwkv_w_k": nrm((NA, D, D), D ** -0.5),
        "rwkv_w_v": nrm((NA, D, D), D ** -0.5),
        "rwkv_w0": unif((NA, D), -4.0, 1.0),
        "rwkv_w1": nrm((NA, D, DECAY_LORA), D ** -0.5),
        "rwkv_w2": nrm((NA, DECAY_LORA, D), 0.1 * DECAY_LORA ** -0.5),
        "rwkv_a0": nrm((NA, D), 0.1),
        "rwkv_a1": nrm((NA, D, AAA_LORA), D ** -0.5),
        "rwkv_a2": nrm((NA, AAA_LORA, D), 0.1 * AAA_LORA ** -0.5),
        "rwkv_g1": nrm((NA, D, GATE_LORA), D ** -0.5),
        "rwkv_g2": nrm((NA, GATE_LORA, D), GATE_LORA ** -0.5),
        "rwkv_k_k": 0.85 + nrm((NA, D), 0.02),
        "rwkv_k_a": 1.0 + nrm((NA, D), 0.02),
        "rwkv_r_k": nrm((NA, RWKV_HEADS, RWKV_HEAD), 0.1),
        "rwkv_ln_w": 1.0 + nrm((NA, D), 0.02),
        "rwkv_ln_b": nrm((NA, D), 0.02),
        "rwkv_w_o": nrm((NA, D, D), D ** -0.5),
        "kv_norm_g": 1.0 + nrm((D,), 0.02),
        "w_kv": nrm((D, 2 * Q_WIDTH), D ** -0.5),
        "attn_w_q": nrm((NB, D, Q_WIDTH), D ** -0.5),
        "attn_w_o": nrm((NB, ATTN_OUT_WIDTH, D), ATTN_OUT_WIDTH ** -0.5),
        "moe_w_grp": nrm((DEPTH, D, N_EXPERT_GROUPS), D ** -0.5),
        "moe_b_grp": nrm((DEPTH, N_EXPERT_GROUPS), 0.01),
        "moe_w_exp": nrm((DEPTH, D, N_EXPERTS), D ** -0.5),
        "moe_b_exp": nrm((DEPTH, N_EXPERTS), 0.01),
        "moe_w_gate": nrm((DEPTH, N_EXPERTS, D, F), D ** -0.5),
        "moe_w_up": nrm((DEPTH, N_EXPERTS, D, F), D ** -0.5),
        "moe_w_down": nrm((DEPTH, N_EXPERTS, F, D), F ** -0.5),
        "final_norm_g": 1.0 + nrm((D,), 0.02),
    }

def reference(x, norm_mix_g, norm_ffn_g, rwkv_mu, rwkv_w_r, rwkv_w_k, rwkv_w_v,
              rwkv_w0, rwkv_w1, rwkv_w2, rwkv_a0, rwkv_a1, rwkv_a2, rwkv_g1, rwkv_g2,
              rwkv_k_k, rwkv_k_a, rwkv_r_k, rwkv_ln_w, rwkv_ln_b, rwkv_w_o,
              kv_norm_g, w_kv, attn_w_q, attn_w_o,
              moe_w_grp, moe_b_grp, moe_w_exp, moe_b_exp, moe_w_gate, moe_w_up, moe_w_down,
              final_norm_g):
    bsz, seq, _ = x.shape
    h = x
    k_sh = None
    v_sh = None
    for layer in range(DEPTH):
        xn = rmsnorm(h, norm_mix_g[layer])
        if layer < N_A_LAYERS:
            i = layer
            h = h + rwkv7_time_mix(xn, rwkv_mu[i], rwkv_w_r[i], rwkv_w_k[i], rwkv_w_v[i],
                                   rwkv_w0[i], rwkv_w1[i], rwkv_w2[i],
                                   rwkv_a0[i], rwkv_a1[i], rwkv_a2[i],
                                   rwkv_g1[i], rwkv_g2[i], rwkv_k_k[i], rwkv_k_a[i],
                                   rwkv_r_k[i], rwkv_ln_w[i], rwkv_ln_b[i], rwkv_w_o[i])
        else:
            i = layer - N_A_LAYERS
            h = h + dilated_attention(xn, k_sh, v_sh, attn_w_q[i], attn_w_o[i])
        h = h + hier_moe(rmsnorm(h, norm_ffn_g[layer]), moe_w_grp[layer], moe_b_grp[layer],
                         moe_w_exp[layer], moe_b_exp[layer], moe_w_gate[layer],
                         moe_w_up[layer], moe_w_down[layer])
        if layer == N_A_LAYERS - 1:
            kv = rmsnorm(h, kv_norm_g) @ w_kv
            k_sh = kv[..., :Q_WIDTH].reshape(bsz, seq, N_DIL_GROUPS, DIL_HEADS, DIL_HEAD_DIM)
            v_sh = kv[..., Q_WIDTH:].reshape(bsz, seq, N_DIL_GROUPS, DIL_HEADS, DIL_HEAD_DIM)
    return rmsnorm(h, final_norm_g)


_drawn_inputs = setup_inputs


def setup_inputs(seed=0):
    import zlib

    import numpy as np

    out = dict(_drawn_inputs(seed))
    spreads = {}
    factors = {'rwkv_w1': 4.179,
     'rwkv_w2': 4.622,
     'rwkv_k_k': 3.472,
     'rwkv_k_a': 2.738,
     'kv_norm_g': 8.0,
     'moe_b_grp': 3.224,
     'moe_b_exp': 3.411,
     'final_norm_g': 2.738}
    for name, (base, spread) in spreads.items():
        noise = np.random.default_rng([zlib.crc32(name.encode()), seed]).standard_normal(out[name].shape)
        drawn = base * np.exp(spread * noise) if base else spread * noise
        out[name] = jnp.asarray(drawn.astype(out[name].dtype))
    for name, factor in factors.items():
        out[name] = (out[name] * factor).astype(out[name].dtype)
    return out
```

```python
import concourse.bass as bass
from concourse import mybir
from contextlib import ExitStack

fp32 = mybir.dt.float32
i32 = mybir.dt.int32
ALU = mybir.AluOpType
ACT = mybir.ActivationFunctionType
AX = mybir.AxisListType

P = 128
T = 512
D = 1024
J = T // P
KT = D // P
HD = 64
H = D // HD
LORA = 64
GLORA = 160
C = 64
NC = T // C
SLAB = 4096
NORM_EPS = 1e-6
GN_EPS = HD * 1e-5
DECAY = float(-(2.718281828459045 ** -0.5))

MU, W0, A0, KK_, KA_, RK_, GMIX, GFFN, GKV = 0, 48, 56, 64, 72, 80, 88, 104, 120


class Chain:

    def __init__(self, eng, sem):
        self.eng, self.sem, self.base, self.n = eng, sem, 0, 0

    def inc(self, ins):
        ins.then_inc(self.sem, 1)
        self.n += 1
        return ins

    def wait(self):
        self.eng.wait_ge(self.sem, self.base + self.n)

    def link(self, ins):
        self.inc(ins)
        self.wait()

    def enter(self, i, per):
        self.before, self.per = self.base + self.n, per
        self.base, self.n = i * per + self.before, 0

    def leave(self, times):
        assert self.n == self.per, f"{self.n} signals an iteration, not {self.per}"
        self.base, self.n = self.before + times * self.per, 0


class Scope(ExitStack):

    def __init__(self, nc, stage):
        super().__init__()
        self.nc, self.stage, self.sems = nc, stage + "_", []
        self.callback(self.clear)

    def clear(self):
        if self.sems:
            self.nc.clear_and_free_semaphores(self.sems)
            self.nc.all_engine_barrier()

    def sb(self, name, shape, dt=fp32):
        return self.enter_context(self.nc.sbuf_tensor(self.stage + name, shape, dt))

    def ps(self, name, shape, dt=fp32):
        return self.enter_context(self.nc.psum_tensor(self.stage + name, shape, dt))

    def sem(self, name):
        self.sems.append(self.nc.alloc_semaphore(self.stage + name))
        return self.sems[-1]


def rwkv_project(nc, io, g, rw):
    with Scope(nc, "project") as s:
        xT = s.sb("xT", [P, KT, T + 1])
        xx = s.sb("xx", [P, KT, T])
        xm = [s.sb(f"xm{i}", [P, KT, T]) for i in range(2)]
        ring = [s.sb(f"ring{i}", [P, SLAB]) for i in range(2)]
        lh = s.sb("lora_hidden", [P, 2, T])
        parrow = s.sb("parrow", [P, P])
        ss = s.sb("ss", [P, J])
        rstd = s.sb("rstd", [P, J])
        r, k, w, a = rw["r"], rw["k"], rw["w"], rw["a"]
        flat = lambda t: t[:, :, :].rearrange("p a b -> p (a b)")
        xtok = r[:, :, :].rearrange("p a b -> p (a b)").rearrange("p (j d) -> p j d", j=J)
        xhat = k[:, :, :].rearrange("p a b -> p (a b)").rearrange("p (j d) -> p j d", j=J)
        kf = flat(k)
        rf = flat(r)
        g1 = kf[:, 0:KT * GLORA].rearrange("p (a b) -> p a b", a=KT)
        g2 = kf[:, 1280:1280 + 2 * D].rearrange("p (a b) -> p a b", a=2)
        w1 = rf[:, 0:512].rearrange("p (a b) -> p a b", a=KT)
        a1 = rf[:, 512:1024].rearrange("p (a b) -> p a b", a=KT)
        w2 = rf[0:LORA, 1024:2048]
        a2 = rf[0:LORA, 2048:3072]
        gout = flat(w).rearrange("p (j d) -> p j d", j=J)
        vout = flat(a).rearrange("p (j d) -> p j d", j=J)
        bank = g["bank"]
        x_in, par_in, lora_g, lora_wa = map(s.sem, ["x_in", "par_in", "lora_g", "lora_wa"])
        slab_in = [s.sem(f"slab_in{i}") for i in range(2)]
        sumsq, rms, rstd_ok, xhat_ok = map(s.sem, ["sumsq", "rms", "rstd_ok", "xhat_ok"])
        par_tr, par_ok, tr, ev_t, xx_ok, zero_ok = map(s.sem, ["par_tr", "par_ok", "tr", "ev_t", "xx_ok", "zero_ok"])
        mixed, unit, ev_act, ev_dve, g_stored, v_stored = map(s.sem, ["mixed", "unit", "ev_act", "ev_dve", "g_stored", "v_stored"])

        order = [("g", 5), ("v", 3), ("w", 1), ("a", 4), ("k", 2), ("r", 0)]
        kinds = {"g": "AA" + "VA" * 4, "v": "VA" * 4, "w": "A" + "A" * 8, "a": "V" + "A" * 8, "k": "VA" * 4, "r": "VA" * 4}
        start, n = {}, 0
        for name, _ in order:
            start[name] = n
            n += len(kinds[name])
        allk = "".join(kinds[name] for name, _ in order)

        def evacuated(eng, u):
            eng.wait_ge(ev_act if allk[u] == "A" else ev_dve, allk[:u + 1].count(allk[u]))

        block = s.enter_context(nc.Block())

        @block.sync
        def _(sp):
            sp.dma_start(xtok, io["x"].rearrange("b (j p) d -> p (b j) d", p=P)).then_inc(x_in, 16)
            rows = [(MU, io["rwkv_mu"].rearrange("a m (k c) -> (a m k) c", c=P)), (W0, io["rwkv_w0"].rearrange("a (k c) -> (a k) c", c=P)),
                    (A0, io["rwkv_a0"].rearrange("a (k c) -> (a k) c", c=P)), (KK_, io["rwkv_k_k"].rearrange("a (k c) -> (a k) c", c=P)),
                    (KA_, io["rwkv_k_a"].rearrange("a (k c) -> (a k) c", c=P)),
                    (RK_, io["rwkv_r_k"].rearrange("a (k b) c -> (a k) (b c)", b=2)),
                    (GMIX, io["norm_mix_g"].rearrange("a (k c) -> (a k) c", c=P)),
                    (GFFN, io["norm_ffn_g"].rearrange("a (k c) -> (a k) c", c=P)),
                    (GKV, io["kv_norm_g"].rearrange("(k c) -> k c", c=P))]
            for at, src in rows:
                sp.dma_start(parrow[at:at + src.shape[0], :], src).then_inc(par_in, 16)
            sp.wait_ge(tr, KT)
            sp.dma_start(g1, io["rwkv_g1"][0].rearrange("(k p) n -> p k n", p=P)).then_inc(lora_g, 16)
            sp.dma_start(g2[:, 0, :], io["rwkv_g2"][0, 0:P, :]).then_inc(lora_g, 16)
            sp.dma_start(g2[0:GLORA - P, 1, :], io["rwkv_g2"][0, P:GLORA, :]).then_inc(lora_g, 16)
            sp.dma_start(w1, io["rwkv_w1"][0].rearrange("(k p) n -> p k n", p=P)).then_inc(lora_wa, 16)
            sp.dma_start(a1, io["rwkv_a1"][0].rearrange("(k p) n -> p k n", p=P)).then_inc(lora_wa, 16)
            sp.dma_start(w2, io["rwkv_w2"][0]).then_inc(lora_wa, 16)
            sp.dma_start(a2, io["rwkv_a2"][0]).then_inc(lora_wa, 16)
            for n, (name, half) in enumerate([(x, y) for x in "vkr" for y in range(2)]):
                if n >= 2:
                    pn, ph = "vkr"[(n - 2) // 2], n % 2
                    sp.wait_ge(unit, start[pn] + (8 if ph or pn == "v" else 4))
                sp.dma_start(ring[n % 2][:, :].rearrange("p (k n) -> p k n", k=KT),
                             io["rwkv_w_" + name][0, :, 512 * half:512 * half + 512].rearrange("(k p) n -> p k n", p=P)).then_inc(slab_in[n % 2], 16)
                if n == 1:
                    for j in range(2 * J):
                        if j % 2:
                            evacuated(sp, start["g"] + 2 + j)
                            evacuated(sp, start["g"] + 1 + j)
                            sp.dma_start(io["g_dram"][P * (j // 2):P * (j // 2) + P, :], gout[:, j // 2, :]).then_inc(g_stored, 16)
                if n == 3:
                    for j in range(2 * J):
                        if j % 2:
                            evacuated(sp, start["v"] + j)
                            evacuated(sp, start["v"] + j - 1)
                            sp.dma_start(io["v_dram"][P * (j // 2):P * (j // 2) + P, :], vout[:, j // 2, :]).then_inc(v_stored, 16)
            sp.wait_ge(g_stored, 16 * J)
            sp.wait_ge(v_stored, 16 * J)

        @block.tensor
        def _(pe):
            pe.wait_ge(par_in, 16 * 9)
            nc.tensor.transpose(bank[7][:, 0:P], parrow[:, :], g["ident"][:, :]).then_inc(par_tr, 1)
            pe.wait_ge(xhat_ok, J)
            for kt in range(KT):
                if kt == KT - 1:
                    pe.wait_ge(par_ok, 1)
                for j in range(J):
                    last = nc.tensor.transpose(bank[kt][:, P * j:P * j + P], xhat[:, j, P * kt:P * kt + P], g["ident"][:, :])
                last.then_inc(tr, 1)

            seen = set()

            def begin(u):
                if u >= 8:
                    evacuated(pe, u - 8)
                elif u == 0:
                    pe.wait_ge(ev_t, KT)
                return bank[u % 8]

            for i, (name, mu) in enumerate(order):
                x = xm[i % 2]
                u = start[name]

                def mix(kt):
                    if (i, kt) not in seen:
                        seen.add((i, kt))
                        pe.wait_ge(mixed, KT * i + kt + 1)

                if name == "g":
                    pe.wait_ge(lora_g, 48)
                    for m, (lo, n) in enumerate([(0, P), (P, GLORA - P)]):
                        b = begin(u)
                        for kt in range(KT):
                            mix(kt)
                            last = nc.tensor.matmul(b[0:n, :], g1[:, kt, lo:lo + n], x[:, kt, :], start=kt == 0, stop=kt == KT - 1)
                        last.then_inc(unit, 1)
                        u += 1
                    evacuated(pe, u - 1)
                    evacuated(pe, u - 2)
                    for j in range(J):
                        for half in range(2):
                            b = begin(u)
                            nc.tensor.matmul(b[:, :], lh[:, 0, P * j:P * j + P], g2[:, 0, 512 * half:512 * half + 512], start=True, stop=False)
                            nc.tensor.matmul(b[:, :], lh[0:GLORA - P, 1, P * j:P * j + P], g2[0:GLORA - P, 1, 512 * half:512 * half + 512],
                                             start=False, stop=True).then_inc(unit, 1)
                            u += 1
                elif name == "v":
                    for j in range(J):
                        for half in range(2):
                            b = begin(u)
                            if j == 0:
                                pe.wait_ge(slab_in[half], 16)
                            wv = ring[half][:, :].rearrange("p (k n) -> p k n", k=KT)
                            for kt in range(KT):
                                mix(kt)
                                last = nc.tensor.matmul(b[:, :], x[:, kt, P * j:P * j + P], wv[:, kt, :], start=kt == 0, stop=kt == KT - 1)
                            last.then_inc(unit, 1)
                            u += 1
                elif name in "wa":
                    if name == "w":
                        pe.wait_ge(lora_wa, 64)
                    l1, l2 = (w1, w2) if name == "w" else (a1, a2)
                    b = begin(u)
                    for kt in range(KT):
                        mix(kt)
                        last = nc.tensor.matmul(b[0:LORA, :], l1[:, kt, :], x[:, kt, :], start=kt == 0, stop=kt == KT - 1)
                    last.then_inc(unit, 1)
                    evacuated(pe, u)
                    u += 1
                    hid = lh[0:LORA, 0 if name == "w" else 1, :]
                    for m in range(KT):
                        b = begin(u)
                        nc.tensor.matmul(b[:, :], l2[:, P * m:P * m + P], hid, start=True, stop=True).then_inc(unit, 1)
                        u += 1
                else:
                    for m in range(KT):
                        b = begin(u)
                        half = m // 4
                        if m % 4 == 0:
                            pe.wait_ge(slab_in[half], 32 if name == "k" else 48)
                        wm = ring[half][:, :].rearrange("p (k n) -> p k n", k=KT)
                        for kt in range(KT):
                            mix(kt)
                            last = nc.tensor.matmul(b[:, :], wm[:, kt, P * (m % 4):P * (m % 4) + P], x[:, kt, :], start=kt == 0, stop=kt == KT - 1)
                        last.then_inc(unit, 1)
                        u += 1

        def evacuate(eng, who):
            for name, _ in order:
                for i, kind in enumerate(kinds[name]):
                    u = start[name] + i
                    if kind != who:
                        if kind == "A" and name == "w" and i == 0 and who == "V":
                            pass
                        continue
                    yield name, i, u

        def move(eng, who, name, i, u):
            b = bank[u % 8]
            eng.wait_ge(unit, u + 1)
            if name == "g" and i < 2:
                n = P if i == 0 else GLORA - P
                return nc.scalar.activation(lh[0:n, i, :], b[0:n, :], ACT.Sigmoid)
            if name == "w" and i == 0:
                return nc.scalar.activation(lh[0:LORA, 0, :], b[0:LORA, :], ACT.Tanh)
            if name == "a" and i == 0:
                return nc.vector.tensor_copy(lh[0:LORA, 1, :], b[0:LORA, :])
            if name == "w":
                if i == 1:
                    eng.wait_ge(g_stored, 16 * J)
                return nc.scalar.activation(w[:, i - 1, :], b[:, :], ACT.Sigmoid, bias=g["par"][:, W0 + i - 1:W0 + i])
            if name == "a":
                if i == 1:
                    eng.wait_ge(v_stored, 16 * J)
                return nc.scalar.activation(a[:, i - 1, :], b[:, :], ACT.Sigmoid, bias=g["par"][:, A0 + i - 1:A0 + i])
            if name == "g":
                out = gout[:, (i - 2) // 2, 512 * (i % 2):512 * (i % 2) + 512]
            elif name == "v":
                out = vout[:, i // 2, 512 * (i % 2):512 * (i % 2) + 512]
            else:
                out = (k if name == "k" else r)[:, i, :]
            if who == "A":
                return nc.scalar.activation(out, b[:, :], ACT.Copy)
            return nc.vector.tensor_copy(out, b[:, :])

        @block.scalar
        def _(act):
            act.wait_ge(x_in, 16)
            for j in range(J):
                nc.scalar.activation(xx[:, 0:2, :].rearrange("p a b -> p (a b)"), xtok[:, j, :], ACT.Square, accum_out=ss[:, j:j + 1]).then_inc(sumsq, 1)
                act.wait_ge(sumsq, j + 1)
            nc.scalar.activation(ss[:, :], ss[:, :], ACT.Sqrt, scale=1.0 / D, bias=g["eps"][:, 0:1]).then_inc(rms, 1)
            act.wait_ge(par_ok, 1)
            for kt in range(0, KT, 2):
                act.wait_ge(tr, kt + 1)
                nc.scalar.activation(xT[:, kt, 1:T + 1], bank[kt][:, :], ACT.Copy, scale=g["par"][:, GMIX + kt:GMIX + kt + 1]).then_inc(ev_t, 1)
            for name, i, u in evacuate(act, "A"):
                if name == "k" and i == 1 or name == "r" and i == 1:
                    act.wait_ge(unit, start[name])
                move(act, "A", name, i, u).then_inc(ev_act, 1)

        @block.vector
        def _(dve):
            dve.wait_ge(par_tr, 1)
            nc.vector.tensor_copy(g["par"][:, :], bank[7][:, 0:P]).then_inc(par_ok, 1)
            nc.vector.memset(xT[:, :, 0:1], 0.0).then_inc(zero_ok, 1)
            dve.wait_ge(rms, 1)
            nc.vector.reciprocal(rstd[:, :], ss[:, :]).then_inc(rstd_ok, 1)
            dve.wait_ge(rstd_ok, 1)
            for j in range(J):
                nc.vector.tensor_scalar(xhat[:, j, :], xtok[:, j, :], rstd[:, j:j + 1], None, ALU.mult).then_inc(xhat_ok, 1)
            dve.wait_ge(par_ok, 1)
            for kt in range(1, KT, 2):
                dve.wait_ge(tr, kt + 1)
                nc.vector.tensor_scalar(xT[:, kt, 1:T + 1], bank[kt][:, :], g["par"][:, GMIX + kt:GMIX + kt + 1], None, ALU.mult).then_inc(ev_t, 1)
            dve.wait_ge(ev_t, KT)
            dve.wait_ge(zero_ok, 1)
            nc.vector.tensor_tensor(xx[:, :, :], xT[:, :, 0:T], xT[:, :, 1:T + 1], ALU.subtract).then_inc(xx_ok, 1)
            dve.wait_ge(xx_ok, 1)
            todo = list(evacuate(dve, "V"))

            def flush(name):
                while todo and todo[0][0] == name:
                    n, i, u = todo.pop(0)
                    move(dve, "V", n, i, u).then_inc(ev_dve, 1)

            for i, (name, mu) in enumerate(order):
                if i >= 2:
                    nm = order[i - 2][0]
                    dve.wait_ge(unit, start[nm] + (len(kinds[nm]) if nm in "vkr" else 2 if nm == "g" else 1))
                for kt in range(KT):
                    nc.vector.scalar_tensor_tensor(out=xm[i % 2][:, kt, :], in0=xx[:, kt, :], scalar=g["par"][:, MU + KT * mu + kt:MU + KT * mu + kt + 1],
                                                   in1=xT[:, kt, 1:T + 1], op0=ALU.mult, op1=ALU.add).then_inc(mixed, 1)
                if i >= 1:
                    flush(order[i - 1][0])
            flush("r")


def rwkv_operands(nc, io, g, rw):
    with Scope(nc, "operands") as s:
        r, k, w, a, n, e1, e2, tmp = (rw[x] for x in ["r", "k", "w", "a", "n", "e1", "e2", "tmp"])
        omk = s.sb("one_minus_ka", [P, KT])
        hsel = s.sb("hsel", [P, KT, 2])
        reset = s.sb("reset", [P, T])
        bank = g["bank"]
        small, n_ok, sq_ok, sum_ok, root_ok, cs_ok, ex_ok = map(s.sem, ["small", "n_ok", "sq_ok", "sum_ok", "root_ok", "cs_ok", "ex_ok"])
        rcp, nn_ok, rate_ok, k_ok, rk_ok, bonus_mm, order, exp_ok = map(s.sem, ["rcp", "nn_ok", "rate_ok", "k_ok", "rk_ok", "bonus_mm", "dve_order", "exp_ok"])
        block = s.enter_context(nc.Block())

        @block.vector
        def _(dve):
            ch = Chain(dve, order)
            par = g["par"]
            ch.inc(nc.vector.memset(reset[:, :], 1.0))
            ch.wait()
            ch.inc(nc.vector.memset(reset[:, 0:T:C], 0.0))
            nc.vector.tensor_scalar(omk[:, :], par[:, KA_:KA_ + KT], -1.0, 1.0, ALU.mult, ALU.add).then_inc(small, 1)
            for i in range(2):
                nc.vector.tensor_scalar(hsel[:, :, i], par[:, RK_:RK_ + KT], g["blockones"][:, HD * i:HD * i + 1], None, ALU.mult).then_inc(small, 1)
            for m in range(KT):
                nc.vector.tensor_scalar(n[:, m, :], k[:, m, :], par[:, KK_ + m:KK_ + m + 1], None, ALU.mult).then_inc(n_ok, 1)
            ch.wait()
            for m in range(KT):
                nc.vector.tensor_tensor_scan(e1[:, m, :], reset[:, :], w[:, m, :], 0.0, ALU.mult, ALU.add).then_inc(cs_ok, 1)
            for m in range(KT):
                dve.wait_ge(cs_ok, m + 1)
                nc.vector.tensor_tensor(w[:, m, :], e1[:, m, :], w[:, m, :], ALU.subtract).then_inc(ex_ok, 1)
            for m in range(KT):
                dve.wait_ge(root_ok, m + 1)
                ch.link(nc.vector.tensor_scalar(e2[:, m, :], e2[:, m, :], 1e-12, None, ALU.max))
                ch.link(nc.vector.reciprocal(e2[:, m, :], e2[:, m, :]))
                nc.vector.tensor_tensor(n[:, m, :], n[:, m, :], e2[:, m, :], ALU.mult).then_inc(nn_ok, 1)
            dve.wait_ge(sum_ok, KT)
            dve.wait_ge(small, 3)
            for m in range(KT):
                nc.vector.tensor_scalar(tmp[:, m, :], a[:, m, :], par[:, KA_ + m:KA_ + m + 1], omk[:, m:m + 1], ALU.mult, ALU.add).then_inc(rate_ok, 1)
            for m in range(KT):
                dve.wait_ge(rate_ok, m + 1)
                dve.wait_ge(n_ok, m + 1)
                nc.vector.tensor_tensor(k[:, m, :], k[:, m, :], tmp[:, m, :], ALU.mult).then_inc(k_ok, 1)
            for m in range(KT):
                dve.wait_ge(k_ok, m + 1)
                nc.vector.tensor_tensor(tmp[:, m, :], r[:, m, :], k[:, m, :], ALU.mult).then_inc(rk_ok, 1)
            for m in range(KT):
                dve.wait_ge(nn_ok, m + 1)
                last = nc.vector.scalar_tensor_tensor(out=a[:, m, :], in0=n[:, m, :], scalar=-1.0, in1=a[:, m, :], op0=ALU.mult, op1=ALU.mult)
            dve.wait_ge(bonus_mm, 1)
            nc.vector.tensor_copy(g["bonus"][:, :, :], bank[0][:, 0:J * H].rearrange("p (j h) -> p j h", j=J))
            dve.wait_ge(exp_ok, 3)
            for i in range(2):
                nc.vector.tensor_copy(rw["pc"][:, :, KT * i:KT * i + KT].rearrange("p c m -> p m c"), e1[HD * i:HD * i + HD, :, C - 1:T:C])

        @block.scalar
        def _(act):
            for m in range(KT):
                act.wait_ge(n_ok, m + 1)
                nc.scalar.activation(tmp[:, m, :], n[:, m, :], ACT.Square).then_inc(sq_ok, 1)
            for m in range(KT):
                act.wait_ge(sum_ok, m + 1)
                nc.scalar.activation(e2[:, m, :], bank[m][:, :], ACT.Sqrt).then_inc(root_ok, 1)
            act.wait_ge(ex_ok, KT)
            nc.scalar.activation(w[:, :, :], w[:, :, :], ACT.Exp, scale=DECAY).then_inc(exp_ok, 1)
            act.wait_ge(nn_ok, KT)
            nc.scalar.activation(e2[:, :, :], e1[:, :, :], ACT.Exp, scale=-DECAY).then_inc(exp_ok, 1)
            act.wait_ge(exp_ok, 2)
            nc.scalar.activation(e1[:, :, :], e1[:, :, :], ACT.Exp, scale=DECAY).then_inc(exp_ok, 1)

        @block.tensor
        def _(pe):
            for m in range(KT):
                pe.wait_ge(sq_ok, m + 1)
                nc.tensor.matmul(bank[m][:, :], g["blockones"][:, :], tmp[:, m, :], start=True, stop=True).then_inc(sum_ok, 1)
            pe.wait_ge(root_ok, KT)
            pe.wait_ge(small, 3)
            for m in range(KT):
                pe.wait_ge(rk_ok, m + 1)
                for j in range(J):
                    last = nc.tensor.matmul(bank[0][:, H * j + 2 * m:H * j + 2 * m + 2], tmp[:, m, j:T:J], hsel[:, m, :], start=True, stop=True)
            last.then_inc(bonus_mm, 1)


def rwkv_chunks(nc, io, g, rw):
    with Scope(nc, "chunks") as s:
        r, k, w, a, n, e1, e2, tmp = (rw[x] for x in ["r", "k", "w", "a", "n", "e1", "e2", "tmp"])
        tf = tmp[:, :, :].rearrange("p a b -> p (a b)")
        AR, BK, BKS = (tf[:, 1024 * i:1024 * i + 1024].rearrange("p (m x t) -> p m x t", m=KT, x=2) for i in range(3))
        first = s.sb("first", [P, H, 2 * C])
        second = s.sb("second", [P, H, 2 * C])
        nq = s.sb("nq", [C, H, 2, C])
        nt = s.sb("nt", [C, H, C])
        sv = s.sb("sv", [P, H, HD])
        zv = s.sb("zv", [P, H, HD])
        decayed = s.sb("decayed", [C, H, HD])
        ybuf = s.sb("ybuf", [P, H, HD])
        bank = g["bank"]
        names = ["ar_ok", "bk_ok", "bks_ok", "lh_ok", "mm_done", "n_done", "t_done", "me_ok", "ne_ok", "te_ok", "q_ok", "lv_done",
                 "nq_ev", "nt_ev", "o1_done", "z_ev", "yp_ev", "fe_done", "fe_ev_d", "fe_ev_a", "o2_done", "so_ev", "dec_ok", "v_in", "y_st"]
        sem = {x: s.sem(x) for x in names}
        setup, turn = s.sem("setup"), s.sem("turn")
        heads = lambda b: slice(b, H, 2)
        NW = [1, 2, 2, 2, 1, 1]
        NQ_PER, NT_PER = 4 * sum(NW), 20
        nq_after = lambda lv, q: 4 * sum(NW[:lv]) + (q + 1) * NW[lv]
        block = s.enter_context(nc.Block())

        def waiter(eng, c):
            return lambda name, per, k: eng.wait_ge(sem[name], c * per + (k + 1))

        @block.sync
        def _(sp):
            for x in ["v_in", "y_st"]:
                sp.sem_inc(sem[x], 1)
            with sp.Fori(0, NC) as c:
                wait = waiter(sp, c)
                wait("o2_done", 2, 0)
                src = io["v_dram"][bass.ds(c * C, C), :]
                sp.dma_start(sv[C:P, :, :].rearrange("p h v -> p (h v)"), src).then_inc(sem["v_in"], 16)
                sp.dma_start(zv[C:P, :, :].rearrange("p h v -> p (h v)"), src).then_inc(sem["v_in"], 16)
                wait("so_ev", 4, 4)
                sp.dma_start(io["y_dram"][bass.ds(c * C, C), :], ybuf[C:P, :, :].rearrange("p h v -> p (h v)")).then_inc(sem["y_st"], 16)
            sp.wait_ge(sem["y_st"], 16 * NC + 1)

        @block.gpsimd
        def _(pool):
            for x in ["ar_ok", "q_ok", "dec_ok"]:
                pool.sem_inc(sem[x], 1)
            nc.gpsimd.memset(sv[0:C, :, :], 0.0).then_inc(setup, 1)
            nc.gpsimd.memset(second[C:P, :, C:2 * C], 0.0).then_inc(setup, 1)
            pool.wait_ge(setup, 2)
            with pool.Fori(0, NC) as c:
                wait = waiter(pool, c)
                wait("t_done", 2, 0)
                wait("lh_ok", 2, 0)
                at = bass.ds(c * C, C)
                nc.gpsimd.tensor_tensor(AR[:, :, 0, :], n[:, :, at], w[:, :, at], ALU.mult).then_inc(sem["ar_ok"], 1)
                nc.gpsimd.tensor_tensor(AR[:, :, 1, :], r[:, :, at], e1[:, :, at], ALU.mult).then_inc(sem["ar_ok"], 1)
                wait("so_ev", 4, 0)
                for i in range(2):
                    nc.gpsimd.tensor_tensor(decayed[:, i::2, :], sv[0:C, i::2, :],
                                            rw["pc"][:, bass.ds(c, 1), KT * i:KT * i + KT].rearrange("p a (m x) -> p (a m) x", x=1).to_broadcast([C, KT, HD]),
                                            ALU.mult).then_inc(sem["dec_ok"], 1)
                for b in range(2):
                    wait("ne_ok", 2, b + 1)
                    nc.gpsimd.tensor_tensor(nq[:, 8 * b:8 * b + 8, 1, :], nq[:, 8 * b:8 * b + 8, 0, :],
                                            g["ident"][0:C, 0:C].rearrange("p (x t) -> p x t", x=1).to_broadcast([C, 8, C]), ALU.add).then_inc(sem["q_ok"], 1)

        @block.scalar
        def _(act):
            for x in ["lh_ok", "te_ok", "nt_ev", "z_ev", "fe_ev_a"]:
                act.sem_inc(sem[x], 1)
            with act.Fori(0, NC) as c:
                wait = waiter(act, c)
                wait("ar_ok", 2, 2)
                wait("o1_done", 2, 0)
                for i in range(2):
                    nc.scalar.activation(first[0:C, 8 * i:8 * i + 8, :], AR[HD * i:HD * i + HD, :, :, :].rearrange("p m x t -> p m (x t)"), ACT.Copy).then_inc(sem["lh_ok"], 1)
                for b in range(2):
                    wait("t_done", 2, b + 1)
                    for rows in (slice(0, C), slice(C, P)):
                        for par in range(2):
                            ins = nc.scalar.activation(second[rows, 8 * par + 4 * b:8 * par + 4 * b + 4, 0:C],
                                                 bank[6 + b][rows, :].rearrange("p (m r k) -> p m r k", m=4, r=2)[:, :, par, :], ACT.Copy)
                        ins.then_inc(sem["te_ok"], 1)
                for lv in range(5):
                    for q in range(4):
                        wait("lv_done", 24, 4 * lv + q + 1)
                        nc.scalar.activation(nt[:, 4 * q:4 * q + 4, :], bank[4 + q][0:C, 0:4 * C].rearrange("p (h t) -> p h t", h=4), ACT.Copy).then_inc(sem["nt_ev"], 1)
                for b in range(2):
                    wait("o1_done", 2, b + 1)
                    nc.scalar.activation(zv[0:C, heads(b), :], bank[4 + b][0:C, :].rearrange("p (h v) -> p h v", h=8), ACT.Copy).then_inc(sem["z_ev"], 1)
                for q in (1, 3):
                    wait("fe_done", 4, q + 1)
                    nc.scalar.activation(second[0:C, 4 * q:4 * q + 4, :], bank[q][0:C, :].rearrange("p (h x) -> p h x", h=4), ACT.Copy).then_inc(sem["fe_ev_a"], 1)

        @block.vector
        def _(dve):
            for x in ["bk_ok", "bks_ok", "me_ok", "ne_ok", "nq_ev", "yp_ev", "fe_ev_d", "so_ev"]:
                dve.sem_inc(sem[x], 1)
            mask = g["chmask"]
            with dve.Fori(0, NC) as c:
                wait = waiter(dve, c)
                at = bass.ds(c * C, C)
                wait("t_done", 2, 0)
                nc.vector.tensor_tensor(BK[:, :, 0, :], a[:, :, at], e2[:, :, at], ALU.mult).then_inc(sem["bk_ok"], 1)
                nc.vector.tensor_tensor(BK[:, :, 1, :], k[:, :, at], e2[:, :, at], ALU.mult).then_inc(sem["bk_ok"], 1)
                last_decay = e1[:, :, bass.ds(c * C + (C - 1), 1)].to_broadcast([P, KT, C])
                for i in range(2):
                    wait("bk_ok", 2, i + 1)
                    nc.vector.tensor_tensor(BKS[:, :, i, :], BK[:, :, i, :], last_decay, ALU.mult).then_inc(sem["bks_ok"], 1)
                for q in range(4):
                    wait("mm_done", 4, q + 1)
                    b = bank[q][:, :].rearrange("p (h x) -> p h x", h=4)
                    hh = slice(4 * q, 4 * q + 4)
                    m3 = lambda rows, lo, hi: mask[rows, lo:hi].rearrange("p (x t) -> p x t", x=1).to_broadcast([C, 4, hi - lo])
                    nc.vector.tensor_tensor(nt[:, hh, :], b[0:C, :, 0:C], m3(slice(0, C), 0, C), ALU.mult).then_inc(sem["me_ok"], 1)
                    nc.vector.tensor_tensor(second[0:C, hh, C:2 * C], b[0:C, :, C:2 * C], m3(slice(0, C), C, 2 * C), ALU.mult).then_inc(sem["me_ok"], 1)
                    nc.vector.tensor_tensor(first[C:P, hh, :], b[C:P, :, :], m3(slice(C, P), 0, 2 * C), ALU.mult).then_inc(sem["me_ok"], 1)
                for b in range(2):
                    wait("n_done", 2, b + 1)
                    nc.vector.tensor_tensor(nq[:, 8 * b:8 * b + 8, 0, :], bank[4 + b][0:C, :].rearrange("p (h t) -> p h t", h=8),
                                            g["lowmask"][:, :].rearrange("p (x t) -> p x t", x=1).to_broadcast([C, 8, C]), ALU.mult).then_inc(sem["ne_ok"], 1)
                for lv in range(6):
                    if lv == 5:
                        wait("y_st", 16, 0)
                        for b in range(2):
                            wait("o1_done", 2, b + 1)
                            nc.vector.tensor_copy(ybuf[C:P, heads(b), :], bank[4 + b][C:P, :].rearrange("p (h v) -> p h v", h=8)).then_inc(sem["yp_ev"], 1)
                    for q in range(4):
                        wait("lv_done", 24, 4 * lv + q + 1)
                        b = bank[q][0:C, :].rearrange("p (h x t) -> p h x t", h=4, x=2)
                        hh = slice(4 * q, 4 * q + 4)
                        if lv == 0:
                            wait("q_ok", 2, q // 2 + 1)
                        if lv < 4:
                            nc.vector.tensor_copy(nq[:, hh, 0, :], b[:, :, 0, :]).then_inc(sem["nq_ev"], 1)
                        if lv > 0:
                            nc.vector.tensor_tensor(nq[:, hh, 1, :], b[:, :, 1, :], nq[:, hh, 1, :], ALU.add).then_inc(sem["nq_ev"], 1)
                for q in (0, 2):
                    wait("fe_done", 4, q + 1)
                    nc.vector.tensor_copy(second[0:C, 4 * q:4 * q + 4, :], bank[q][0:C, :].rearrange("p (h x) -> p h x", h=4)).then_inc(sem["fe_ev_d"], 1)
                wait("dec_ok", 2, 2)
                wait("yp_ev", 2, 2)
                for b in range(2):
                    wait("o2_done", 2, b + 1)
                    o = bank[6 + b][:, :].rearrange("p (h v) -> p h v", h=8)
                    nc.vector.tensor_tensor(sv[0:C, heads(b), :], o[0:C, :, :], decayed[:, heads(b), :], ALU.add).then_inc(sem["so_ev"], 1)
                    nc.vector.tensor_tensor(ybuf[C:P, heads(b), :], o[C:P, :, :], ybuf[C:P, heads(b), :], ALU.add).then_inc(sem["so_ev"], 1)

        @block.tensor
        def _(pe):
            for x in ["mm_done", "n_done", "t_done", "lv_done", "o1_done", "fe_done", "o2_done"]:
                pe.sem_inc(sem[x], 1)
            pe.wait_ge(setup, 2)
            head = lambda place: (2 * place, 0) if place < 8 else (2 * (place - 8) + 1, 1)
            with pe.Fori(0, NC) as c:
                wait = waiter(pe, c)
                wait("ar_ok", 2, 2)
                wait("bk_ok", 2, 2)
                wait("fe_ev_d", 2, 0)
                wait("fe_ev_a", 2, 0)
                for place in range(H):
                    h, par = head(place)
                    rows = slice(HD * par, HD * par + HD)
                    ins = nc.tensor.matmul(bank[place // 4][:, 128 * (place % 4):128 * (place % 4) + 128],
                                           BK[rows, h // 2, :, :].rearrange("p x t -> p (x t)"), AR[rows, h // 2, :, :].rearrange("p x t -> p (x t)"), start=True, stop=True)
                    if place % 4 == 3:
                        ins.then_inc(sem["mm_done"], 1)
                wait("z_ev", 2, 0)
                wait("yp_ev", 2, 0)
                pe.sem_inc(turn, 1)
                for place in range(H):
                    h, par = head(place)
                    rows = slice(HD * par, HD * par + HD)
                    ins = nc.tensor.matmul(bank[4 + place // 8][0:C, C * (place % 8):C * (place % 8) + C],
                                           AR[rows, h // 2, 0, :], BK[rows, h // 2, 0, :], start=True, stop=True)
                    if place % 8 == 7:
                        ins.then_inc(sem["n_done"], 1)
                wait("bks_ok", 2, 2)
                wait("so_ev", 4, 0)
                for m in range(KT):
                    ins = nc.tensor.transpose(bank[6 + m // 4][:, 128 * (m % 4):128 * (m % 4) + 128], BKS[:, m, :, :].rearrange("p x t -> p (x t)"), g["ident"][:, :])
                    if m % 4 == 3:
                        ins.then_inc(sem["t_done"], 1)
                for lv in range(6):
                    if lv == 5:
                        wait("lh_ok", 2, 2)
                        wait("v_in", 32, 32)
                        for b in range(2):
                            wait("nt_ev", NT_PER, 16 + b + 1)
                            for i in range(8):
                                ins = nc.tensor.matmul(bank[4 + b][:, HD * i:HD * i + HD], first[:, 8 * b + i, :], sv[:, 2 * i + b, :], start=True, stop=True)
                            ins.then_inc(sem["o1_done"], 1)
                    for q in range(4):
                        if lv == 0:
                            wait("me_ok", 12, 3 * (q + 1))
                            wait("ne_ok", 2, 2)
                            if q >= 2:
                                wait("te_ok", 4, 2 * (q - 1))
                        else:
                            wait("nq_ev", NQ_PER, nq_after(lv - 1, q))
                            wait("nt_ev", NT_PER, 4 * (lv - 1) + q + 1)
                        if lv == 1:
                            wait("q_ok", 2, q // 2 + 1)
                        pe.sem_inc(turn, 1)
                        for i in range(4):
                            place = 4 * q + i
                            lo, hi = (0, 1) if lv == 0 else (0, 2) if lv < 4 else (1, 2)
                            ins = nc.tensor.matmul(bank[q][0:C, 128 * i + C * lo:128 * i + C * hi], nt[:, place, :],
                                                   nq[:, place, lo:hi, :].rearrange("p x t -> p (x t)"), start=True, stop=True)
                        if lv < 5:
                            for i in range(4):
                                place = 4 * q + i
                                ins = nc.tensor.matmul(bank[4 + q][0:C, C * i:C * i + C], nq[:, place, 0, :], nt[:, place, :], start=True, stop=True)
                        ins.then_inc(sem["lv_done"], 1)
                for q in range(4):
                    wait("nq_ev", NQ_PER, nq_after(5, q))
                    wait("te_ok", 4, 4)
                    pe.sem_inc(turn, 1)
                    for i in range(4):
                        place = 4 * q + i
                        ins = nc.tensor.matmul(bank[q][0:C, 128 * i:128 * i + 128], nq[:, place, 1, :], second[0:C, place, :], start=True, stop=True)
                    ins.then_inc(sem["fe_done"], 1)
                wait("nt_ev", NT_PER, 20)
                for b in range(2):
                    wait("z_ev", 2, b + 1)
                    wait("fe_ev_d", 2, b + 1)
                    wait("fe_ev_a", 2, b + 1)
                    for i in range(8):
                        ins = nc.tensor.matmul(bank[6 + b][:, HD * i:HD * i + HD], second[:, 8 * b + i, :], zv[:, 2 * i + b, :], start=True, stop=True)
                    ins.then_inc(sem["o2_done"], 1)


def rwkv_finish(nc, io, g, rw):
    h = g["h"]
    with Scope(nc, "finish") as s:
        big = lambda x: rw[x][:, :, :].rearrange("p a b -> p (a b)").rearrange("p (j d) -> p j d", j=J)
        y, v, gate, sq, zT = big("r"), big("k"), big("w"), big("a"), rw["n"]
        ring = [rw[x][:, :, :] for x in ["e1", "e2"]]
        lnw, lnb = (rw["tmp"][:, 2 * i:2 * i + 2, :].rearrange("p a b -> p (a b)") for i in range(2))
        mu = s.sb("mu", [P, J, H])
        var = s.sb("var", [P, J, H])
        bank = g["bank"]
        y_in, vg_in, h_in, wo_in, order, mu_ok, cent_ok, sq_ok, var_ok, root_ok = map(
            s.sem, ["y_in", "vg_in", "h_in", "wo_in", "order", "mu_ok", "cent_ok", "sq_ok", "var_ok", "root_ok"])
        rstd_ok, normed, z_ok, tr, ev_a, ev_d, o_done, h_ok, pool_order, ln_in = map(
            s.sem, ["rstd_ok", "normed", "z_ok", "tr", "ev_a", "ev_d", "o_done", "h_ok", "pool_order", "ln_in"])
        wide = lambda t, j: t[:, j, :].rearrange("p (h x) -> p h x", x=1).to_broadcast([P, H, HD])
        split = lambda t, j: t[:, j, :].rearrange("p (h x) -> p h x", h=H)
        block = s.enter_context(nc.Block())

        @block.sync
        def _(sp):
            tiles = lambda d: d.rearrange("(p j) d -> p j d", j=J)
            sp.dma_start(y, tiles(io["y_dram"])).then_inc(y_in, 16)
            sp.dma_start(v, tiles(io["v_dram"])).then_inc(vg_in, 16)
            sp.dma_start(gate, tiles(io["g_dram"])).then_inc(vg_in, 16)
            sp.dma_start(lnw, io["rwkv_ln_w"].to_broadcast([P, D])).then_inc(ln_in, 16)
            sp.dma_start(lnb, io["rwkv_ln_b"].to_broadcast([P, D])).then_inc(ln_in, 16)
            for i in range(2):
                sp.dma_start(ring[i], io["rwkv_w_o"][0, :, 512 * i:512 * i + 512].rearrange("(k p) n -> p k n", p=P)).then_inc(wo_in, 16)
            sp.dma_start(h[:, :, :], tiles(io["x"][0])).then_inc(h_in, 16)

        @block.vector
        def _(dve):
            dve.wait_ge(y_in, 16)
            ch = Chain(dve, order)
            for j in range(J):
                nc.vector.tensor_reduce(out=mu[:, j, :], in_=split(y, j), axis=AX.X, op=ALU.add).then_inc(mu_ok, 1)
            for j in range(J):
                dve.wait_ge(mu_ok, j + 1)
                ch.link(nc.vector.tensor_scalar(mu[:, j, :], mu[:, j, :], 1.0 / HD, None, ALU.mult))
                nc.vector.tensor_tensor(split(y, j), split(y, j), wide(mu, j), ALU.subtract).then_inc(cent_ok, 1)
            dve.wait_ge(vg_in, 32)
            for j in range(J):
                ch.inc(nc.vector.tensor_tensor(split(v, j), split(v, j), wide(g["bonus"], j), ALU.mult))
            for j in range(J):
                dve.wait_ge(sq_ok, j + 1)
                nc.vector.tensor_reduce(out=var[:, j, :], in_=split(sq, j), axis=AX.X, op=ALU.add).then_inc(var_ok, 1)
                dve.wait_ge(root_ok, j + 1)
                nc.vector.reciprocal(var[:, j, :], var[:, j, :]).then_inc(rstd_ok, 1)
            ch.wait()
            for j in range(J):
                dve.wait_ge(normed, j + 1)
                ch.link(nc.vector.tensor_tensor(y[:, j, :], y[:, j, :], v[:, j, :], ALU.add))
                nc.vector.tensor_tensor(y[:, j, :], y[:, j, :], gate[:, j, :], ALU.mult).then_inc(z_ok, 1)
            for kt in range(1, KT, 2):
                dve.wait_ge(tr, kt + 1)
                nc.vector.tensor_copy(zT[:, kt, :], bank[kt][:, :]).then_inc(ev_d, 1)
            dve.wait_ge(h_in, 16)
            for u in range(2 * J):
                dve.wait_ge(o_done, u + 1)
                hh = h[:, u // 2, 512 * (u % 2):512 * (u % 2) + 512]
                nc.vector.tensor_tensor(hh, bank[u][:, :], hh, ALU.add).then_inc(h_ok, 1)

        @block.gpsimd
        def _(pool):
            ch = Chain(pool, pool_order)
            pool.wait_ge(ln_in, 32)
            for j in range(J):
                pool.wait_ge(rstd_ok, j + 1)
                ch.link(nc.gpsimd.tensor_tensor(split(y, j), split(y, j), wide(var, j), ALU.mult))
                ch.link(nc.gpsimd.tensor_tensor(y[:, j, :], y[:, j, :], lnw, ALU.mult))
                nc.gpsimd.tensor_tensor(y[:, j, :], y[:, j, :], lnb, ALU.add).then_inc(normed, 1)

        @block.scalar
        def _(act):
            for j in range(J):
                act.wait_ge(cent_ok, j + 1)
                nc.scalar.activation(sq[:, j, :], y[:, j, :], ACT.Square).then_inc(sq_ok, 1)
            for j in range(J):
                act.wait_ge(var_ok, j + 1)
                nc.scalar.activation(var[:, j, :], var[:, j, :], ACT.Sqrt, scale=1.0 / HD, bias=g["eps"][:, 1:2]).then_inc(root_ok, 1)
            for kt in range(0, KT, 2):
                act.wait_ge(tr, kt + 1)
                nc.scalar.activation(zT[:, kt, :], bank[kt][:, :], ACT.Copy).then_inc(ev_a, 1)

        @block.tensor
        def _(pe):
            pe.wait_ge(z_ok, J)
            for kt in range(KT):
                for j in range(J):
                    last = nc.tensor.transpose(bank[kt][:, P * j:P * j + P], y[:, j, P * kt:P * kt + P], g["ident"][:, :])
                last.then_inc(tr, 1)
            pe.wait_ge(ev_a, KT // 2)
            pe.wait_ge(ev_d, KT // 2)
            pe.wait_ge(wo_in, 32)
            for u in range(2 * J):
                for kt in range(KT):
                    last = nc.tensor.matmul(bank[u][:, :], zT[:, kt, P * (u // 2):P * (u // 2) + P], ring[u % 2][:, kt, :], start=kt == 0, stop=kt == KT - 1)
                last.then_inc(o_done, 1)


def moe(nc, io, g, layer):
    h, bank = g["h"], g["bank"]
    NE, NG, EG = 16, 4, 4
    FH = D // 2
    with Scope(nc, f"moe{layer}") as s:
        xn = s.sb("xn", [P, J, D])
        xnT = s.sb("xnT", [P, KT, T])
        gb = s.sb("gb", [P, D])
        ring = [s.sb(f"ring{i}", [P, SLAB]) for i in range(6)]
        xg = [s.sb(f"xg{i}", [P, D]) for i in range(2)]
        xgT = [s.sb(f"xgT{i}", [P, KT, P]) for i in range(2)]
        sg = s.sb("sg", [P, FH])
        hid = s.sb("hid", [P, FH])
        hidT = s.sb("hidT", [P, FH // P, P])
        yo = [s.sb(f"yo{i}", [P, D]) for i in range(2)]
        wr = s.sb("wr", [P, KT, NG + NE])
        br = s.sb("br", [P, NG + NE])
        ss, rstd = s.sb("ss", [P, J]), s.sb("rstd", [P, J])
        lg = s.sb("logits", [P, J, NG + NE])
        v4 = [s.sb(f"v4_{i}", [P, J]) for i in range(10)]
        v16 = [s.sb(f"v16_{i}", [P, J, 4]) for i in range(7)]
        v64 = [s.sb(f"v64_{i}", [P, J, NG, EG]) for i in range(5)]
        rank = s.sb("rank", [P, J, NE])
        msum = s.sb("msum", [P, NE])
        posf = s.sb("posf", [P, 2, J])
        pos = s.sb("pos", [P, 2, J], i32)
        first_place, later = s.sb("first_place", [P, 2, J]), s.sb("later", [P, 2, J])
        wgt = s.sb("wgt", [P, 2, J])
        zeros = s.sb("zeros", [NE * J, P])
        tokrow = s.sb("tokrow", [NE * J, P])
        idx = s.sb("idx", [P, NE * J], i32)
        idxcol = [s.sb(f"idxcol{i}", [P, 1], i32) for i in range(2)]
        most = s.sb("most", [P, 2])
        mosti = s.sb("mosti", [P, 1], i32)
        par_in, sumsq, rms, rstd_ok, xhat_ok, xn_ok, xn_st, tr, ev_a, ev_d, lg_done, order = map(
            s.sem, ["par_in", "sumsq", "rms", "rstd_ok", "xhat_ok", "xn_ok", "xn_st", "tr", "ev_a", "ev_d", "lg_done", "order"])
        gs_ok, eg_ok, d_ok, e2_ok, ms_ok, rank_done, pos_ok, tok_zero, tok_st, tok_in, tok_tr, idx_ok, zero_ok = map(
            s.sem, ["gs_ok", "eg_ok", "d_ok", "e2_ok", "ms_ok", "rank_done", "pos_ok", "tok_zero", "tok_st", "tok_in", "tok_tr", "idx_ok", "zero_ok"])
        comb_in = [s.sem(f"comb_in{i}") for i in range(J)]
        comb_ok, turn = s.sem("comb_ok"), s.sem("turn")

        def loop_sems(tag, bufs):
            r = {x: s.sem(tag + x) for x in ["slab_used", "xt_done", "xt_a", "xt_d", "g_done", "u_done", "sg_ok", "hid_ok", "ht_done", "ht_ok",
                                             "y_done", "y_a", "y_d", "col_ok"]}
            r["slab_in"] = [s.sem(f"{tag}slab_in{i}") for i in range(3 * bufs)]
            r["xg_in"] = [s.sem(f"{tag}xg_in{i}") for i in range(bufs)]
            r["y_st"] = [s.sem(f"{tag}y_st{i}") for i in range(bufs)]
            return r

        main, more = loop_sems("", 2), loop_sems("more_", 1)
        xn_dram, tok_dram, out_dram = io[f"xn_dram{layer}"], io[f"tok_dram{layer}"], io[f"out_dram{layer}"]
        block = s.enter_context(nc.Block())

        xnT2 = xnT[:, :, :].rearrange("p a b -> p (a b)").rearrange("p (j d) -> p j d", j=J)

        def load_expert(sp, m, e, n, x, bufs):
            for i, name in enumerate(["moe_w_gate", "moe_w_up", "moe_w_down"]):
                sp.wait_ge(m["slab_used"], n * (3 * bufs) + (3 * x + i + 1))
                w = ring[3 * x + i][:, :]
                k = KT if i < 2 else FH // P
                sp.dma_start(w.rearrange("p (k n) -> p k n", k=k),
                             io[name][layer, bass.ds(e, 1), :, :].rearrange("a (k p) n -> p (a k) n", p=P)).then_inc(m["slab_in"][3 * x + i], 16)

        def pe_transposes(pe, m, n, x, bufs, count):
            pe.wait_ge(m["xg_in"][x], n * 16 + 16)
            pe.wait_ge(m["xt_a"], count + 1)
            pe.wait_ge(m["xt_d"], count + 1)
            for kt in range(KT):
                ins = nc.tensor.transpose(bank[kt // 4][:, P * (kt % 4):P * (kt % 4) + P], xg[x][:, P * kt:P * kt + P], g["ident"][:, :])
            ins.then_inc(m["xt_done"], 1)

        def pe_expert(pe, m, n, x, bufs, count, between=None):
            for i, (b, done) in enumerate([(2, "g_done"), (3, "u_done")]):
                w = ring[3 * x + i][:, :].rearrange("p (k n) -> p k n", k=KT)
                pe.wait_ge(m["slab_in"][3 * x + i], n * 16 + 16)
                if i == 0:
                    pe.wait_ge(m["xt_a"], count + 2)
                    pe.wait_ge(m["xt_d"], count + 2)
                    pe.wait_ge(m["sg_ok"], count + 1)
                else:
                    pe.wait_ge(m["hid_ok"], count + 1)
                for kt in range(KT):
                    ins = nc.tensor.matmul(bank[b][:, :], xgT[x][:, kt, :], w[:, kt, :], start=kt == 0, stop=kt == KT - 1)
                ins.then_inc(m[done], 1)
            if between:
                between()
            pe.wait_ge(m["hid_ok"], count + 2)
            pe.wait_ge(m["ht_ok"], count + 1)
            for kt in range(FH // P):
                ins = nc.tensor.transpose(bank[4][:, P * kt:P * kt + P], hid[:, P * kt:P * kt + P], g["ident"][:, :])
            ins.then_inc(m["ht_done"], 1)
            w = ring[3 * x + 2][:, :].rearrange("p (k n) -> p k n", k=FH // P)
            pe.wait_ge(m["slab_in"][3 * x + 2], n * 16 + 16)
            pe.wait_ge(m["ht_ok"], count + 2)
            for half in range(2):
                pe.wait_ge(m["y_a" if half == 0 else "y_d"], count + 1)
                for kt in range(FH // P):
                    ins = nc.tensor.matmul(bank[5 + half][:, :], hidT[:, kt, :], w[:, kt, 512 * half:512 * half + 512], start=kt == 0, stop=kt == FH // P - 1)
                ins.then_inc(m["y_done"], 1)
            pe.wait_ge(m["y_done"], count * 2 + 3)
            pe.sem_inc(m["slab_used"], 3)

        def act_xt(act, m, x, count):
            act.wait_ge(m["xt_done"], count + 2)
            nc.scalar.activation(xgT[x][:, 0:4, :], bank[0][:, :].rearrange("p (k t) -> p k t", k=4), ACT.Copy).then_inc(m["xt_a"], 1)

        def act_expert(act, m, row, n, x, bufs, count, between=None):
            act.wait_ge(m["g_done"], count + 2)
            act.wait_ge(m["hid_ok"], count + 1)
            nc.scalar.activation(sg[:, :], bank[2][:, :], ACT.Silu).then_inc(m["sg_ok"], 1)
            if between:
                between()
            act.wait_ge(m["ht_done"], count + 2)
            nc.scalar.activation(hidT[:, :, :], bank[4][:, :].rearrange("p (k t) -> p k t", k=4), ACT.Copy).then_inc(m["ht_ok"], 1)
            act.wait_ge(m["y_done"], count * 2 + 2)
            act.wait_ge(m["y_st"][x], n * 16 + 1)
            nc.scalar.activation(yo[x][:, 0:512], bank[5][:, :], ACT.Copy).then_inc(m["y_a"], 1)
            act.wait_ge(m["y_a"], count + 2)
            act.wait_ge(m["y_d"], count + 2)
            act.dma_start(out_dram[bass.ds(row, P), :], yo[x][:, :]).then_inc(m["y_st"][x], 16)

        def dve_xt(dve, m, x, count):
            dve.wait_ge(m["xt_done"], count + 2)
            nc.vector.tensor_copy(xgT[x][:, 4:8, :], bank[1][:, :].rearrange("p (k t) -> p k t", k=4)).then_inc(m["xt_d"], 1)

        def dve_expert(dve, m, n, x, bufs, count, between=None):
            dve.wait_ge(m["u_done"], count + 2)
            dve.wait_ge(m["sg_ok"], count + 2)
            dve.wait_ge(m["ht_done"], count + 1)
            nc.vector.tensor_tensor(hid[:, :], bank[3][:, :], sg[:, :], ALU.mult).then_inc(m["hid_ok"], 1)
            if between:
                between()
            dve.wait_ge(m["y_done"], count * 2 + 3)
            dve.wait_ge(m["y_st"][x], n * 16 + 1)
            nc.vector.tensor_copy(yo[x][:, 512:1024], bank[6][:, :]).then_inc(m["y_d"], 1)

        def overflow(eng):
            longest = eng.value_load(mosti[0:1, 0:1], min_val=0, max_val=T)
            return eng.If(longest > P)

        def no_overflow(eng):
            return eng.If(eng.value_load(mosti[0:1, 0:1], min_val=0, max_val=T) < P + 1)

        @block.sync
        def _(sp):
            sp.dma_start(gb[:, :], io["norm_ffn_g"][layer:layer + 1, :].to_broadcast([P, D])).then_inc(par_in, 16)
            sp.dma_start(wr[:, :, 0:NG], io["moe_w_grp"][layer].rearrange("(k p) n -> p k n", p=P)).then_inc(par_in, 16)
            sp.dma_start(wr[:, :, NG:], io["moe_w_exp"][layer].rearrange("(k p) n -> p k n", p=P)).then_inc(par_in, 16)
            sp.dma_start(br[:, 0:NG], io["moe_b_grp"][layer:layer + 1, :].to_broadcast([P, NG])).then_inc(par_in, 16)
            sp.dma_start(br[:, NG:], io["moe_b_exp"][layer:layer + 1, :].to_broadcast([P, NE])).then_inc(par_in, 16)
            sp.wait_ge(zero_ok, 1)
            sp.dma_start(tok_dram.rearrange("(a b) x -> a (b x)", b=P), zeros[:, :]).then_inc(tok_zero, 16)
            sp.sem_inc(main["slab_used"], 6)
            with sp.Fori(0, NE // 2) as i:
                for x in range(2):
                    load_expert(sp, main, i * 2 + x, i, x, 2)
            sp.wait_ge(pos_ok, 2)
            with overflow(sp):
                sp.wait_ge(main["slab_used"], 6 + 3 * NE)
                sp.sem_inc(more["slab_used"], 3)
                with sp.Fori(0, NE) as e:
                    with sp.Fori(1, J) as b:
                        load_expert(sp, more, e, e * (J - 1) + (b - 1), 0, 1)

        @block.gpsimd
        def _(pool):
            nc.gpsimd.memset(zeros[:, :], 0.0).then_inc(zero_ok, 1)
            for x in ["col_ok"]:
                pool.sem_inc(main[x], 1)
            pool.wait_ge(pos_ok, 2)
            pool.wait_ge(tok_zero, 16)
            for k in range(2):
                for j in range(J):
                    pool.indirect_dma_start(tok_dram, bass.IndirectOffsetOnAxis(ap=pos[:, k, j:j + 1], axis=0), g["tokid"][:, j:j + 1], None).then_inc(tok_st, 16)
            pool.wait_ge(tok_st, 16 * 2 * J)
            pool.dma_start(tokrow[:, :], tok_dram.rearrange("(a b) x -> a (b x)", b=P)).then_inc(tok_in, 16)
            pool.wait_ge(idx_ok, 1)
            pool.wait_ge(xn_st, 16)

            def fetch(m, col, x, used, copied):
                pool.wait_ge(m["xt_done"], used)
                nc.gpsimd.tensor_copy(idxcol[x][:, :], idx[:, bass.ds(col, 1)]).then_inc(m["col_ok"], 1)
                pool.wait_ge(m["col_ok"], copied)
                pool.sem_inc(turn, 1)
                pool.indirect_dma_start(xg[x][:, :], None, xn_dram, bass.IndirectOffsetOnAxis(ap=idxcol[x][:, :], axis=0)).then_inc(m["xg_in"][x], 16)

            fetch(main, 0, 0, 1, 2)
            with pool.Fori(0, NE // 2) as i:
                fetch(main, i * 2 + 1, 1, i * 2 + 1, i * 2 + 3)
                fetch(main, i * 2 + 2, 0, i * 2 + 2, i * 2 + 4)
            with overflow(pool):
                pool.sem_inc(more["col_ok"], 1)
                pool.wait_ge(main["xg_in"][0], 16 * (NE // 2 + 1))
                with pool.Fori(0, NE) as e:
                    with pool.Fori(1, J) as b:
                        n = e * (J - 1) + (b - 1)
                        fetch(more, b * NE + e, 0, n + 1, n + 2)
            for x in range(2):
                pool.wait_ge(main["y_st"][x], 16 * (NE // 2) + 1)
            with overflow(pool):
                pool.wait_ge(more["y_st"][0], 16 * NE * (J - 1) + 1)

            def outputs(rows):
                for j in range(J):
                    for k in range(2):
                        dst = (xn if k == 0 else xnT2)[:, j, :]
                        pool.indirect_dma_start(dst, None, rows, bass.IndirectOffsetOnAxis(ap=pos[:, k, j:j + 1], axis=0)).then_inc(comb_in[j], 16)

            with overflow(pool):
                outputs(out_dram)
            with no_overflow(pool):
                outputs(out_dram[0:NE * P, :])
            for j in range(J):
                pool.wait_ge(comb_in[j], 32)

        @block.scalar
        def _(act):
            for x in ["xt_a", "sg_ok", "ht_ok", "y_a"]:
                act.sem_inc(main[x], 1)
            for x in range(2):
                act.sem_inc(main["y_st"][x], 1)
            for j in range(J):
                nc.scalar.activation(yo[0][:, :], h[:, j, :], ACT.Square, accum_out=ss[:, j:j + 1]).then_inc(sumsq, 1)
                act.wait_ge(sumsq, j + 1)
            nc.scalar.activation(ss[:, :], ss[:, :], ACT.Sqrt, scale=1.0 / D, bias=g["eps"][:, 0:1]).then_inc(rms, 1)
            act.wait_ge(xn_ok, J)
            act.dma_start(xn_dram.rearrange("(p j) d -> p j d", j=J), xn[:, :, :]).then_inc(xn_st, 16)
            for kt in range(0, KT, 2):
                act.wait_ge(tr, kt + 1)
                nc.scalar.activation(xnT[:, kt, :], bank[kt][:, :], ACT.Copy).then_inc(ev_a, 1)
            act.wait_ge(gs_ok, 1)
            nc.scalar.activation(v16[0][:, :, :], v16[0][:, :, :], ACT.Exp).then_inc(eg_ok, 1)
            act.wait_ge(d_ok, 1)
            nc.scalar.activation(v4[5][:, :], v4[5][:, :], ACT.Exp).then_inc(e2_ok, 1)
            act.wait_ge(rank_done, 1)
            act_xt(act, main, 0, 0)
            with act.Fori(0, NE // 2) as i:
                for x in range(2):
                    count = i * 2 + x
                    act_expert(act, main, i * (2 * P) + x * P, i, x, 2, count, between=lambda: act_xt(act, main, 1 - x, count + 1))
            act.wait_ge(pos_ok, 2)
            with overflow(act):
                for x in ["xt_a", "sg_ok", "ht_ok", "y_a"]:
                    act.sem_inc(more[x], 1)
                act.sem_inc(more["y_st"][0], 1)
                act.wait_ge(main["y_st"][0], 16 * (NE // 2) + 1)
                with act.Fori(0, NE) as e:
                    with act.Fori(1, J) as b:
                        n = e * (J - 1) + (b - 1)
                        act_xt(act, more, 0, n)
                        act_expert(act, more, b * (NE * P) + e * P, n, 0, 1, n)

        @block.vector
        def _(dve):
            for x in ["xt_d", "hid_ok", "y_d"]:
                dve.sem_inc(main[x], 1)
            dve.wait_ge(rms, 1)
            nc.vector.reciprocal(rstd[:, :], ss[:, :]).then_inc(rstd_ok, 1)
            dve.wait_ge(rstd_ok, 1)
            dve.wait_ge(par_in, 80)
            for j in range(J):
                nc.vector.scalar_tensor_tensor(out=xn[:, j, :], in0=h[:, j, :], scalar=rstd[:, j:j + 1], in1=gb[:, :], op0=ALU.mult, op1=ALU.mult).then_inc(xn_ok, 1)
            for kt in range(1, KT, 2):
                dve.wait_ge(tr, kt + 1)
                nc.vector.tensor_copy(xnT[:, kt, :], bank[kt][:, :]).then_inc(ev_d, 1)
            ch = Chain(dve, order)
            V = nc.vector
            gl = lg[:, :, 0:NG]
            el = lg[:, :, NG:].rearrange("p j (g e) -> p j g e", g=NG)
            over = lambda t: t[:, :].rearrange("p (j x) -> p j x", x=1).to_broadcast([P, J, 4])
            reduce = lambda out, in_, op: ch.link(V.tensor_reduce(out=out, in_=in_, axis=AX.X, op=op))
            tt = lambda out, a, b, op: ch.link(V.tensor_tensor(out, a, b, op))
            dve.wait_ge(lg_done, 1)
            tt(lg[:, :, :], bank[0][:, 0:J * (NG + NE)].rearrange("p (j n) -> p j n", j=J),
               br[:, :].rearrange("p (x n) -> p x n", x=1).to_broadcast([P, J, NG + NE]), ALU.add)
            gm, psum, m1, m2, top, dd = v4[0], v4[1], v4[2], v4[3], v4[4], v4[5]
            reduce(gm[:, :], gl, ALU.max)
            V.tensor_tensor(v16[0][:, :, :], gl, over(gm), ALU.subtract).then_inc(gs_ok, 1)

            def first_equal(out, vals, m):
                tt(out[:, :, :], vals, over(m), ALU.is_equal)
                tt(out[:, :, :], out[:, :, :], g["down4"][:, :].rearrange("p (x n) -> p x n", x=1).to_broadcast([P, J, 4]), ALU.mult)
                reduce(top[:, :], out[:, :, :], ALU.max)
                tt(out[:, :, :], out[:, :, :], over(top), ALU.is_equal)

            og, sel, o1, sel2, o2 = v16[1], v16[2], v16[3], v16[4], v16[5]
            first_equal(og, gl, gm)
            inner = lambda t: t[:, :, :].rearrange("p j (n x) -> p j n x", x=1).to_broadcast([P, J, NG, EG])
            outer = lambda t: t[:, :, :].rearrange("p j (x n) -> p j x n", x=1).to_broadcast([P, J, NG, EG])
            tt(v64[0][:, :, :, :], el, inner(og), ALU.mult)
            reduce(sel[:, :, :], v64[0][:, :, :, :].rearrange("p j g e -> p j e g"), ALU.add)
            reduce(m1[:, :], sel[:, :, :], ALU.max)
            first_equal(o1, sel[:, :, :], m1)
            ch.link(V.scalar_tensor_tensor(out=sel2[:, :, :], in0=o1[:, :, :], scalar=-3.0e38, in1=sel[:, :, :], op0=ALU.mult, op1=ALU.add))
            reduce(m2[:, :], sel2[:, :, :], ALU.max)
            V.tensor_tensor(dd[:, :], m2[:, :], m1[:, :], ALU.subtract).then_inc(d_ok, 1)
            first_equal(o2, sel2[:, :, :], m2)
            M1, M2, M = v64[1], v64[2], v64[3]
            tt(M1[:, :, :, :], inner(og), outer(o1), ALU.mult)
            tt(M2[:, :, :, :], inner(og), outer(o2), ALU.mult)
            tt(M[:, :, :, :], M1[:, :, :, :], M2[:, :, :, :], ALU.add)
            flat = lambda t: t[:, :, :, :].rearrange("p j g e -> p j (g e)")
            V.tensor_reduce(out=msum[:, :], in_=flat(M).rearrange("p j n -> p n j"), axis=AX.X, op=ALU.add).then_inc(ms_ok, 1)
            dve.wait_ge(eg_ok, 1)
            reduce(psum[:, :], v16[0][:, :, :], ALU.add)
            dve.wait_ge(e2_ok, 1)
            ch.link(V.tensor_scalar(v4[6][:, :], dd[:, :], 1.0, None, ALU.add))
            tt(v4[6][:, :], v4[6][:, :], psum[:, :], ALU.mult)
            ch.link(V.reciprocal(wgt[:, 0, :], v4[6][:, :]))
            tt(wgt[:, 1, :], wgt[:, 0, :], dd[:, :], ALU.mult)
            dve.wait_ge(rank_done, 1)
            ch.link(V.tensor_copy(rank[:, 0, :], bank[1][:, 0:NE]))
            for j in range(1, J):
                tt(rank[:, j, :], rank[:, j - 1, :], flat(M)[:, j - 1, :], ALU.add)
            for k, Mk in enumerate([M1, M2]):
                tt(v64[4][:, :, :, :].rearrange("p j g e -> p j (g e)"), flat(Mk), rank[:, :, :], ALU.mult)
                reduce(posf[:, k, :], flat(v64[4]), ALU.add)
                tt(flat(v64[4]), flat(Mk), g["base16"][:, :].rearrange("p (x n) -> p x n", x=1).to_broadcast([P, J, NE]), ALU.mult)
                reduce(first_place[:, k, :], flat(v64[4]), ALU.add)
            for b in range(1, J):
                ch.link(V.tensor_scalar(later[:, :, :], posf[:, :, :], float(P * b), float(NE * P - P), ALU.is_ge, ALU.mult))
                tt(first_place[:, :, :], first_place[:, :, :], later[:, :, :], ALU.add)
            tt(posf[:, :, :], posf[:, :, :], first_place[:, :, :], ALU.add)
            V.tensor_copy(pos[:, :, :], posf[:, :, :]).then_inc(pos_ok, 1)
            reduce(most[:, 0:1], bank[1][:, NE:2 * NE], ALU.max)
            V.tensor_copy(mosti[:, :], most[:, 0:1]).then_inc(pos_ok, 1)
            dve.wait_ge(tok_tr, 1)
            V.tensor_copy(idx[:, 0:NE * J], bank[2][:, 0:NE * J]).then_inc(idx_ok, 1)
            dve_xt(dve, main, 0, 0)
            with dve.Fori(0, NE // 2) as i:
                for x in range(2):
                    count = i * 2 + x
                    dve_expert(dve, main, i, x, 2, count, between=lambda: dve_xt(dve, main, 1 - x, count + 1))
            dve.wait_ge(pos_ok, 2)
            with overflow(dve):
                for x in ["xt_d", "hid_ok", "y_d"]:
                    dve.sem_inc(more[x], 1)
                with dve.Fori(0, NE) as e:
                    with dve.Fori(1, J) as b:
                        n = e * (J - 1) + (b - 1)
                        dve_xt(dve, more, 0, n)
                        dve_expert(dve, more, n, 0, 1, n)
            for j in range(J):
                dve.wait_ge(comb_in[j], 32)
                for k in range(2):
                    src = (xn if k == 0 else xnT2)[:, j, :]
                    V.scalar_tensor_tensor(out=h[:, j, :], in0=src, scalar=wgt[:, k, j:j + 1], in1=h[:, j, :], op0=ALU.mult, op1=ALU.add).then_inc(comb_ok, 1)
                    dve.wait_ge(comb_ok, 2 * j + k + 1)

        @block.tensor
        def _(pe):
            for x in ["xt_done", "g_done", "u_done", "ht_done", "y_done"]:
                pe.sem_inc(main[x], 1)
            pe.wait_ge(xn_ok, J)
            for kt in range(KT):
                for j in range(J):
                    last = nc.tensor.transpose(bank[kt][:, P * j:P * j + P], xn[:, j, P * kt:P * kt + P], g["ident"][:, :])
                last.then_inc(tr, 1)
            pe.wait_ge(ev_a, KT // 2)
            pe.wait_ge(ev_d, KT // 2)
            pe.wait_ge(par_in, 80)
            for j in range(J):
                for kt in range(KT):
                    last = nc.tensor.matmul(bank[0][:, (NG + NE) * j:(NG + NE) * (j + 1)], xnT[:, kt, P * j:P * j + P], wr[:, kt, :], start=kt == 0, stop=kt == KT - 1)
            last.then_inc(lg_done, 1)
            pe.wait_ge(ms_ok, 1)
            nc.tensor.matmul(bank[1][:, 0:NE], g["upper"][:, :], msum[:, :], start=True, stop=True)
            nc.tensor.matmul(bank[1][:, NE:2 * NE], g["ones"][:, :], msum[:, :], start=True, stop=True).then_inc(rank_done, 1)
            pe.wait_ge(tok_in, 16)
            nc.tensor.transpose(bank[2][:, 0:NE * J], tokrow[:, :], g["ident"][0:NE * J, 0:NE * J]).then_inc(tok_tr, 1)
            pe.wait_ge(idx_ok, 1)
            pe_transposes(pe, main, 0, 0, 2, 0)
            with pe.Fori(0, NE // 2) as i:
                pe_expert(pe, main, i, 0, 2, i * 2, between=lambda: pe_transposes(pe, main, i, 1, 2, i * 2 + 1))
                pe_expert(pe, main, i, 1, 2, i * 2 + 1, between=lambda: pe_transposes(pe, main, i + 1, 0, 2, i * 2 + 2))
            pe.wait_ge(pos_ok, 2)
            with overflow(pe):
                for x in ["xt_done", "g_done", "u_done", "ht_done", "y_done"]:
                    pe.sem_inc(more[x], 1)
                for x in ["xt_a", "xt_d", "y_a", "y_d"]:
                    pe.wait_ge(main[x], NE + 1)
                with pe.Fori(0, NE) as e:
                    with pe.Fori(1, J) as b:
                        n = e * (J - 1) + (b - 1)
                        pe_transposes(pe, more, n, 0, 1, n)
                        pe_expert(pe, more, n, 0, 1, n)


def attention(nc, io, g):
    h, bank = g["h"], g["bank"]
    G, AH = 3, 8
    W = AH * HD
    SCALE = HD ** -0.5
    FAR = -1.0e30
    with Scope(nc, "attn") as s:
        xhat = s.sb("xhat", [P, J, D])
        xk = s.sb("xk", [P, KT, T])
        xq = s.sb("xq", [P, KT, T])
        ring = [s.sb(f"ring{i}", [P, KT, W]) for i in range(3)]
        kT = [s.sb(f"kT{i}", [P, AH // 2, T]) for i in range(G)]
        qT = [s.sb(f"qT{i}", [P, AH // 2, T]) for i in range(G)]
        vv = [s.sb(f"v{i}", [P, J, W]) for i in range(G)]
        sm, pr, pT = ([xhat[:, n, 512 * i:512 * i + 512] for i in range(2)] for n in range(3))
        oacc = [xk[:, 0:4, :], xk[:, 4:8, :], xq[:, 0:4, :]]
        oT = xq[:, 4:8, :]
        mask = [s.sb("mask0", [P, J, T]), s.sb("mask1", [P, P]), s.sb("mask2", [P, P])]
        residue = s.sb("residue", [P, P])
        ss, rstd = s.sb("ss", [P, J]), s.sb("rstd", [P, J])
        negm = s.sb("negm", [P, G, J, AH])
        lsum = s.sb("lsum", [P, G, J, AH])
        least = s.sb("least", [P, J, AH])
        den = s.sb("den", [P, J, AH])
        sumsq, rms, rstd_ok, xhat_ok, tr, xk_ok, xq_ok, unit, ev_a, ev_d = map(
            s.sem, ["sumsq", "rms", "rstd_ok", "xhat_ok", "tr", "xk_ok", "xq_ok", "unit", "ev_a", "ev_d"])
        pool_order, mask_ok, res_mm, m2_ok, s_done, sm_ok, max_ok, p_ok, t_done, pt_ok, o_done, o_ev = map(
            s.sem, ["pool_order", "mask_ok", "res_mm", "m2_ok", "s_done", "sm_ok", "max_ok", "p_ok", "t_done", "pt_ok", "o_done", "o_ev"])
        order, d_ok, e_ok, w_ok, comb_ok, otr, ot_a, ot_d, out_done, h_ok = map(
            s.sem, ["order", "d_ok", "e_ok", "w_ok", "comb_ok", "otr", "ot_a", "ot_d", "out_done", "h_ok"])
        slab_in = [s.sem(f"slab_in{i}") for i in range(3)]
        units = [(0, hh, (j,)) for hh in range(AH) for j in range(J)] + [(gi, hh, tuple(range(J))) for gi in (1, 2) for hh in range(AH)]
        NU = len(units)
        NPROJ = 12 * G
        block = s.enter_context(nc.Block())

        def evacuated(eng, u):
            eng.wait_ge(ev_d if u % 2 else ev_a, u // 2 + 1)

        def projected(u):
            gi, kind, i = u // 12, u % 12 // 4, u % 4
            return (kT, qT, vv)[kind][gi][:, i, :]

        @block.sync
        def _(sp):
            def load(i, src, k, need):
                if need:
                    sp.wait_ge(unit, need)
                sp.dma_start(ring[i][:, :, :] if k == KT else ring[i][:, :, :].rearrange("p a b -> p (a b)").rearrange("p (a b) -> p a b", a=k),
                             src.rearrange("(k p) n -> p k n", p=P)).then_inc(slab_in[i], 16)

            for gi in range(G):
                for i, src in enumerate([io["w_kv"][:, W * gi:W * gi + W], io["attn_w_q"][0, :, W * gi:W * gi + W],
                                         io["w_kv"][:, W * (G + gi):W * (G + gi) + W]]):
                    load(i, src, KT, 12 * (gi - 1) + 4 * (i + 1) if gi else 0)
            load(0, io["attn_w_o"][0], W // P, 12 * (G - 1) + 4)

        @block.gpsimd
        def _(pool):
            ch = Chain(pool, pool_order)
            ch.inc(nc.gpsimd.memset(mask[0][:, :, :], 0.0))
            ch.inc(nc.gpsimd.memset(mask[1][:, :], 0.0))
            ch.inc(nc.gpsimd.memset(mask[2][:, :], 1.0))
            ch.link(nc.gpsimd.memset(residue[:, :], 0.0))

            def keep(m, op, fill, base, pattern, per_partition):
                ch.link(nc.gpsimd.affine_select(out=m, in_=m, compare_op=op, fill=fill, base=base, pattern=pattern, channel_multiplier=per_partition))

            m0 = mask[0][:, :, :].rearrange("p j (i k) -> p j i k", i=J)
            window = P
            keep(m0, ALU.is_ge, FAR, 0, [[1, J], [-1, J], [-J, P]], J)
            keep(m0, ALU.is_ge, FAR, window, [[-1, J], [1, J], [J, P]], -J)
            keep(mask[1][:, :], ALU.is_ge, FAR, 0, [[-1, P]], 1)
            keep(mask[2][:, :], ALU.is_ge, 0.0, 0, [[-1, P]], 1)
            r4 = residue[:, :].rearrange("p (a b) -> p a b", b=4)
            nc.gpsimd.affine_select(out=r4, in_=r4, compare_op=ALU.not_equal, fill=1.0, base=0, pattern=[[0, P // 4], [-1, 4]],
                                    channel_multiplier=1).then_inc(mask_ok, 1)

        @block.scalar
        def _(act):
            for j in range(J):
                nc.scalar.activation(xq[:, 0:2, :].rearrange("p a b -> p (a b)"), h[:, j, :], ACT.Square, accum_out=ss[:, j:j + 1]).then_inc(sumsq, 1)
                act.wait_ge(sumsq, j + 1)
            nc.scalar.activation(ss[:, :], ss[:, :], ACT.Sqrt, scale=1.0 / D, bias=g["eps"][:, 0:1]).then_inc(rms, 1)
            for kt in range(KT):
                act.wait_ge(tr, kt + 1)
                act.wait_ge(xk_ok, kt + 1)
                nc.scalar.activation(xq[:, kt, :], bank[kt][:, :], ACT.Copy, scale=g["par"][:, GMIX + KT + kt:GMIX + KT + kt + 1]).then_inc(xq_ok, 1)
            for u in range(0, NPROJ, 2):
                act.wait_ge(unit, u + 1)
                nc.scalar.activation(projected(u), bank[u % 8][:, :], ACT.Copy).then_inc(ev_a, 1)

            def transposed(u):
                act.wait_ge(t_done, u + 1)
                if u >= 2:
                    act.wait_ge(o_done, u - 1)
                nc.scalar.activation(pT[u % 2], bank[3 + u % 2][:, :], ACT.Copy).then_inc(pt_ok, 1)

            for u, (gi, hh, js) in enumerate(units):
                act.wait_ge(max_ok, u + 1)
                if u >= 2:
                    act.wait_ge(t_done, u - 1)
                n = T // len(js)
                for i, j in enumerate(js):
                    ins = nc.scalar.activation(pr[u % 2][:, n * i:n * i + n], sm[u % 2][:, n * i:n * i + n], ACT.Exp,
                                               bias=negm[:, gi, j, hh:hh + 1], accum_out=lsum[:, gi, j, hh:hh + 1])
                ins.then_inc(p_ok, 1)
                if u >= 1:
                    transposed(u - 1)
            transposed(NU - 1)
            act.wait_ge(d_ok, 1)
            nc.scalar.activation(negm[:, :, :, :], negm[:, :, :, :], ACT.Exp, scale=-1.0).then_inc(e_ok, 1)
            for b in range(0, 4, 2):
                act.wait_ge(otr, b + 1)
                nc.scalar.activation(oT[:, b, :], bank[b][:, :], ACT.Copy).then_inc(ot_a, 1)

        @block.vector
        def _(dve):
            V = nc.vector
            dve.wait_ge(rms, 1)
            V.reciprocal(rstd[:, :], ss[:, :]).then_inc(rstd_ok, 1)
            dve.wait_ge(rstd_ok, 1)
            for j in range(J):
                V.tensor_scalar(xhat[:, j, :], h[:, j, :], rstd[:, j:j + 1], None, ALU.mult).then_inc(xhat_ok, 1)
            for kt in range(KT):
                dve.wait_ge(tr, kt + 1)
                V.tensor_scalar(xk[:, kt, :], bank[kt][:, :], g["par"][:, GKV + kt:GKV + kt + 1], None, ALU.mult).then_inc(xk_ok, 1)
            for u in range(1, NPROJ, 2):
                dve.wait_ge(unit, u + 1)
                V.tensor_copy(projected(u), bank[u % 8][:, :]).then_inc(ev_d, 1)
            ch = Chain(dve, order)
            dve.wait_ge(res_mm, 1)
            ch.link(V.tensor_tensor(mask[2][:, :], bank[7][:, 0:P], mask[2][:, :], ALU.mult))
            ch.link(V.tensor_scalar(mask[2][:, :], mask[2][:, :], 1.0, -FAR, ALU.subtract, ALU.mult))

            def output(u):
                gi, hh, js = units[u]
                dve.wait_ge(o_done, u + 1)
                src = bank[5 + u % 2][:, 0:HD * len(js)].rearrange("p (j v) -> p j v", j=len(js))
                V.tensor_copy(oacc[gi][:, js[0]:js[0] + len(js), HD * hh:HD * hh + HD], src).then_inc(o_ev, 1)

            dve.wait_ge(ev_a, NPROJ // 2)
            for u, (gi, hh, js) in enumerate(units):
                dve.wait_ge(s_done, u + 1)
                if u >= 2:
                    dve.wait_ge(p_ok, u - 1)
                if gi == 0:
                    V.scalar_tensor_tensor(out=sm[u % 2], in0=bank[u % 3][:, :], scalar=SCALE, in1=mask[0][:, js[0], :], op0=ALU.mult, op1=ALU.add).then_inc(sm_ok, 1)
                    dve.wait_ge(sm_ok, u + 1)
                    V.tensor_reduce(out=negm[:, gi, js[0], hh:hh + 1], in_=sm[u % 2], axis=AX.X, op=ALU.max, negate=True).then_inc(max_ok, 1)
                else:
                    v3 = lambda x: x.rearrange("p (j t) -> p j t", j=J)
                    V.scalar_tensor_tensor(out=v3(sm[u % 2]), in0=v3(bank[u % 3][:, :]), scalar=SCALE,
                                           in1=mask[gi][:, :].rearrange("p (x t) -> p x t", x=1).to_broadcast([P, J, P]), op0=ALU.mult, op1=ALU.add).then_inc(sm_ok, 1)
                    dve.wait_ge(sm_ok, u + 1)
                    V.tensor_reduce(out=negm[:, gi, :, hh], in_=v3(sm[u % 2]), axis=AX.X, op=ALU.max, negate=True).then_inc(max_ok, 1)
                if u >= 2:
                    output(u - 2)
            output(NU - 2)
            output(NU - 1)
            dve.wait_ge(p_ok, NU)
            dve.wait_ge(max_ok, NU)
            ch.link(V.tensor_tensor(least[:, :, :], negm[:, 0, :, :], negm[:, 1, :, :], ALU.min))
            ch.link(V.tensor_tensor(least[:, :, :], least[:, :, :], negm[:, 2, :, :], ALU.min))
            for gi in range(G):
                ins = V.tensor_tensor(negm[:, gi, :, :], negm[:, gi, :, :], least[:, :, :], ALU.subtract)
                if gi < G - 1:
                    ch.inc(ins)
                else:
                    ch.wait()
                    ins.then_inc(d_ok, 1)
            dve.wait_ge(e_ok, 1)
            for gi in range(G):
                ch.link(V.tensor_tensor(lsum[:, gi, :, :], lsum[:, gi, :, :], negm[:, gi, :, :], ALU.mult))
            ch.link(V.tensor_tensor(den[:, :, :], lsum[:, 0, :, :], lsum[:, 1, :, :], ALU.add))
            ch.link(V.tensor_tensor(den[:, :, :], den[:, :, :], lsum[:, 2, :, :], ALU.add))
            ch.link(V.reciprocal(den[:, :, :], den[:, :, :]))
            for gi in range(G):
                ch.link(V.tensor_tensor(negm[:, gi, :, :], negm[:, gi, :, :], den[:, :, :], ALU.mult))
            dve.wait_ge(o_ev, NU)
            heads = lambda t, j: t[:, j, :].rearrange("p (h v) -> p h v", h=AH)
            for j in range(J):
                for gi in range(G):
                    ch.link(V.tensor_tensor(heads(oacc[gi], j), heads(oacc[gi], j),
                                            negm[:, gi, j, :].rearrange("p (h x) -> p h x", x=1).to_broadcast([P, AH, HD]), ALU.mult))
                ch.link(V.tensor_tensor(oacc[0][:, j, :], oacc[0][:, j, :], oacc[1][:, j, :], ALU.add))
                V.tensor_tensor(oacc[0][:, j, :], oacc[0][:, j, :], oacc[2][:, j, :], ALU.add).then_inc(comb_ok, 1)
            for b in range(1, 4, 2):
                dve.wait_ge(otr, b + 1)
                V.tensor_copy(oT[:, b, :], bank[b][:, :]).then_inc(ot_d, 1)
            for u in range(2 * J):
                dve.wait_ge(out_done, u + 1)
                hh = h[:, u // 2, 512 * (u % 2):512 * (u % 2) + 512]
                V.tensor_tensor(hh, bank[u][:, :], hh, ALU.add).then_inc(h_ok, 1)

        @block.tensor
        def _(pe):
            pe.wait_ge(xhat_ok, J)
            for kt in range(KT):
                for j in range(J):
                    last = nc.tensor.transpose(bank[kt][:, P * j:P * j + P], xhat[:, j, P * kt:P * kt + P], g["ident"][:, :])
                last.then_inc(tr, 1)
            for u in range(NPROJ):
                gi, kind, i = u // 12, u % 12 // 4, u % 4
                b = bank[u % 8]
                if u >= 8:
                    evacuated(pe, u - 8)
                else:
                    pe.wait_ge(xq_ok, KT)
                if i == 0:
                    pe.wait_ge(slab_in[kind], 16 * (gi + 1))
                x = xq if kind == 1 else xk
                for kt in range(KT):
                    w = ring[kind][:, kt, :]
                    a, c = (x[:, kt, P * i:P * i + P], w) if kind == 2 else (w[:, P * i:P * i + P], x[:, kt, :])
                    last = nc.tensor.matmul(b[:, :], a, c, start=kt == 0, stop=kt == KT - 1)
                last.then_inc(unit, 1)
            pe.wait_ge(mask_ok, 1)
            pe.wait_ge(ev_a, NPROJ // 2)
            pe.wait_ge(ev_d, NPROJ // 2)
            nc.tensor.matmul(bank[7][:, 0:P], residue[:, :], residue[:, :], start=True, stop=True).then_inc(res_mm, 1)

            def scores(u):
                gi, hh, js = units[u]
                rows = slice(HD * (hh % 2), HD * (hh % 2) + HD)
                if u >= 3:
                    pe.wait_ge(sm_ok, u - 2)
                for i, j in enumerate(js):
                    q = qT[gi][rows, hh // 2, P * j:P * j + P]
                    out, k = (bank[u % 3][:, :], kT[gi][rows, hh // 2, :]) if gi == 0 else (bank[u % 3][:, P * i:P * i + P], kT[gi][rows, hh // 2, P * j:P * j + P])
                    ins = nc.tensor.matmul(out, q, k, start=True, stop=True)
                ins.then_inc(s_done, 1)

            def values(u):
                gi, hh, js = units[u]
                pe.wait_ge(pt_ok, u + 1)
                if u >= 2:
                    pe.wait_ge(o_ev, u - 1)
                for i in range(J):
                    out = bank[5 + u % 2][:, 0:HD] if gi == 0 else bank[5 + u % 2][:, HD * i:HD * i + HD]
                    ins = nc.tensor.matmul(out, pT[u % 2][:, P * i:P * i + P], vv[gi][:, i, HD * hh:HD * hh + HD],
                                           start=gi > 0 or i == 0, stop=gi > 0 or i == J - 1)
                ins.then_inc(o_done, 1)

            scores(0)
            scores(1)
            for u in range(NU):
                if u + 2 < NU:
                    scores(u + 2)
                pe.wait_ge(p_ok, u + 1)
                if u >= 2:
                    pe.wait_ge(pt_ok, u - 1)
                for i in range(J):
                    ins = nc.tensor.transpose(bank[3 + u % 2][:, P * i:P * i + P], pr[u % 2][:, P * i:P * i + P], g["ident"][:, :])
                ins.then_inc(t_done, 1)
                if u >= 1:
                    values(u - 1)
            values(NU - 1)
            pe.wait_ge(comb_ok, J)
            for b in range(W // P):
                for j in range(J):
                    ins = nc.tensor.transpose(bank[b][:, P * j:P * j + P], oacc[0][:, j, P * b:P * b + P], g["ident"][:, :])
                ins.then_inc(otr, 1)
            pe.wait_ge(ot_a, 2)
            pe.wait_ge(ot_d, 2)
            pe.wait_ge(slab_in[0], 16 * (G + 1))
            wo = ring[0][:, :, :].rearrange("p a b -> p (a b)").rearrange("p (a b) -> p a b", a=W // P)
            for u in range(2 * J):
                for kt in range(W // P):
                    ins = nc.tensor.matmul(bank[u][:, :], oT[:, kt, P * (u // 2):P * (u // 2) + P], wo[:, kt, 512 * (u % 2):512 * (u % 2) + 512],
                                           start=kt == 0, stop=kt == W // P - 1)
                ins.then_inc(out_done, 1)


def final_norm(nc, io, g, out):
    h = g["h"]
    with Scope(nc, "final") as s:
        gb = s.sb("gb", [P, D])
        junk = s.sb("junk", [P, D])
        ss, rstd = s.sb("ss", [P, J]), s.sb("rstd", [P, J])
        g_in, sumsq, rms, rstd_ok, done, stored = map(s.sem, ["g_in", "sumsq", "rms", "rstd_ok", "done", "stored"])
        block = s.enter_context(nc.Block())

        @block.sync
        def _(sp):
            sp.dma_start(gb[:, :], io["final_norm_g"].rearrange("(a d) -> a d", a=1).to_broadcast([P, D])).then_inc(g_in, 16)
            for j in range(J):
                sp.wait_ge(done, j + 1)
                sp.dma_start(out[0].rearrange("(p j) d -> p j d", j=J)[:, j, :], h[:, j, :]).then_inc(stored, 16)
            sp.wait_ge(stored, 16 * J)

        @block.scalar
        def _(act):
            for j in range(J):
                nc.scalar.activation(junk[:, :], h[:, j, :], ACT.Square, accum_out=ss[:, j:j + 1]).then_inc(sumsq, 1)
                act.wait_ge(sumsq, j + 1)
            nc.scalar.activation(ss[:, :], ss[:, :], ACT.Sqrt, scale=1.0 / D, bias=g["eps"][:, 0:1]).then_inc(rms, 1)

        @block.vector
        def _(dve):
            dve.wait_ge(rms, 1)
            nc.vector.reciprocal(rstd[:, :], ss[:, :]).then_inc(rstd_ok, 1)
            dve.wait_ge(rstd_ok, 1)
            dve.wait_ge(g_in, 16)
            for j in range(J):
                nc.vector.scalar_tensor_tensor(out=h[:, j, :], in0=h[:, j, :], scalar=rstd[:, j:j + 1], in1=gb[:, :], op0=ALU.mult, op1=ALU.mult).then_inc(done, 1)


_EXTRA = 0


def build(nc, io, out):
    top = Scope(nc, "all")
    with top:
        g = {
            "ident": top.sb("ident", [P, P]), "par": top.sb("par", [P, P]), "eps": top.sb("eps", [P, 2]),
            "blockones": top.sb("blockones", [P, P]), "chmask": top.sb("chmask", [P, P]), "upper": top.sb("upper", [P, P]), "ones": top.sb("ones", [P, P]), "h": top.sb("h", [P, J, D]),
            "down4": top.sb("down4", [P, 4]), "base16": top.sb("base16", [P, 16]), "tokid": top.sb("tokid", [P, J]), "ints": top.sb("ints", [P, 16], i32), "lowmask": top.sb("lowmask", [C, C]), "bonus": top.sb("bonus", [P, J, H]),
            "bank": [top.ps(f"bank{i}", [P, 512]) for i in range(8)],
            "ready": top.sem("constants_ready"),
        }
        io["g_dram"] = nc.dram_tensor("g_dram", [T, D], fp32).ap()
        for i in range(2):
            io[f"xn_dram{i}"] = nc.dram_tensor(f"xn_dram{i}", [T, D], fp32).ap()
            io[f"tok_dram{i}"] = nc.dram_tensor(f"tok_dram{i}", [16 * T, 1], fp32).ap()
            io[f"out_dram{i}"] = nc.dram_tensor(f"out_dram{i}", [16 * T, D], fp32).ap()
        io["y_dram"] = nc.dram_tensor("y_dram", [T, D], fp32).ap()
        io["v_dram"] = nc.dram_tensor("v_dram", [T, D], fp32).ap()
        with nc.Block() as block:
            @block.gpsimd
            def _(pool):
                ch = Chain(pool, g["ready"])
                ones = lambda name, v=1.0: ch.inc(nc.gpsimd.memset(g[name][:, :], v))
                ones("ident", 0.0)
                ones("blockones", 0.0)
                for name in ["upper", "chmask", "lowmask", "ones"]:
                    ones(name)
                ch.inc(nc.gpsimd.memset(g["eps"][:, 0:1], NORM_EPS))
                ch.link(nc.gpsimd.memset(g["eps"][:, 1:2], GN_EPS))

                def keep(m, fill, op, base, step, per_partition):
                    ch.link(nc.gpsimd.affine_select(out=m, in_=m, compare_op=op, fill=fill, base=base,
                                                    pattern=[[step, m.shape[1]]], channel_multiplier=per_partition))

                for name, n, step, base, per_partition in (("down4", 4, -1, 4, 0), ("base16", 16, P, 0, 0), ("tokid", J, 1, 0, J)):
                    ch.link(nc.gpsimd.iota(g["ints"][:, 0:n], pattern=[[step, n]], base=base, channel_multiplier=per_partition))
                    ch.link(nc.gpsimd.tensor_copy(g[name][:, :], g["ints"][:, 0:n]))
                keep(g["ident"][:, :], 1.0, ALU.not_equal, 0, -1, 1)
                keep(g["upper"][:, :], 0.0, ALU.is_ge, -1, 1, -1)
                for rows, base in ((P, C), (C, 0)):
                    for x in range(2):
                        keep(g["chmask"][0:rows, C * x:C * x + C], 0.0, ALU.is_ge, base - 1 + x, 1, -1)
                keep(g["lowmask"][:, :], 0.0, ALU.is_ge, -1, -1, 1)
                for i in range(2):
                    ch.link(nc.gpsimd.memset(g["blockones"][HD * i:HD * i + HD, HD * i:HD * i + HD], 1.0))

        with Scope(nc, "rwkv") as s:
            rw = {n: s.sb("rw_" + n, [P, KT, T]) for n in "rkwa"}
            rwkv_project(nc, io, g, rw)
            for x in ["n", "e1", "e2", "tmp"]:
                rw[x] = s.sb("rw_" + x, [P, KT, T])
            rw["pc"] = s.sb("rw_pc", [C, NC, H])
            rwkv_operands(nc, io, g, rw)
            rwkv_chunks(nc, io, g, rw)
            rwkv_finish(nc, io, g, rw)
        if _STAGE >= 2:
            moe(nc, io, g, 0)
        if _STAGE >= 3:
            attention(nc, io, g)
        if _STAGE >= 4:
            moe(nc, io, g, 1)
            final_norm(nc, io, g, out)
            return
        with Scope(nc, "end") as s:
            dump = s.sem("dump")
            with nc.Block() as block:
                @block.sync
                def _(sp):
                    sp.dma_start(out[0].rearrange("(p j) d -> p j d", j=J), g["h"][:, :, :]).then_inc(dump, 16)
                    sp.wait_ge(dump, 16)


_STAGE = 4
_DUMP = "r"
_INS = ["x", "norm_mix_g", "norm_ffn_g", "rwkv_mu", "rwkv_w_r", "rwkv_w_k", "rwkv_w_v", "rwkv_w0", "rwkv_w1", "rwkv_w2",
        "rwkv_a0", "rwkv_a1", "rwkv_a2", "rwkv_g1", "rwkv_g2", "rwkv_k_k", "rwkv_k_a", "rwkv_r_k", "rwkv_ln_w", "rwkv_ln_b",
        "rwkv_w_o", "kv_norm_g", "w_kv", "attn_w_q", "attn_w_o", "moe_w_grp", "moe_b_grp", "moe_w_exp", "moe_b_exp",
        "moe_w_gate", "moe_w_up", "moe_w_down", "final_norm_g"]


def kernel(**inputs):
    import numpy as _np
    import concourse.bacc as _bacc
    from concourse import mybir as _mybir
    from concourse.bass_utils import run_bass_kernel_spmd as _run

    nc = _bacc.Bacc("TRN2", target_bir_lowering=False, num_devices=1)
    arrays, io = {}, {}
    for name in _INS:
        a = _np.ascontiguousarray(inputs[name])
        arrays[f"in_{name}_dram"] = a
        io[name] = nc.dram_tensor(f"in_{name}_dram", a.shape, _mybir.dt.from_np(a.dtype), kind="ExternalInput").ap()
    out = nc.dram_tensor("out_0_dram", (1, T, D), _mybir.dt.float32, kind="ExternalOutput").ap()
    build(nc, io, out)
    r = _run(nc, [arrays], core_ids=[0])
    return r.results[0]["out_0_dram"]
```

```python
import concourse.bass as bass
from concourse import mybir
from contextlib import ExitStack

fp32 = mybir.dt.float32
i32 = mybir.dt.int32
fp32r = mybir.dt.float32r
ALU = mybir.AluOpType
ACT = mybir.ActivationFunctionType
AX = mybir.AxisListType

P = 128
T = 512
D = 1024
J = T // P
KT = D // P
HD = 64
H = D // HD
LORA = 64
GLORA = 160
C = 64
NC = T // C
SLAB = 4096
NORM_EPS = 1e-6
GN_EPS = HD * 1e-5
DECAY = float(-(2.718281828459045 ** -0.5))

MU, W0, A0, KK_, KA_, RK_, GMIX, GFFN, GKV = 0, 48, 56, 64, 72, 80, 88, 104, 120


class Chain:

    def __init__(self, eng, sem):
        self.eng, self.sem, self.base, self.n = eng, sem, 0, 0

    def inc(self, ins):
        ins.then_inc(self.sem, 1)
        self.n += 1
        return ins

    def wait(self):
        self.eng.wait_ge(self.sem, self.base + self.n)

    def link(self, ins):
        self.inc(ins)
        self.wait()

    def enter(self, i, per):
        self.before, self.per = self.base + self.n, per
        self.base, self.n = i * per + self.before, 0

    def leave(self, times):
        assert self.n == self.per, f"{self.n} signals an iteration, not {self.per}"
        self.base, self.n = self.before + times * self.per, 0


class Scope(ExitStack):

    def __init__(self, nc, stage):
        super().__init__()
        self.nc, self.stage, self.sems = nc, stage + "_", []
        self.callback(self.clear)

    def clear(self):
        if self.sems:
            self.nc.clear_and_free_semaphores(self.sems)
            self.nc.all_engine_barrier()

    def sb(self, name, shape, dt=fp32):
        return self.enter_context(self.nc.sbuf_tensor(self.stage + name, shape, dt))

    def ps(self, name, shape, dt=fp32):
        return self.enter_context(self.nc.psum_tensor(self.stage + name, shape, dt))

    def sem(self, name):
        self.sems.append(self.nc.alloc_semaphore(self.stage + name))
        return self.sems[-1]


def rwkv_project(nc, io, g, rw):
    with Scope(nc, "project") as s:
        xT = s.sb("xT", [P, KT, T + 1])
        xx = s.sb("xx", [P, KT, T])
        xm = [s.sb(f"xm{i}", [P, KT, T]) for i in range(2)]
        ring = [s.sb(f"ring{i}", [P, SLAB]) for i in range(2)]
        lh = s.sb("lora_hidden", [P, 2, T])
        parrow = s.sb("parrow", [P, P])
        ss = s.sb("ss", [P, J])
        rstd = s.sb("rstd", [P, J])
        r, k, w, a = rw["r"], rw["k"], rw["w"], rw["a"]
        flat = lambda t: t[:, :, :].rearrange("p a b -> p (a b)")
        xtok = r[:, :, :].rearrange("p a b -> p (a b)").rearrange("p (j d) -> p j d", j=J)
        xhat = k[:, :, :].rearrange("p a b -> p (a b)").rearrange("p (j d) -> p j d", j=J)
        kf = flat(k)
        rf = flat(r)
        g1 = kf[:, 0:KT * GLORA].rearrange("p (a b) -> p a b", a=KT)
        g2 = kf[:, 1280:1280 + 2 * D].rearrange("p (a b) -> p a b", a=2)
        w1 = rf[:, 0:512].rearrange("p (a b) -> p a b", a=KT)
        a1 = rf[:, 512:1024].rearrange("p (a b) -> p a b", a=KT)
        w2 = rf[0:LORA, 1024:2048]
        a2 = rf[0:LORA, 2048:3072]
        gout = flat(w).rearrange("p (j d) -> p j d", j=J)
        vout = flat(a).rearrange("p (j d) -> p j d", j=J)
        bank = g["bank"]
        x_in, par_in, lora_g, lora_wa = map(s.sem, ["x_in", "par_in", "lora_g", "lora_wa"])
        slab_in = [s.sem(f"slab_in{i}") for i in range(2)]
        sumsq, rms, rstd_ok, xhat_ok = map(s.sem, ["sumsq", "rms", "rstd_ok", "xhat_ok"])
        par_tr, par_ok, tr, ev_t, xx_ok, zero_ok = map(s.sem, ["par_tr", "par_ok", "tr", "ev_t", "xx_ok", "zero_ok"])
        mixed, unit, ev_act, ev_dve, g_stored, v_stored = map(s.sem, ["mixed", "unit", "ev_act", "ev_dve", "g_stored", "v_stored"])

        order = [("g", 5), ("v", 3), ("w", 1), ("a", 4), ("k", 2), ("r", 0)]
        kinds = {"g": "AA" + "VA" * 4, "v": "VA" * 4, "w": "A" + "A" * 8, "a": "V" + "A" * 8, "k": "VA" * 4, "r": "VA" * 4}
        start, n = {}, 0
        for name, _ in order:
            start[name] = n
            n += len(kinds[name])
        allk = "".join(kinds[name] for name, _ in order)

        def evacuated(eng, u):
            eng.wait_ge(ev_act if allk[u] == "A" else ev_dve, allk[:u + 1].count(allk[u]))

        block = s.enter_context(nc.Block())

        @block.sync
        def _(sp):
            sp.dma_start(xtok, io["x"].rearrange("b (j p) d -> p (b j) d", p=P)).then_inc(x_in, 16)
            rows = [(MU, io["rwkv_mu"].rearrange("a m (k c) -> (a m k) c", c=P)), (W0, io["rwkv_w0"].rearrange("a (k c) -> (a k) c", c=P)),
                    (A0, io["rwkv_a0"].rearrange("a (k c) -> (a k) c", c=P)), (KK_, io["rwkv_k_k"].rearrange("a (k c) -> (a k) c", c=P)),
                    (KA_, io["rwkv_k_a"].rearrange("a (k c) -> (a k) c", c=P)),
                    (RK_, io["rwkv_r_k"].rearrange("a (k b) c -> (a k) (b c)", b=2)),
                    (GMIX, io["norm_mix_g"].rearrange("a (k c) -> (a k) c", c=P)),
                    (GFFN, io["norm_ffn_g"].rearrange("a (k c) -> (a k) c", c=P)),
                    (GKV, io["kv_norm_g"].rearrange("(k c) -> k c", c=P))]
            for at, src in rows:
                sp.dma_start(parrow[at:at + src.shape[0], :], src).then_inc(par_in, 16)
            sp.wait_ge(tr, KT)
            sp.dma_start(g1, io["rwkv_g1"][0].rearrange("(k p) n -> p k n", p=P)).then_inc(lora_g, 16)
            sp.dma_start(g2[:, 0, :], io["rwkv_g2"][0, 0:P, :]).then_inc(lora_g, 16)
            sp.dma_start(g2[0:GLORA - P, 1, :], io["rwkv_g2"][0, P:GLORA, :]).then_inc(lora_g, 16)
            sp.dma_start(w1, io["rwkv_w1"][0].rearrange("(k p) n -> p k n", p=P)).then_inc(lora_wa, 16)
            sp.dma_start(a1, io["rwkv_a1"][0].rearrange("(k p) n -> p k n", p=P)).then_inc(lora_wa, 16)
            sp.dma_start(w2, io["rwkv_w2"][0]).then_inc(lora_wa, 16)
            sp.dma_start(a2, io["rwkv_a2"][0]).then_inc(lora_wa, 16)
            for n, (name, half) in enumerate([(x, y) for x in "vkr" for y in range(2)]):
                if n >= 2:
                    pn, ph = "vkr"[(n - 2) // 2], n % 2
                    sp.wait_ge(unit, start[pn] + (8 if ph or pn == "v" else 4))
                sp.dma_start(ring[n % 2][:, :].rearrange("p (k n) -> p k n", k=KT),
                             io["rwkv_w_" + name][0, :, 512 * half:512 * half + 512].rearrange("(k p) n -> p k n", p=P)).then_inc(slab_in[n % 2], 16)
                if n == 1:
                    for j in range(2 * J):
                        if j % 2:
                            evacuated(sp, start["g"] + 2 + j)
                            evacuated(sp, start["g"] + 1 + j)
                            sp.dma_start(io["g_dram"][P * (j // 2):P * (j // 2) + P, :], gout[:, j // 2, :]).then_inc(g_stored, 16)
                if n == 3:
                    for j in range(2 * J):
                        if j % 2:
                            evacuated(sp, start["v"] + j)
                            evacuated(sp, start["v"] + j - 1)
                            sp.dma_start(io["v_dram"][P * (j // 2):P * (j // 2) + P, :], vout[:, j // 2, :]).then_inc(v_stored, 16)
            sp.wait_ge(g_stored, 16 * J)
            sp.wait_ge(v_stored, 16 * J)

        @block.tensor
        def _(pe):
            pe.wait_ge(par_in, 16 * 9)
            nc.tensor.transpose(bank[7][:, 0:P], parrow[:, :], g["ident"][:, :]).then_inc(par_tr, 1)
            pe.wait_ge(xhat_ok, J)
            for kt in range(KT):
                if kt == KT - 1:
                    pe.wait_ge(par_ok, 1)
                for j in range(J):
                    last = nc.tensor.transpose(bank[kt][:, P * j:P * j + P], xhat[:, j, P * kt:P * kt + P], g["ident"][:, :])
                last.then_inc(tr, 1)

            seen = set()

            def begin(u):
                if u >= 8:
                    evacuated(pe, u - 8)
                elif u == 0:
                    pe.wait_ge(ev_t, KT)
                return bank[u % 8]

            for i, (name, mu) in enumerate(order):
                x = xm[i % 2]
                u = start[name]

                def mix(kt):
                    if (i, kt) not in seen:
                        seen.add((i, kt))
                        pe.wait_ge(mixed, KT * i + kt + 1)

                if name == "g":
                    pe.wait_ge(lora_g, 48)
                    for m, (lo, n) in enumerate([(0, P), (P, GLORA - P)]):
                        b = begin(u)
                        for kt in range(KT):
                            mix(kt)
                            last = nc.tensor.matmul(b[0:n, :], g1[:, kt, lo:lo + n], x[:, kt, :], start=kt == 0, stop=kt == KT - 1)
                        last.then_inc(unit, 1)
                        u += 1
                    evacuated(pe, u - 1)
                    evacuated(pe, u - 2)
                    for j in range(J):
                        for half in range(2):
                            b = begin(u)
                            nc.tensor.matmul(b[:, :], lh[:, 0, P * j:P * j + P], g2[:, 0, 512 * half:512 * half + 512], start=True, stop=False)
                            nc.tensor.matmul(b[:, :], lh[0:GLORA - P, 1, P * j:P * j + P], g2[0:GLORA - P, 1, 512 * half:512 * half + 512],
                                             start=False, stop=True).then_inc(unit, 1)
                            u += 1
                elif name == "v":
                    for j in range(J):
                        for half in range(2):
                            b = begin(u)
                            if j == 0:
                                pe.wait_ge(slab_in[half], 16)
                            wv = ring[half][:, :].rearrange("p (k n) -> p k n", k=KT)
                            for kt in range(KT):
                                mix(kt)
                                last = nc.tensor.matmul(b[:, :], x[:, kt, P * j:P * j + P], wv[:, kt, :], start=kt == 0, stop=kt == KT - 1)
                            last.then_inc(unit, 1)
                            u += 1
                elif name in "wa":
                    if name == "w":
                        pe.wait_ge(lora_wa, 64)
                    l1, l2 = (w1, w2) if name == "w" else (a1, a2)
                    b = begin(u)
                    for kt in range(KT):
                        mix(kt)
                        last = nc.tensor.matmul(b[0:LORA, :], l1[:, kt, :], x[:, kt, :], start=kt == 0, stop=kt == KT - 1)
                    last.then_inc(unit, 1)
                    evacuated(pe, u)
                    u += 1
                    hid = lh[0:LORA, 0 if name == "w" else 1, :]
                    for m in range(KT):
                        b = begin(u)
                        nc.tensor.matmul(b[:, :], l2[:, P * m:P * m + P], hid, start=True, stop=True).then_inc(unit, 1)
                        u += 1
                else:
                    for m in range(KT):
                        b = begin(u)
                        half = m // 4
                        if m % 4 == 0:
                            pe.wait_ge(slab_in[half], 32 if name == "k" else 48)
                        wm = ring[half][:, :].rearrange("p (k n) -> p k n", k=KT)
                        for kt in range(KT):
                            mix(kt)
                            last = nc.tensor.matmul(b[:, :], wm[:, kt, P * (m % 4):P * (m % 4) + P], x[:, kt, :], start=kt == 0, stop=kt == KT - 1)
                        last.then_inc(unit, 1)
                        u += 1

        def evacuate(eng, who):
            for name, _ in order:
                for i, kind in enumerate(kinds[name]):
                    u = start[name] + i
                    if kind != who:
                        if kind == "A" and name == "w" and i == 0 and who == "V":
                            pass
                        continue
                    yield name, i, u

        def move(eng, who, name, i, u):
            b = bank[u % 8]
            eng.wait_ge(unit, u + 1)
            if name == "g" and i < 2:
                n = P if i == 0 else GLORA - P
                return nc.scalar.activation(lh[0:n, i, :], b[0:n, :], ACT.Sigmoid)
            if name == "w" and i == 0:
                return nc.scalar.activation(lh[0:LORA, 0, :], b[0:LORA, :], ACT.Tanh)
            if name == "a" and i == 0:
                return nc.vector.tensor_copy(lh[0:LORA, 1, :], b[0:LORA, :])
            if name == "w":
                if i == 1:
                    eng.wait_ge(g_stored, 16 * J)
                return nc.scalar.activation(w[:, i - 1, :], b[:, :], ACT.Sigmoid, bias=g["par"][:, W0 + i - 1:W0 + i])
            if name == "a":
                if i == 1:
                    eng.wait_ge(v_stored, 16 * J)
                return nc.scalar.activation(a[:, i - 1, :], b[:, :], ACT.Sigmoid, bias=g["par"][:, A0 + i - 1:A0 + i])
            if name == "g":
                out = gout[:, (i - 2) // 2, 512 * (i % 2):512 * (i % 2) + 512]
            elif name == "v":
                out = vout[:, i // 2, 512 * (i % 2):512 * (i % 2) + 512]
            else:
                out = (k if name == "k" else r)[:, i, :]
            if who == "A":
                return nc.scalar.activation(out, b[:, :], ACT.Copy)
            return nc.vector.tensor_copy(out, b[:, :])

        @block.scalar
        def _(act):
            act.wait_ge(x_in, 16)
            for j in range(J):
                nc.scalar.activation(xx[:, 0:2, :].rearrange("p a b -> p (a b)"), xtok[:, j, :], ACT.Square, accum_out=ss[:, j:j + 1]).then_inc(sumsq, 1)
                act.wait_ge(sumsq, j + 1)
            nc.scalar.activation(ss[:, :], ss[:, :], ACT.Sqrt, scale=1.0 / D, bias=g["eps"][:, 0:1]).then_inc(rms, 1)
            act.wait_ge(par_ok, 1)
            for kt in range(0, KT, 2):
                act.wait_ge(tr, kt + 1)
                nc.scalar.activation(xT[:, kt, 1:T + 1], bank[kt][:, :], ACT.Copy, scale=g["par"][:, GMIX + kt:GMIX + kt + 1]).then_inc(ev_t, 1)
            for name, i, u in evacuate(act, "A"):
                if name == "k" and i == 1 or name == "r" and i == 1:
                    act.wait_ge(unit, start[name])
                move(act, "A", name, i, u).then_inc(ev_act, 1)

        @block.vector
        def _(dve):
            dve.wait_ge(par_tr, 1)
            nc.vector.tensor_copy(g["par"][:, :], bank[7][:, 0:P]).then_inc(par_ok, 1)
            nc.vector.memset(xT[:, :, 0:1], 0.0).then_inc(zero_ok, 1)
            dve.wait_ge(rms, 1)
            nc.vector.reciprocal(rstd[:, :], ss[:, :]).then_inc(rstd_ok, 1)
            dve.wait_ge(rstd_ok, 1)
            for j in range(J):
                nc.vector.tensor_scalar(xhat[:, j, :], xtok[:, j, :], rstd[:, j:j + 1], None, ALU.mult).then_inc(xhat_ok, 1)
            dve.wait_ge(par_ok, 1)
            for kt in range(1, KT, 2):
                dve.wait_ge(tr, kt + 1)
                nc.vector.tensor_scalar(xT[:, kt, 1:T + 1], bank[kt][:, :], g["par"][:, GMIX + kt:GMIX + kt + 1], None, ALU.mult).then_inc(ev_t, 1)
            dve.wait_ge(ev_t, KT)
            dve.wait_ge(zero_ok, 1)
            nc.vector.tensor_tensor(xx[:, :, :], xT[:, :, 0:T], xT[:, :, 1:T + 1], ALU.subtract).then_inc(xx_ok, 1)
            dve.wait_ge(xx_ok, 1)
            todo = list(evacuate(dve, "V"))

            def flush(name):
                while todo and todo[0][0] == name:
                    n, i, u = todo.pop(0)
                    move(dve, "V", n, i, u).then_inc(ev_dve, 1)

            for i, (name, mu) in enumerate(order):
                if i >= 2:
                    nm = order[i - 2][0]
                    dve.wait_ge(unit, start[nm] + (len(kinds[nm]) if nm in "vkr" else 2 if nm == "g" else 1))
                for kt in range(KT):
                    nc.vector.scalar_tensor_tensor(out=xm[i % 2][:, kt, :], in0=xx[:, kt, :], scalar=g["par"][:, MU + KT * mu + kt:MU + KT * mu + kt + 1],
                                                   in1=xT[:, kt, 1:T + 1], op0=ALU.mult, op1=ALU.add).then_inc(mixed, 1)
                if i >= 1:
                    flush(order[i - 1][0])
            flush("r")


def rwkv_operands(nc, io, g, rw):
    with Scope(nc, "operands") as s:
        r, k, w, a, n, e1, e2, tmp = (rw[x] for x in ["r", "k", "w", "a", "n", "e1", "e2", "tmp"])
        omk = s.sb("one_minus_ka", [P, KT])
        hsel = s.sb("hsel", [P, KT, 2])
        reset = s.sb("reset", [P, T])
        bank = g["bank"]
        small, n_ok, sq_ok, sum_ok, root_ok, cs_ok, ex_ok = map(s.sem, ["small", "n_ok", "sq_ok", "sum_ok", "root_ok", "cs_ok", "ex_ok"])
        rcp, nn_ok, rate_ok, k_ok, rk_ok, bonus_mm, order, exp_ok = map(s.sem, ["rcp", "nn_ok", "rate_ok", "k_ok", "rk_ok", "bonus_mm", "dve_order", "exp_ok"])
        block = s.enter_context(nc.Block())

        @block.vector
        def _(dve):
            ch = Chain(dve, order)
            par = g["par"]
            ch.inc(nc.vector.memset(reset[:, :], 1.0))
            ch.wait()
            ch.inc(nc.vector.memset(reset[:, 0:T:C], 0.0))
            nc.vector.tensor_scalar(omk[:, :], par[:, KA_:KA_ + KT], -1.0, 1.0, ALU.mult, ALU.add).then_inc(small, 1)
            for i in range(2):
                nc.vector.tensor_scalar(hsel[:, :, i], par[:, RK_:RK_ + KT], g["blockones"][:, HD * i:HD * i + 1], None, ALU.mult).then_inc(small, 1)
            for m in range(KT):
                nc.vector.tensor_scalar(n[:, m, :], k[:, m, :], par[:, KK_ + m:KK_ + m + 1], None, ALU.mult).then_inc(n_ok, 1)
            ch.wait()
            for m in range(KT):
                nc.vector.tensor_tensor_scan(e1[:, m, :], reset[:, :], w[:, m, :], 0.0, ALU.mult, ALU.add).then_inc(cs_ok, 1)
            for m in range(KT):
                dve.wait_ge(cs_ok, m + 1)
                nc.vector.tensor_tensor(w[:, m, :], e1[:, m, :], w[:, m, :], ALU.subtract).then_inc(ex_ok, 1)
            for m in range(KT):
                dve.wait_ge(root_ok, m + 1)
                ch.link(nc.vector.tensor_scalar(e2[:, m, :], e2[:, m, :], 1e-12, None, ALU.max))
                ch.link(nc.vector.reciprocal(e2[:, m, :], e2[:, m, :]))
                nc.vector.tensor_tensor(n[:, m, :], n[:, m, :], e2[:, m, :], ALU.mult).then_inc(nn_ok, 1)
            dve.wait_ge(sum_ok, KT)
            dve.wait_ge(small, 3)
            for m in range(KT):
                nc.vector.tensor_scalar(tmp[:, m, :], a[:, m, :], par[:, KA_ + m:KA_ + m + 1], omk[:, m:m + 1], ALU.mult, ALU.add).then_inc(rate_ok, 1)
            for m in range(KT):
                dve.wait_ge(rate_ok, m + 1)
                dve.wait_ge(n_ok, m + 1)
                nc.vector.tensor_tensor(k[:, m, :], k[:, m, :], tmp[:, m, :], ALU.mult).then_inc(k_ok, 1)
            for m in range(KT):
                dve.wait_ge(k_ok, m + 1)
                nc.vector.tensor_tensor(tmp[:, m, :], r[:, m, :], k[:, m, :], ALU.mult).then_inc(rk_ok, 1)
            for m in range(KT):
                dve.wait_ge(nn_ok, m + 1)
                last = nc.vector.scalar_tensor_tensor(out=a[:, m, :], in0=n[:, m, :], scalar=-1.0, in1=a[:, m, :], op0=ALU.mult, op1=ALU.mult)
            dve.wait_ge(bonus_mm, 1)
            nc.vector.tensor_copy(g["bonus"][:, :, :], bank[0][:, 0:J * H].rearrange("p (j h) -> p j h", j=J))
            dve.wait_ge(exp_ok, 3)
            for i in range(2):
                nc.vector.tensor_copy(rw["pc"][:, :, KT * i:KT * i + KT].rearrange("p c m -> p m c"), e1[HD * i:HD * i + HD, :, C - 1:T:C])

        @block.scalar
        def _(act):
            for m in range(KT):
                act.wait_ge(n_ok, m + 1)
                nc.scalar.activation(tmp[:, m, :], n[:, m, :], ACT.Square).then_inc(sq_ok, 1)
            for m in range(KT):
                act.wait_ge(sum_ok, m + 1)
                nc.scalar.activation(e2[:, m, :], bank[m][:, :], ACT.Sqrt).then_inc(root_ok, 1)
            act.wait_ge(ex_ok, KT)
            nc.scalar.activation(w[:, :, :], w[:, :, :], ACT.Exp, scale=DECAY).then_inc(exp_ok, 1)
            act.wait_ge(nn_ok, KT)
            nc.scalar.activation(e2[:, :, :], e1[:, :, :], ACT.Exp, scale=-DECAY).then_inc(exp_ok, 1)
            act.wait_ge(exp_ok, 2)
            nc.scalar.activation(e1[:, :, :], e1[:, :, :], ACT.Exp, scale=DECAY).then_inc(exp_ok, 1)

        @block.tensor
        def _(pe):
            for m in range(KT):
                pe.wait_ge(sq_ok, m + 1)
                nc.tensor.matmul(bank[m][:, :], g["blockones"][:, :], tmp[:, m, :], start=True, stop=True).then_inc(sum_ok, 1)
            pe.wait_ge(root_ok, KT)
            pe.wait_ge(small, 3)
            for m in range(KT):
                pe.wait_ge(rk_ok, m + 1)
                for j in range(J):
                    last = nc.tensor.matmul(bank[0][:, H * j + 2 * m:H * j + 2 * m + 2], tmp[:, m, j:T:J], hsel[:, m, :], start=True, stop=True)
            last.then_inc(bonus_mm, 1)


def rwkv_chunks(nc, io, g, rw):
    PAIRS, GP = H // 2, 4
    with Scope(nc, "chunks") as s:
        r, k, w, a, n, e1, e2, tmp = (rw[x] for x in ["r", "k", "w", "a", "n", "e1", "e2", "tmp"])
        tf = tmp[:, :, :].rearrange("p a b -> p (a b)")
        AR, BK, BKS = (tf[:, 1024 * i:1024 * i + 1024].rearrange("p (m x t) -> p m x t", m=KT, x=2) for i in range(3))
        first = s.sb("first", [P, H, 2 * C])
        second = s.sb("second", [P, H, 2 * C])
        nq = s.sb("nq", [P, PAIRS, 2, C])
        nt = s.sb("nt", [P, PAIRS, C])
        be = s.sb("be", [P, PAIRS, 2, C])
        n_diag, t_diag, q_diag = (s.sb(x, [P, PAIRS, 2 * C]) for x in ["n_diag", "t_diag", "q_diag"])
        sv = s.sb("sv", [P, H, HD])
        zv = s.sb("zv", [P, H, HD])
        decayed = s.sb("decayed", [C, H, HD])
        ybuf = s.sb("ybuf", [P, H, HD])
        bank = g["bank"]
        names = ["ar_ok", "bk_ok", "bks_ok", "lh_ok", "mm_done", "n_done", "t_done", "me_ok", "ne_ok", "te_ok", "q_ok", "lv_done", "td_ok", "nd_ok",
                 "nq_ev", "nt_ev", "o1_done", "z_ev", "yp_ev", "fe_done", "fe_ev_d", "fe_ev_a", "o2_done", "so_ev", "dec_ok", "v_in", "y_st"]
        sem = {x: s.sem(x) for x in names}
        setup, zeroed, turn = s.sem("setup"), s.sem("zeroed"), s.sem("turn")
        heads = lambda b: slice(b, H, 2)
        half = lambda b: slice(C * b, C * b + C)
        pairs = lambda gr: slice(GP * gr, GP * gr + GP)
        spread = lambda t, m: t.rearrange("p (x t) -> p x t", x=1).to_broadcast([t.shape[0], m, t.shape[1]])
        QUARTERS = [0, 2, 1, 3]
        NW, TW = [3, 4, 4, 3, 1, 2], [3, 3, 3, 3, 2]
        NQ_PER, NT_PER = 2 * sum(NW), 2 * sum(TW)
        nq_after = lambda lv, gr: 2 * sum(NW[:lv]) + (gr + 1) * NW[lv]
        nt_after = lambda lv, gr: 2 * sum(TW[:lv]) + (gr + 1) * TW[lv]
        block = s.enter_context(nc.Block())

        def waiter(eng, c):
            return lambda name, per, k: eng.wait_ge(sem[name], c * per + (k + 1))

        @block.sync
        def _(sp):
            for x in ["v_in", "y_st"]:
                sp.sem_inc(sem[x], 1)
            with sp.Fori(0, NC) as c:
                wait = waiter(sp, c)
                wait("o2_done", 2, 0)
                src = io["v_dram"][bass.ds(c * C, C), :]
                sp.dma_start(sv[C:P, :, :].rearrange("p h v -> p (h v)"), src).then_inc(sem["v_in"], 16)
                sp.dma_start(zv[C:P, :, :].rearrange("p h v -> p (h v)"), src).then_inc(sem["v_in"], 16)
                wait("so_ev", 4, 4)
                sp.dma_start(io["y_dram"][bass.ds(c * C, C), :], ybuf[C:P, :, :].rearrange("p h v -> p (h v)")).then_inc(sem["y_st"], 16)
            sp.wait_ge(sem["y_st"], 16 * NC + 1)

        @block.gpsimd
        def _(pool):
            for x in ["ar_ok", "bk_ok", "bks_ok", "lh_ok", "q_ok", "dec_ok"]:
                pool.sem_inc(sem[x], 1)
            nc.gpsimd.memset(sv[0:C, :, :], 0.0).then_inc(setup, 1)
            pool.wait_ge(setup, 1)
            nc.gpsimd.memset(second[C:P, :, C:2 * C], 0.0).then_inc(setup, 1)
            pool.wait_ge(setup, 2)
            with pool.Fori(0, NC) as c:
                wait = waiter(pool, c)
                wait("t_done", 2, 0)
                wait("n_done", 2, 0)
                pool.sem_inc(turn, 1)
                at = bass.ds(c * C, C)
                nc.gpsimd.tensor_tensor(BK[:, :, 0, :], a[:, :, at], e2[:, :, at], ALU.mult).then_inc(sem["bk_ok"], 1)
                nc.gpsimd.tensor_tensor(BK[:, :, 1, :], k[:, :, at], e2[:, :, at], ALU.mult).then_inc(sem["bk_ok"], 1)
                last_decay = e1[:, :, bass.ds(c * C + (C - 1), 1)].to_broadcast([P, KT, C])
                for i in range(2):
                    wait("bk_ok", 2, i + 1)
                    pool.sem_inc(turn, 1)
                    nc.gpsimd.tensor_tensor(BKS[:, :, i, :], BK[:, :, i, :], last_decay, ALU.mult).then_inc(sem["bks_ok"], 1)
                wait("lh_ok", 2, 0)
                pool.sem_inc(turn, 1)
                nc.gpsimd.tensor_tensor(AR[:, :, 0, :], n[:, :, at], w[:, :, at], ALU.mult).then_inc(sem["ar_ok"], 1)
                nc.gpsimd.tensor_tensor(AR[:, :, 1, :], r[:, :, at], e1[:, :, at], ALU.mult).then_inc(sem["ar_ok"], 1)
                wait("ar_ok", 2, 2)
                wait("o1_done", 2, 0)
                for i in range(2):
                    pool.sem_inc(turn, 1)
                    nc.gpsimd.tensor_copy(first[0:C, 8 * i:8 * i + 8, :], AR[half(i), :, :, :].rearrange("p m x t -> p m (x t)")).then_inc(sem["lh_ok"], 1)
                    wait("lh_ok", 2, i + 1)
                wait("so_ev", 4, 0)
                for i in range(2):
                    pool.sem_inc(turn, 1)
                    nc.gpsimd.tensor_tensor(decayed[:, i::2, :], sv[0:C, i::2, :],
                                            rw["pc"][:, bass.ds(c, 1), KT * i:KT * i + KT].rearrange("p a (m x) -> p (a m) x", x=1).to_broadcast([C, KT, HD]),
                                            ALU.mult).then_inc(sem["dec_ok"], 1)
                    wait("dec_ok", 2, i + 1)
                wait("ne_ok", 2, 2)
                for gr in range(2):
                    nc.gpsimd.tensor_tensor(nq[:, pairs(gr), 1, :], nq[:, pairs(gr), 0, :], spread(g["ident2"][:, :], GP), ALU.add).then_inc(sem["q_ok"], 1)

        @block.scalar
        def _(act):
            for x in ["te_ok", "td_ok", "nd_ok", "nt_ev", "z_ev", "fe_ev_a"]:
                act.sem_inc(sem[x], 1)
            act.wait_ge(zeroed, 3)
            with act.Fori(0, NC) as c:
                wait = waiter(act, c)
                for b in range(2):
                    wait("t_done", 2, b + 1)
                    src = bank[6 + b][:, :].rearrange("p (m r k) -> p m r k", m=GP, r=2)
                    for par in range(2):
                        nc.scalar.activation(be[half(par), pairs(b), 0, :], src[0:C, :, par, :], ACT.Copy).then_inc(sem["te_ok"], 1)
                        nc.scalar.activation(second[C:P, 8 * par + GP * b:8 * par + GP * b + GP, 0:C], src[C:P, :, par, :], ACT.Copy).then_inc(sem["te_ok"], 1)
                for i, q in enumerate(QUARTERS):
                    wait("me_ok", 12, 3 * i + 1)
                    nc.scalar.activation(t_diag[half(q // 2), pairs(q % 2), half(q // 2)], nt[half(q // 2), pairs(q % 2), :], ACT.Copy).then_inc(sem["td_ok"], 1)
                for b in range(2):
                    wait("ne_ok", 2, b + 1)
                    nc.scalar.activation(n_diag[half(b), :, half(b)], nq[half(b), :, 0, :], ACT.Copy).then_inc(sem["nd_ok"], 1)
                for lv in range(5):
                    for gr in range(2):
                        wait("lv_done", 12, 2 * lv + gr + 1)
                        src = bank[2 + gr][:, 0:GP * C].rearrange("p (h t) -> p h t", h=GP)
                        for b in range(2):
                            nc.scalar.activation(t_diag[half(b), pairs(gr), half(b)], src[half(b), :, :], ACT.Copy).then_inc(sem["nt_ev"], 1)
                        if lv < 4:
                            nc.scalar.activation(nt[:, pairs(gr), :], src, ACT.Copy).then_inc(sem["nt_ev"], 1)
                for b in range(2):
                    wait("o1_done", 2, b + 1)
                    nc.scalar.activation(zv[0:C, heads(b), :], bank[4 + b][0:C, :].rearrange("p (h v) -> p h v", h=8), ACT.Copy).then_inc(sem["z_ev"], 1)
                for gr in range(2):
                    wait("fe_done", 2, gr + 1)
                    nc.scalar.activation(second[0:C, 8 + GP * gr:8 + GP * gr + GP, :], bank[gr][C:P, :].rearrange("p (h x) -> p h x", h=GP), ACT.Copy).then_inc(sem["fe_ev_a"], 1)

        @block.vector
        def _(dve):
            for x in ["me_ok", "ne_ok", "nq_ev", "yp_ev", "fe_ev_d", "so_ev"]:
                dve.sem_inc(sem[x], 1)
            mask = g["chmask"]
            for t in (n_diag, t_diag, q_diag):
                nc.vector.memset(t[:, :, :], 0.0).then_inc(zeroed, 1)
            dve.wait_ge(zeroed, 3)
            with dve.Fori(0, NC) as c:
                wait = waiter(dve, c)
                for i, q in enumerate(QUARTERS):
                    wait("mm_done", 4, i + 1)
                    b = bank[q][:, :].rearrange("p (h x) -> p h x", h=GP)
                    top, at = half(q // 2), pairs(q % 2)
                    nc.vector.tensor_tensor(nt[top, at, :], b[0:C, :, 0:C], spread(mask[0:C, 0:C], GP), ALU.mult).then_inc(sem["me_ok"], 1)
                    nc.vector.tensor_tensor(be[top, at, 1, :], b[0:C, :, C:2 * C], spread(mask[0:C, C:2 * C], GP), ALU.mult).then_inc(sem["me_ok"], 1)
                    nc.vector.tensor_tensor(first[C:P, GP * q:GP * q + GP, :], b[C:P, :, :], spread(mask[C:P, :], GP), ALU.mult).then_inc(sem["me_ok"], 1)
                for b in range(2):
                    wait("n_done", 2, b + 1)
                    nc.vector.tensor_tensor(nq[half(b), :, 0, :], bank[4 + b][0:C, :].rearrange("p (h t) -> p h t", h=8),
                                            spread(g["lowmask"][:, :], 8), ALU.mult).then_inc(sem["ne_ok"], 1)
                for lv in range(6):
                    for gr in range(2):
                        wait("lv_done", 12, 2 * lv + gr + 1)
                        b = bank[gr][:, :].rearrange("p (h x t) -> p h x t", h=GP, x=2)
                        at = pairs(gr)
                        if lv == 0:
                            wait("q_ok", 2, gr + 1)
                        if 0 < lv < 5:
                            nc.vector.tensor_tensor(nq[:, at, 1, :], b[:, :, 1, :], nq[:, at, 1, :], ALU.add).then_inc(sem["nq_ev"], 1)
                        if lv < 3:
                            nc.vector.tensor_copy(nq[:, at, 0, :], b[:, :, 0, :]).then_inc(sem["nq_ev"], 1)
                        for x in range(2):
                            if lv < 4:
                                nc.vector.tensor_copy(n_diag[half(x), at, half(x)], b[half(x), :, 0, :]).then_inc(sem["nq_ev"], 1)
                            if lv == 5:
                                nc.vector.tensor_tensor(q_diag[half(x), at, half(x)], b[half(x), :, 1, :], nq[half(x), at, 1, :], ALU.add).then_inc(sem["nq_ev"], 1)
                wait("y_st", 16, 0)
                for b in range(2):
                    wait("o1_done", 2, b + 1)
                    nc.vector.tensor_copy(ybuf[C:P, heads(b), :], bank[4 + b][C:P, :].rearrange("p (h v) -> p h v", h=8)).then_inc(sem["yp_ev"], 1)
                for gr in range(2):
                    wait("fe_done", 2, gr + 1)
                    nc.vector.tensor_copy(second[0:C, GP * gr:GP * gr + GP, :], bank[gr][0:C, :].rearrange("p (h x) -> p h x", h=GP)).then_inc(sem["fe_ev_d"], 1)
                wait("dec_ok", 2, 2)
                wait("yp_ev", 2, 2)
                for b in range(2):
                    wait("o2_done", 2, b + 1)
                    o = bank[4 + b][:, :].rearrange("p (h v) -> p h v", h=8)
                    nc.vector.tensor_tensor(sv[0:C, heads(b), :], o[0:C, :, :], decayed[:, heads(b), :], ALU.add).then_inc(sem["so_ev"], 1)
                    nc.vector.tensor_tensor(ybuf[C:P, heads(b), :], o[C:P, :, :], ybuf[C:P, heads(b), :], ALU.add).then_inc(sem["so_ev"], 1)

        @block.tensor
        def _(pe):
            for x in ["mm_done", "n_done", "t_done", "lv_done", "o1_done", "fe_done", "o2_done"]:
                pe.sem_inc(sem[x], 1)
            pe.wait_ge(setup, 2)
            pe.wait_ge(zeroed, 3)
            head = lambda place: (2 * place, 0) if place < 8 else (2 * (place - 8) + 1, 1)
            flat = lambda t: t.rearrange("p x t -> p (x t)")
            with pe.Fori(0, NC) as c:
                wait = waiter(pe, c)
                wait("bks_ok", 2, 2)
                wait("te_ok", 8, 0)
                for m in range(KT):
                    ins = nc.tensor.transpose(bank[6 + m // 4][:, 128 * (m % 4):128 * (m % 4) + 128], flat(BKS[:, m, :, :]), g["ident"][:, :])
                    if m % 4 == 3:
                        ins.then_inc(sem["t_done"], 1)
                wait("ar_ok", 2, 2)
                wait("bk_ok", 2, 2)
                wait("fe_ev_d", 2, 0)
                wait("fe_ev_a", 2, 0)
                for q in QUARTERS:
                    for place in range(GP * q, GP * q + GP):
                        h, par = head(place)
                        ins = nc.tensor.matmul(bank[q][:, 128 * (place % 4):128 * (place % 4) + 128],
                                               flat(BK[half(par), h // 2, :, :]), flat(AR[half(par), h // 2, :, :]), start=True, stop=True)
                    ins.then_inc(sem["mm_done"], 1)
                wait("so_ev", 4, 0)
                pe.sem_inc(turn, 1)
                for place in range(H):
                    h, par = head(place)
                    ins = nc.tensor.matmul(bank[4 + place // 8][0:C, C * (place % 8):C * (place % 8) + C],
                                           AR[half(par), h // 2, 0, :], BK[half(par), h // 2, 0, :], start=True, stop=True)
                    if place % 8 == 7:
                        ins.then_inc(sem["n_done"], 1)
                for lv in range(6):
                    for gr in range(2):
                        if lv == 0:
                            wait("me_ok", 12, 6 * (gr + 1))
                            wait("ne_ok", 2, 2)
                            wait("td_ok", 4, 2 * (gr + 1))
                            wait("nd_ok", 2, 2)
                        else:
                            wait("nq_ev", NQ_PER, nq_after(lv - 1, gr))
                            wait("nt_ev", NT_PER, nt_after(lv - 1, gr))
                        if lv == 1:
                            wait("q_ok", 2, gr + 1)
                        lo, hi = (0, 1) if lv == 0 else (0, 2) if lv < 4 else (1, 2)
                        for i in range(GP):
                            ins = nc.tensor.matmul(bank[gr][:, 2 * C * i + C * lo:2 * C * i + C * hi], t_diag[:, GP * gr + i, :],
                                                   flat(nq[:, GP * gr + i, lo:hi, :]), start=True, stop=True)
                        if lv < 5:
                            for i in range(GP):
                                ins = nc.tensor.matmul(bank[2 + gr][:, C * i:C * i + C], n_diag[:, GP * gr + i, :], nt[:, GP * gr + i, :], start=True, stop=True)
                        ins.then_inc(sem["lv_done"], 1)
                wait("lh_ok", 2, 2)
                wait("v_in", 32, 32)
                for b in range(2):
                    for i in range(8):
                        ins = nc.tensor.matmul(bank[4 + b][:, HD * i:HD * i + HD], first[:, 8 * b + i, :], sv[:, 2 * i + b, :], start=True, stop=True)
                    ins.then_inc(sem["o1_done"], 1)
                wait("te_ok", 8, 8)
                for gr in range(2):
                    wait("nq_ev", NQ_PER, nq_after(5, gr))
                    for i in range(GP):
                        ins = nc.tensor.matmul(bank[gr][:, 128 * i:128 * i + 128], q_diag[:, GP * gr + i, :], flat(be[:, GP * gr + i, :, :]), start=True, stop=True)
                    ins.then_inc(sem["fe_done"], 1)
                for b in range(2):
                    wait("z_ev", 2, b + 1)
                    wait("yp_ev", 2, b + 1)
                    wait("fe_ev_a" if b else "fe_ev_d", 2, 2)
                    for i in range(8):
                        ins = nc.tensor.matmul(bank[4 + b][:, HD * i:HD * i + HD], second[:, 8 * b + i, :], zv[:, 2 * i + b, :], start=True, stop=True)
                    ins.then_inc(sem["o2_done"], 1)


def rwkv_finish(nc, io, g, rw):
    h = g["h"]
    with Scope(nc, "finish") as s:
        big = lambda x: rw[x][:, :, :].rearrange("p a b -> p (a b)").rearrange("p (j d) -> p j d", j=J)
        y, v, gate, sq, zT = big("r"), big("k"), big("w"), big("a"), rw["n"]
        ring = [rw[x][:, :, :] for x in ["e1", "e2"]]
        lnw, lnb = (rw["tmp"][:, 2 * i:2 * i + 2, :].rearrange("p a b -> p (a b)") for i in range(2))
        mu = s.sb("mu", [P, J, H])
        var = s.sb("var", [P, J, H])
        bank = g["bank"]
        y_in, vg_in, h_in, wo_in, order, mu_ok, cent_ok, sq_ok, var_ok, root_ok = map(
            s.sem, ["y_in", "vg_in", "h_in", "wo_in", "order", "mu_ok", "cent_ok", "sq_ok", "var_ok", "root_ok"])
        rstd_ok, normed, z_ok, tr, ev_a, ev_d, o_done, h_ok, pool_order, ln_in = map(
            s.sem, ["rstd_ok", "normed", "z_ok", "tr", "ev_a", "ev_d", "o_done", "h_ok", "pool_order", "ln_in"])
        wide = lambda t, j: t[:, j, :].rearrange("p (h x) -> p h x", x=1).to_broadcast([P, H, HD])
        split = lambda t, j: t[:, j, :].rearrange("p (h x) -> p h x", h=H)
        block = s.enter_context(nc.Block())

        @block.sync
        def _(sp):
            tiles = lambda d: d.rearrange("(p j) d -> p j d", j=J)
            sp.dma_start(y, tiles(io["y_dram"])).then_inc(y_in, 16)
            sp.dma_start(v, tiles(io["v_dram"])).then_inc(vg_in, 16)
            sp.dma_start(gate, tiles(io["g_dram"])).then_inc(vg_in, 16)
            sp.dma_start(lnw, io["rwkv_ln_w"].to_broadcast([P, D])).then_inc(ln_in, 16)
            sp.dma_start(lnb, io["rwkv_ln_b"].to_broadcast([P, D])).then_inc(ln_in, 16)
            for i in range(2):
                sp.dma_start(ring[i], io["rwkv_w_o"][0, :, 512 * i:512 * i + 512].rearrange("(k p) n -> p k n", p=P)).then_inc(wo_in, 16)
            sp.dma_start(h[:, :, :], tiles(io["x"][0])).then_inc(h_in, 16)

        @block.vector
        def _(dve):
            dve.wait_ge(y_in, 16)
            ch = Chain(dve, order)
            for j in range(J):
                nc.vector.tensor_reduce(out=mu[:, j, :], in_=split(y, j), axis=AX.X, op=ALU.add).then_inc(mu_ok, 1)
            for j in range(J):
                dve.wait_ge(mu_ok, j + 1)
                ch.link(nc.vector.tensor_scalar(mu[:, j, :], mu[:, j, :], 1.0 / HD, None, ALU.mult))
                nc.vector.tensor_tensor(split(y, j), split(y, j), wide(mu, j), ALU.subtract).then_inc(cent_ok, 1)
            dve.wait_ge(vg_in, 32)
            for j in range(J):
                ch.inc(nc.vector.tensor_tensor(split(v, j), split(v, j), wide(g["bonus"], j), ALU.mult))
            for j in range(J):
                dve.wait_ge(sq_ok, j + 1)
                nc.vector.tensor_reduce(out=var[:, j, :], in_=split(sq, j), axis=AX.X, op=ALU.add).then_inc(var_ok, 1)
                dve.wait_ge(root_ok, j + 1)
                nc.vector.reciprocal(var[:, j, :], var[:, j, :]).then_inc(rstd_ok, 1)
            ch.wait()
            for j in range(J):
                dve.wait_ge(normed, j + 1)
                ch.link(nc.vector.tensor_tensor(y[:, j, :], y[:, j, :], v[:, j, :], ALU.add))
                nc.vector.tensor_tensor(y[:, j, :], y[:, j, :], gate[:, j, :], ALU.mult).then_inc(z_ok, 1)
            for kt in range(1, KT, 2):
                dve.wait_ge(tr, kt + 1)
                nc.vector.tensor_copy(zT[:, kt, :], bank[kt][:, :]).then_inc(ev_d, 1)
            dve.wait_ge(h_in, 16)
            for u in range(2 * J):
                dve.wait_ge(o_done, u + 1)
                hh = h[:, u // 2, 512 * (u % 2):512 * (u % 2) + 512]
                nc.vector.tensor_tensor(hh, bank[u][:, :], hh, ALU.add).then_inc(h_ok, 1)

        @block.gpsimd
        def _(pool):
            ch = Chain(pool, pool_order)
            pool.wait_ge(ln_in, 32)
            for j in range(J):
                pool.wait_ge(rstd_ok, j + 1)
                ch.link(nc.gpsimd.tensor_tensor(split(y, j), split(y, j), wide(var, j), ALU.mult))
                ch.link(nc.gpsimd.tensor_tensor(y[:, j, :], y[:, j, :], lnw, ALU.mult))
                nc.gpsimd.tensor_tensor(y[:, j, :], y[:, j, :], lnb, ALU.add).then_inc(normed, 1)

        @block.scalar
        def _(act):
            for j in range(J):
                act.wait_ge(cent_ok, j + 1)
                nc.scalar.activation(sq[:, j, :], y[:, j, :], ACT.Square).then_inc(sq_ok, 1)
            for j in range(J):
                act.wait_ge(var_ok, j + 1)
                nc.scalar.activation(var[:, j, :], var[:, j, :], ACT.Sqrt, scale=1.0 / HD, bias=g["eps"][:, 1:2]).then_inc(root_ok, 1)
            for kt in range(0, KT, 2):
                act.wait_ge(tr, kt + 1)
                nc.scalar.activation(zT[:, kt, :], bank[kt][:, :], ACT.Copy).then_inc(ev_a, 1)

        @block.tensor
        def _(pe):
            pe.wait_ge(z_ok, J)
            for kt in range(KT):
                for j in range(J):
                    last = nc.tensor.transpose(bank[kt][:, P * j:P * j + P], y[:, j, P * kt:P * kt + P], g["ident"][:, :])
                last.then_inc(tr, 1)
            pe.wait_ge(ev_a, KT // 2)
            pe.wait_ge(ev_d, KT // 2)
            pe.wait_ge(wo_in, 32)
            for u in range(2 * J):
                for kt in range(KT):
                    last = nc.tensor.matmul(bank[u][:, :], zT[:, kt, P * (u // 2):P * (u // 2) + P], ring[u % 2][:, kt, :], start=kt == 0, stop=kt == KT - 1)
                last.then_inc(o_done, 1)


def moe(nc, io, g, layer):
    h, bank = g["h"], g["bank"]
    NE, NG, EG = 16, 4, 4
    FH = D // 2
    SPLITS = 4
    PIECE = 2048
    with Scope(nc, f"moe{layer}") as s:
        xn = s.sb("xn", [P, J, D])
        xnT = s.sb("xnT", [P, KT, T])
        gb = s.sb("gb", [P, D])
        raw = [s.sb(f"raw{i}", [P, PIECE]) for i in range(6)]
        whi = [s.sb(f"whi{i}", [P, PIECE], fp32r) for i in range(SPLITS)]
        wlo = [s.sb(f"wlo{i}", [P, PIECE], fp32r) for i in range(SPLITS)]
        xg = s.sb("xg", [P, D])
        xhi = [s.sb(f"xhi{i}", [P, KT, P], fp32r) for i in range(2)]
        xlo = [s.sb(f"xlo{i}", [P, KT, P], fp32r) for i in range(2)]
        sg = s.sb("sg", [P, FH])
        hid = s.sb("hid", [P, FH])
        hhi = s.sb("hhi", [P, FH // P, P], fp32r)
        hlo = s.sb("hlo", [P, FH // P, P], fp32r)
        yo = s.sb("yo", [P, D])
        wr = s.sb("wr", [P, KT, NG + NE])
        br = s.sb("br", [P, NG + NE])
        ss, rstd = s.sb("ss", [P, J]), s.sb("rstd", [P, J])
        lg = s.sb("logits", [P, J, NG + NE])
        v4 = [s.sb(f"v4_{i}", [P, J]) for i in range(10)]
        v16 = [s.sb(f"v16_{i}", [P, J, 4]) for i in range(7)]
        v64 = [s.sb(f"v64_{i}", [P, J, NG, EG]) for i in range(5)]
        rank = s.sb("rank", [P, J, NE])
        msum = s.sb("msum", [P, NE])
        posf = s.sb("posf", [P, 2, J])
        pos = s.sb("pos", [P, 2, J], i32)
        first_place, later = s.sb("first_place", [P, 2, J]), s.sb("later", [P, 2, J])
        wgt = s.sb("wgt", [P, 2, J])
        zeros = s.sb("zeros", [NE * J, P])
        tokrow = s.sb("tokrow", [NE * J, P])
        idx = s.sb("idx", [P, NE * J], i32)
        idxcol = s.sb("idxcol", [P, 1], i32)
        most = s.sb("most", [P, 2])
        mosti = s.sb("mosti", [P, 1], i32)
        par_in, sumsq, rms, rstd_ok, xhat_ok, xn_ok, xn_st, tr, ev_a, ev_d, lg_done, order = map(
            s.sem, ["par_in", "sumsq", "rms", "rstd_ok", "xhat_ok", "xn_ok", "xn_st", "tr", "ev_a", "ev_d", "lg_done", "order"])
        gs_ok, eg_ok, d_ok, e2_ok, ms_ok, rank_done, pos_ok, tok_zero, tok_st, tok_in, tok_tr, idx_ok, zero_ok = map(
            s.sem, ["gs_ok", "eg_ok", "d_ok", "e2_ok", "ms_ok", "rank_done", "pos_ok", "tok_zero", "tok_st", "tok_in", "tok_tr", "idx_ok", "zero_ok"])
        comb_in = [s.sem(f"comb_in{i}") for i in range(J)]
        comb_ok, turn = s.sem("comb_ok"), s.sem("turn")

        def loop_sems(tag):
            r = {x: s.sem(tag + x) for x in ["hi_ok", "split_ok", "piece_used", "xt_done", "xh_ok", "xl_ok", "sg_ok", "hid_ok", "ht_done", "hh_ok", "hl_ok",
                                             "y_ok", "col_ok", "xg_in", "y_st"]}
            r["lead"] = 2 if tag else SPLITS
            r["raw_in"] = [s.sem(f"{tag}raw_in{i}") for i in range(6)]
            return r

        main, more = loop_sems(""), loop_sems("more_")
        xn_dram, tok_dram, out_dram = io[f"xn_dram{layer}"], io[f"tok_dram{layer}"], io[f"out_dram{layer}"]
        block = s.enter_context(nc.Block())

        xnT2 = xnT[:, :, :].rearrange("p a b -> p (a b)").rearrange("p (j d) -> p j d", j=J)

        def start(eng, m, names):
            for x in names:
                eng.sem_inc(m[x], {"split_ok": 6, "piece_used": m["lead"]}.get(x, 1))

        def load_piece(sp, m, n, slot, kind, e, half):
            sp.wait_ge(m["split_ok"], n + 1)
            w = io["moe_w_" + kind][layer, bass.ds(e, 1), :, :]
            w = w[:, :, 512 * half:512 * half + 512] if kind == "down" else w[:, 512 * half:512 * half + 512, :]
            sp.dma_start(raw[slot % 6][:, :].rearrange("p (k n) -> p k n", k=4),
                         w.rearrange("a (k p) n -> p (a k) n", p=P)).then_inc(m["raw_in"][slot % 6], 16)

        def split_hi(act, m, n, slot, uses):
            act.wait_ge(m["raw_in"][slot % 6], uses * 16)
            act.wait_ge(m["piece_used"], n + 1)
            nc.scalar.activation(whi[slot % SPLITS][:, :], raw[slot % 6][:, :], ACT.Copy).then_inc(m["hi_ok"], 1)

        def split_lo(dve, m, n, slot):
            dve.wait_ge(m["hi_ok"], n + 2)
            nc.vector.tensor_tensor(wlo[slot % SPLITS][:, :], raw[slot % 6][:, :], whi[slot % SPLITS][:, :].bitcast(fp32), ALU.subtract).then_inc(m["split_ok"], 1)

        def product(pe, m, n, slot, b, hi, lo, k0, begin, end):
            pe.wait_ge(m["split_ok"], n + 7)
            wh, wl = (w[slot % SPLITS][:, :].rearrange("p (k n) -> p k n", k=4) for w in (whi, wlo))
            for k in range(4):
                nc.tensor.matmul(bank[b][:, :], hi[:, k0 + k, :], wh[:, k, :], start=begin and k == 0, stop=False)
                nc.tensor.matmul(bank[b][:, :], hi[:, k0 + k, :], wl[:, k, :], start=False, stop=False)
                ins = nc.tensor.matmul(bank[b][:, :], lo[:, k0 + k, :], wh[:, k, :], start=False, stop=end and k == 3)
            ins.then_inc(m["piece_used"], 1)

        def pe_tokens(pe, m, c):
            pe.wait_ge(m["xg_in"], c * 16 + 16)
            pe.wait_ge(m["xl_ok"], c * 2 + 1)
            for kt in range(KT):
                ins = nc.tensor.transpose(bank[kt // 4][:, P * (kt % 4):P * (kt % 4) + P], xg[:, P * kt:P * kt + P], g["ident"][:, :])
            ins.then_inc(m["xt_done"], 1)

        def pe_hidden(pe, m, c):
            pe.wait_ge(m["hid_ok"], c + 2)
            pe.wait_ge(m["hl_ok"], c + 1)
            for kt in range(FH // P):
                ins = nc.tensor.transpose(bank[4][:, P * kt:P * kt + P], hid[:, P * kt:P * kt + P], g["ident"][:, :])
            ins.then_inc(m["ht_done"], 1)

        def pe_gate(pe, m, c, x, half, n, slot):
            if half == 0:
                pe.wait_ge(m["xl_ok"], c * 2 + 3)
                pe.wait_ge(m["sg_ok"], c + 1)
            product(pe, m, n, slot, 2, xhi[x], xlo[x], 4 * half, half == 0, half == 1)

        def pe_up(pe, m, c, x, half, n, slot):
            if half == 0:
                pe.wait_ge(m["hid_ok"], c + 1)
            product(pe, m, n, slot, 3, xhi[x], xlo[x], 4 * half, half == 0, half == 1)

        def pe_down(pe, m, c, half, n, slot):
            pe.wait_ge(m["y_ok"], c * 2 + 1)
            if half == 0:
                pe.wait_ge(m["hl_ok"], c + 2)
            product(pe, m, n, slot, 5 + half, hhi, hlo, 0, True, True)

        def act_tokens(act, m, c, x):
            act.wait_ge(m["xt_done"], c + 2)
            for b in range(2):
                nc.scalar.activation(xhi[x][:, 4 * b:4 * b + 4, :], bank[b][:, :].rearrange("p (k t) -> p k t", k=4), ACT.Copy).then_inc(m["xh_ok"], 1)

        def dve_tokens(dve, m, c, x):
            for b in range(2):
                dve.wait_ge(m["xh_ok"], c * 2 + b + 2)
                nc.vector.tensor_tensor(xlo[x][:, 4 * b:4 * b + 4, :], bank[b][:, :].rearrange("p (k t) -> p k t", k=4),
                                        xhi[x][:, 4 * b:4 * b + 4, :].bitcast(fp32), ALU.subtract).then_inc(m["xl_ok"], 1)

        def act_gate(act, m, c, n):
            act.wait_ge(m["piece_used"], n + m["lead"] + 1)
            act.wait_ge(m["hid_ok"], c + 1)
            nc.scalar.activation(sg[:, :], bank[2][:, :], ACT.Silu).then_inc(m["sg_ok"], 1)

        def dve_up(dve, m, c, n):
            dve.wait_ge(m["piece_used"], n + m["lead"] + 1)
            dve.wait_ge(m["sg_ok"], c + 2)
            dve.wait_ge(m["ht_done"], c + 1)
            nc.vector.tensor_tensor(hid[:, :], bank[3][:, :], sg[:, :], ALU.mult).then_inc(m["hid_ok"], 1)

        def act_hidden(act, m, c):
            act.wait_ge(m["ht_done"], c + 2)
            nc.scalar.activation(hhi[:, :, :], bank[4][:, :].rearrange("p (k t) -> p k t", k=4), ACT.Copy).then_inc(m["hh_ok"], 1)

        def dve_hidden(dve, m, c):
            dve.wait_ge(m["hh_ok"], c + 2)
            nc.vector.tensor_tensor(hlo[:, :, :], bank[4][:, :].rearrange("p (k t) -> p k t", k=4), hhi[:, :, :].bitcast(fp32),
                                    ALU.subtract).then_inc(m["hl_ok"], 1)

        def act_output(act, m, c, half, n):
            act.wait_ge(m["piece_used"], n + m["lead"] + 1)
            if half == 0:
                act.wait_ge(m["y_st"], c * 16 + 1)
            nc.scalar.activation(yo[:, 512 * half:512 * half + 512], bank[5 + half][:, :], ACT.Copy).then_inc(m["y_ok"], 1)

        def store_output(act, m, c, row):
            act.wait_ge(m["y_ok"], c * 2 + 3)
            act.dma_start(out_dram[bass.ds(row, P), :], yo[:, :]).then_inc(m["y_st"], 16)

        def piece(e, x, k):
            if isinstance(e, int) and e == 0:
                return k, k, 1
            return e * 6 + (k - 2), (6 * x + k - 2) % 12, e + (0 if k < 2 else 1)

        def rounds(eng, body):
            body(0, 0)
            with eng.Fori(0, NE // 2 - 1) as i:
                body(i * 2 + 1, 1)
                body(i * 2 + 2, 0)
            body(NE - 1, 1)

        def each_further(eng, body):
            with eng.Fori(0, NE) as e:
                with eng.Fori(1, J) as b:
                    body(e, b, e * (J - 1) + (b - 1))

        def overflow(eng):
            longest = eng.value_load(mosti[0:1, 0:1], min_val=0, max_val=T)
            return eng.If(longest > P)

        def no_overflow(eng):
            return eng.If(eng.value_load(mosti[0:1, 0:1], min_val=0, max_val=T) < P + 1)

        @block.sync
        def _(sp):
            sp.dma_start(gb[:, :], io["norm_ffn_g"][layer:layer + 1, :].to_broadcast([P, D])).then_inc(par_in, 16)
            sp.dma_start(wr[:, :, 0:NG], io["moe_w_grp"][layer].rearrange("(k p) n -> p k n", p=P)).then_inc(par_in, 16)
            sp.dma_start(wr[:, :, NG:], io["moe_w_exp"][layer].rearrange("(k p) n -> p k n", p=P)).then_inc(par_in, 16)
            sp.dma_start(br[:, 0:NG], io["moe_b_grp"][layer:layer + 1, :].to_broadcast([P, NG])).then_inc(par_in, 16)
            sp.dma_start(br[:, NG:], io["moe_b_exp"][layer:layer + 1, :].to_broadcast([P, NE])).then_inc(par_in, 16)
            sp.wait_ge(zero_ok, 1)
            sp.dma_start(tok_dram.rearrange("(a b) x -> a (b x)", b=P), zeros[:, :]).then_inc(tok_zero, 16)
            def load_round(e, x):
                first = isinstance(e, int) and e == 0
                todo = [("gate", 0, e), ("gate", 1, e)] + ([] if first else [("down", 0, e - 1), ("down", 1, e - 1)]) + [("up", 0, e), ("up", 1, e)]
                for k, (kind, half, ee) in enumerate(todo):
                    n, slot, uses = piece(e, x, k)
                    load_piece(sp, main, n, slot, kind, ee, half)

            rounds(sp, load_round)
            for half in range(2):
                n, slot, uses = piece(NE, 0, half)
                load_piece(sp, main, n, slot, "down", NE - 1, half)
            sp.wait_ge(pos_ok, 2)
            with overflow(sp):
                sp.wait_ge(main["split_ok"], 6 + 6 * NE)

                def further_round(e, b, c):
                    for k, (kind, half) in enumerate([("gate", 0), ("gate", 1), ("up", 0), ("up", 1), ("down", 0), ("down", 1)]):
                        load_piece(sp, more, c * 6 + k, k, kind, e, half)

                each_further(sp, further_round)

        @block.gpsimd
        def _(pool):
            nc.gpsimd.memset(zeros[:, :], 0.0).then_inc(zero_ok, 1)
            start(pool, main, ["col_ok"])
            pool.wait_ge(pos_ok, 2)
            pool.wait_ge(tok_zero, 16)
            for k in range(2):
                for j in range(J):
                    pool.indirect_dma_start(tok_dram, bass.IndirectOffsetOnAxis(ap=pos[:, k, j:j + 1], axis=0), g["tokid"][:, j:j + 1], None).then_inc(tok_st, 16)
            pool.wait_ge(tok_st, 16 * 2 * J)
            pool.dma_start(tokrow[:, :], tok_dram.rearrange("(a b) x -> a (b x)", b=P)).then_inc(tok_in, 16)
            pool.wait_ge(idx_ok, 1)
            pool.wait_ge(xn_st, 16)

            def fetch(m, col, c):
                pool.wait_ge(m["xt_done"], c + 1)
                nc.gpsimd.tensor_copy(idxcol[:, :], idx[:, bass.ds(col, 1)]).then_inc(m["col_ok"], 1)
                pool.wait_ge(m["col_ok"], c + 2)
                pool.sem_inc(turn, 1)
                pool.indirect_dma_start(xg[:, :], None, xn_dram, bass.IndirectOffsetOnAxis(ap=idxcol[:, :], axis=0)).then_inc(m["xg_in"], 16)

            with pool.Fori(0, NE) as e:
                fetch(main, e, e)
            with overflow(pool):
                start(pool, more, ["col_ok"])
                pool.wait_ge(main["xt_done"], NE + 1)
                each_further(pool, lambda e, b, c: fetch(more, b * NE + e, c))
            pool.wait_ge(main["y_st"], 16 * NE + 1)
            with overflow(pool):
                pool.wait_ge(more["y_st"], 16 * NE * (J - 1) + 1)

            def outputs(rows):
                for j in range(J):
                    for k in range(2):
                        dst = (xn if k == 0 else xnT2)[:, j, :]
                        pool.indirect_dma_start(dst, None, rows, bass.IndirectOffsetOnAxis(ap=pos[:, k, j:j + 1], axis=0)).then_inc(comb_in[j], 16)

            with overflow(pool):
                outputs(out_dram)
            with no_overflow(pool):
                outputs(out_dram[0:NE * P, :])
            for j in range(J):
                pool.wait_ge(comb_in[j], 32)

        @block.scalar
        def _(act):
            start(act, main, ["hi_ok", "xh_ok", "sg_ok", "hh_ok", "y_ok", "y_st"])
            for j in range(J):
                nc.scalar.activation(yo[:, :], h[:, j, :], ACT.Square, accum_out=ss[:, j:j + 1]).then_inc(sumsq, 1)
                act.wait_ge(sumsq, j + 1)
            nc.scalar.activation(ss[:, :], ss[:, :], ACT.Sqrt, scale=1.0 / D, bias=g["eps"][:, 0:1]).then_inc(rms, 1)
            act.wait_ge(xn_ok, J)
            act.dma_start(xn_dram.rearrange("(p j) d -> p j d", j=J), xn[:, :, :]).then_inc(xn_st, 16)
            for kt in range(0, KT, 2):
                act.wait_ge(tr, kt + 1)
                nc.scalar.activation(xnT[:, kt, :], bank[kt][:, :], ACT.Copy).then_inc(ev_a, 1)
            act.wait_ge(gs_ok, 1)
            nc.scalar.activation(v16[0][:, :, :], v16[0][:, :, :], ACT.Exp).then_inc(eg_ok, 1)
            act.wait_ge(d_ok, 1)
            nc.scalar.activation(v4[5][:, :], v4[5][:, :], ACT.Exp).then_inc(e2_ok, 1)
            act.wait_ge(rank_done, 1)
            for k in range(SPLITS):
                split_hi(act, main, *piece(0, 0, k))
            act_tokens(act, main, 0, 0)

            def round_(e, x):
                first, last = (isinstance(e, int) and e == v for v in (0, NE - 1))
                todo = ([] if first else [piece(e, x, k) for k in (4, 5)]) + [piece(e + 1, 1 - x, k) for k in range(2 if last else 4)]
                hi = lambda: split_hi(act, main, *todo.pop(0))
                if not first:
                    act_hidden(act, main, e - 1)
                    hi()
                act_gate(act, main, e, piece(e, x, 1)[0])
                hi()
                if not first:
                    act_output(act, main, e - 1, 0, piece(e, x, 2)[0])
                    hi()
                    act_output(act, main, e - 1, 1, piece(e, x, 3)[0])
                    store_output(act, main, e - 1, (e - 1) * P)
                if not last:
                    act_tokens(act, main, e + 1, 1 - x)
                while todo:
                    hi()

            rounds(act, round_)
            act_hidden(act, main, NE - 1)
            for half in range(2):
                act_output(act, main, NE - 1, half, piece(NE, 0, half)[0])
            store_output(act, main, NE - 1, (NE - 1) * P)
            with overflow(act):
                start(act, more, ["hi_ok", "xh_ok", "sg_ok", "hh_ok", "y_ok", "y_st"])
                act.wait_ge(main["y_st"], 16 * NE + 1)

                def further_round(e, b, c):
                    act_tokens(act, more, c, 0)
                    for k in range(6):
                        split_hi(act, more, c * 6 + k, k, c + 1)
                        if k == 3:
                            act_gate(act, more, c, c * 6 + 1)
                    act_hidden(act, more, c)
                    for half in range(2):
                        act_output(act, more, c, half, c * 6 + (4 + half))
                    store_output(act, more, c, b * (NE * P) + e * P)

                each_further(act, further_round)

        @block.vector
        def _(dve):
            start(dve, main, ["split_ok", "xl_ok", "hid_ok", "hl_ok"])
            dve.wait_ge(rms, 1)
            nc.vector.reciprocal(rstd[:, :], ss[:, :]).then_inc(rstd_ok, 1)
            dve.wait_ge(rstd_ok, 1)
            dve.wait_ge(par_in, 80)
            for j in range(J):
                nc.vector.scalar_tensor_tensor(out=xn[:, j, :], in0=h[:, j, :], scalar=rstd[:, j:j + 1], in1=gb[:, :], op0=ALU.mult, op1=ALU.mult).then_inc(xn_ok, 1)
            for kt in range(1, KT, 2):
                dve.wait_ge(tr, kt + 1)
                nc.vector.tensor_copy(xnT[:, kt, :], bank[kt][:, :]).then_inc(ev_d, 1)
            ch = Chain(dve, order)
            V = nc.vector
            gl = lg[:, :, 0:NG]
            el = lg[:, :, NG:].rearrange("p j (g e) -> p j g e", g=NG)
            over = lambda t: t[:, :].rearrange("p (j x) -> p j x", x=1).to_broadcast([P, J, 4])
            reduce = lambda out, in_, op: ch.link(V.tensor_reduce(out=out, in_=in_, axis=AX.X, op=op))
            tt = lambda out, a, b, op: ch.link(V.tensor_tensor(out, a, b, op))
            dve.wait_ge(lg_done, 1)
            tt(lg[:, :, :], bank[0][:, 0:J * (NG + NE)].rearrange("p (j n) -> p j n", j=J),
               br[:, :].rearrange("p (x n) -> p x n", x=1).to_broadcast([P, J, NG + NE]), ALU.add)
            gm, psum, m1, m2, top, dd = v4[0], v4[1], v4[2], v4[3], v4[4], v4[5]
            reduce(gm[:, :], gl, ALU.max)
            V.tensor_tensor(v16[0][:, :, :], gl, over(gm), ALU.subtract).then_inc(gs_ok, 1)

            def first_equal(out, vals, m):
                tt(out[:, :, :], vals, over(m), ALU.is_equal)
                tt(out[:, :, :], out[:, :, :], g["down4"][:, :].rearrange("p (x n) -> p x n", x=1).to_broadcast([P, J, 4]), ALU.mult)
                reduce(top[:, :], out[:, :, :], ALU.max)
                tt(out[:, :, :], out[:, :, :], over(top), ALU.is_equal)

            og, sel, o1, sel2, o2 = v16[1], v16[2], v16[3], v16[4], v16[5]
            first_equal(og, gl, gm)
            inner = lambda t: t[:, :, :].rearrange("p j (n x) -> p j n x", x=1).to_broadcast([P, J, NG, EG])
            outer = lambda t: t[:, :, :].rearrange("p j (x n) -> p j x n", x=1).to_broadcast([P, J, NG, EG])
            tt(v64[0][:, :, :, :], el, inner(og), ALU.mult)
            reduce(sel[:, :, :], v64[0][:, :, :, :].rearrange("p j g e -> p j e g"), ALU.add)
            reduce(m1[:, :], sel[:, :, :], ALU.max)
            first_equal(o1, sel[:, :, :], m1)
            ch.link(V.scalar_tensor_tensor(out=sel2[:, :, :], in0=o1[:, :, :], scalar=-3.0e38, in1=sel[:, :, :], op0=ALU.mult, op1=ALU.add))
            reduce(m2[:, :], sel2[:, :, :], ALU.max)
            V.tensor_tensor(dd[:, :], m2[:, :], m1[:, :], ALU.subtract).then_inc(d_ok, 1)
            first_equal(o2, sel2[:, :, :], m2)
            M1, M2, M = v64[1], v64[2], v64[3]
            tt(M1[:, :, :, :], inner(og), outer(o1), ALU.mult)
            tt(M2[:, :, :, :], inner(og), outer(o2), ALU.mult)
            tt(M[:, :, :, :], M1[:, :, :, :], M2[:, :, :, :], ALU.add)
            flat = lambda t: t[:, :, :, :].rearrange("p j g e -> p j (g e)")
            V.tensor_reduce(out=msum[:, :], in_=flat(M).rearrange("p j n -> p n j"), axis=AX.X, op=ALU.add).then_inc(ms_ok, 1)
            dve.wait_ge(eg_ok, 1)
            reduce(psum[:, :], v16[0][:, :, :], ALU.add)
            dve.wait_ge(e2_ok, 1)
            ch.link(V.tensor_scalar(v4[6][:, :], dd[:, :], 1.0, None, ALU.add))
            tt(v4[6][:, :], v4[6][:, :], psum[:, :], ALU.mult)
            ch.link(V.reciprocal(wgt[:, 0, :], v4[6][:, :]))
            tt(wgt[:, 1, :], wgt[:, 0, :], dd[:, :], ALU.mult)
            dve.wait_ge(rank_done, 1)
            ch.link(V.tensor_copy(rank[:, 0, :], bank[1][:, 0:NE]))
            for j in range(1, J):
                tt(rank[:, j, :], rank[:, j - 1, :], flat(M)[:, j - 1, :], ALU.add)
            for k, Mk in enumerate([M1, M2]):
                tt(v64[4][:, :, :, :].rearrange("p j g e -> p j (g e)"), flat(Mk), rank[:, :, :], ALU.mult)
                reduce(posf[:, k, :], flat(v64[4]), ALU.add)
                tt(flat(v64[4]), flat(Mk), g["base16"][:, :].rearrange("p (x n) -> p x n", x=1).to_broadcast([P, J, NE]), ALU.mult)
                reduce(first_place[:, k, :], flat(v64[4]), ALU.add)
            for b in range(1, J):
                ch.link(V.tensor_scalar(later[:, :, :], posf[:, :, :], float(P * b), float(NE * P - P), ALU.is_ge, ALU.mult))
                tt(first_place[:, :, :], first_place[:, :, :], later[:, :, :], ALU.add)
            tt(posf[:, :, :], posf[:, :, :], first_place[:, :, :], ALU.add)
            V.tensor_copy(pos[:, :, :], posf[:, :, :]).then_inc(pos_ok, 1)
            reduce(most[:, 0:1], bank[1][:, NE:2 * NE], ALU.max)
            V.tensor_copy(mosti[:, :], most[:, 0:1]).then_inc(pos_ok, 1)
            dve.wait_ge(tok_tr, 1)
            V.tensor_copy(idx[:, 0:NE * J], bank[2][:, 0:NE * J]).then_inc(idx_ok, 1)
            for k in range(SPLITS):
                split_lo(dve, main, *piece(0, 0, k)[:2])
            dve_tokens(dve, main, 0, 0)

            def round_(e, x):
                first, last = (isinstance(e, int) and e == v for v in (0, NE - 1))
                todo = ([] if first else [piece(e, x, k) for k in (4, 5)]) + [piece(e + 1, 1 - x, k) for k in range(2 if last else 4)]
                lo = lambda: split_lo(dve, main, *todo.pop(0)[:2])
                if not first:
                    dve_hidden(dve, main, e - 1)
                    lo()
                    lo()
                lo()
                if not last:
                    dve_tokens(dve, main, e + 1, 1 - x)
                while len(todo) > 1:
                    lo()
                dve_up(dve, main, e, piece(e, x, 3 if first else 5)[0])
                lo()

            rounds(dve, round_)
            dve_hidden(dve, main, NE - 1)
            with overflow(dve):
                start(dve, more, ["split_ok", "xl_ok", "hid_ok", "hl_ok"])

                def further_round(e, b, c):
                    dve_tokens(dve, more, c, 0)
                    for k in range(6):
                        split_lo(dve, more, c * 6 + k, k)
                    dve_up(dve, more, c, c * 6 + 3)
                    dve_hidden(dve, more, c)

                each_further(dve, further_round)
            for j in range(J):
                dve.wait_ge(comb_in[j], 32)
                for k in range(2):
                    src = (xn if k == 0 else xnT2)[:, j, :]
                    V.scalar_tensor_tensor(out=h[:, j, :], in0=src, scalar=wgt[:, k, j:j + 1], in1=h[:, j, :], op0=ALU.mult, op1=ALU.add).then_inc(comb_ok, 1)
                    dve.wait_ge(comb_ok, 2 * j + k + 1)

        @block.tensor
        def _(pe):
            start(pe, main, ["piece_used", "xt_done", "ht_done"])
            pe.wait_ge(xn_ok, J)
            for kt in range(KT):
                for j in range(J):
                    last = nc.tensor.transpose(bank[kt][:, P * j:P * j + P], xn[:, j, P * kt:P * kt + P], g["ident"][:, :])
                last.then_inc(tr, 1)
            pe.wait_ge(ev_a, KT // 2)
            pe.wait_ge(ev_d, KT // 2)
            pe.wait_ge(par_in, 80)
            for j in range(J):
                for kt in range(KT):
                    last = nc.tensor.matmul(bank[0][:, (NG + NE) * j:(NG + NE) * (j + 1)], xnT[:, kt, P * j:P * j + P], wr[:, kt, :], start=kt == 0, stop=kt == KT - 1)
            last.then_inc(lg_done, 1)
            pe.wait_ge(ms_ok, 1)
            nc.tensor.matmul(bank[1][:, 0:NE], g["upper"][:, :], msum[:, :], start=True, stop=True)
            nc.tensor.matmul(bank[1][:, NE:2 * NE], g["ones"][:, :], msum[:, :], start=True, stop=True).then_inc(rank_done, 1)
            pe.wait_ge(tok_in, 16)
            nc.tensor.transpose(bank[2][:, 0:NE * J], tokrow[:, :], g["ident"][0:NE * J, 0:NE * J]).then_inc(tok_tr, 1)
            pe.wait_ge(idx_ok, 1)
            pe_tokens(pe, main, 0)

            def round_(e, x):
                first, last = (isinstance(e, int) and e == v for v in (0, NE - 1))
                k = iter(range(6))
                at = lambda: piece(e, x, next(k))[:2]
                pe_gate(pe, main, e, x, 0, *at())
                if not first:
                    pe_hidden(pe, main, e - 1)
                pe_gate(pe, main, e, x, 1, *at())
                if not first:
                    for half in range(2):
                        pe_down(pe, main, e - 1, half, *at())
                if not last:
                    pe_tokens(pe, main, e + 1)
                for half in range(2):
                    pe_up(pe, main, e, x, half, *at())

            rounds(pe, round_)
            pe_hidden(pe, main, NE - 1)
            for half in range(2):
                pe_down(pe, main, NE - 1, half, *piece(NE, 0, half)[:2])
            with overflow(pe):
                start(pe, more, ["piece_used", "xt_done", "ht_done"])
                pe.wait_ge(main["y_ok"], 2 * NE + 1)

                def further_round(e, b, c):
                    pe_tokens(pe, more, c)
                    for k, part in enumerate([pe_gate, pe_up]):
                        for half in range(2):
                            part(pe, more, c, 0, half, c * 6 + (2 * k + half), 2 * k + half)
                    pe_hidden(pe, more, c)
                    for half in range(2):
                        pe_down(pe, more, c, half, c * 6 + (4 + half), 4 + half)

                each_further(pe, further_round)



def attention(nc, io, g):
    h, bank = g["h"], g["bank"]
    G, AH = 3, 8
    W = AH * HD
    SCALE = HD ** -0.5
    FAR = -1.0e30
    with Scope(nc, "attn") as s:
        xhat = s.sb("xhat", [P, J, D])
        xk = s.sb("xk", [P, KT, T])
        xq = s.sb("xq", [P, KT, T])
        ring = [s.sb(f"ring{i}", [P, KT, W]) for i in range(3)]
        kT = [s.sb(f"kT{i}", [P, AH // 2, T]) for i in range(G)]
        qT = [s.sb(f"qT{i}", [P, AH // 2, T]) for i in range(G)]
        vv = [s.sb(f"v{i}", [P, J, W]) for i in range(G)]
        sm, pr, pT = ([xhat[:, n, 512 * i:512 * i + 512] for i in range(2)] for n in range(3))
        oacc = [xk[:, 0:4, :], xk[:, 4:8, :], xq[:, 0:4, :]]
        oT = xq[:, 4:8, :]
        mask = [s.sb("mask0", [P, J, T]), s.sb("mask1", [P, P]), s.sb("mask2", [P, P])]
        residue = s.sb("residue", [P, P])
        ss, rstd = s.sb("ss", [P, J]), s.sb("rstd", [P, J])
        negm = s.sb("negm", [P, G, J, AH])
        lsum = s.sb("lsum", [P, G, J, AH])
        least = s.sb("least", [P, J, AH])
        den = s.sb("den", [P, J, AH])
        sumsq, rms, rstd_ok, xhat_ok, tr, xk_ok, xq_ok, unit, ev_a, ev_d = map(
            s.sem, ["sumsq", "rms", "rstd_ok", "xhat_ok", "tr", "xk_ok", "xq_ok", "unit", "ev_a", "ev_d"])
        pool_order, mask_ok, res_mm, m2_ok, s_done, sm_ok, max_ok, p_ok, t_done, pt_ok, o_done, o_ev = map(
            s.sem, ["pool_order", "mask_ok", "res_mm", "m2_ok", "s_done", "sm_ok", "max_ok", "p_ok", "t_done", "pt_ok", "o_done", "o_ev"])
        order, d_ok, e_ok, w_ok, comb_ok, otr, ot_a, ot_d, out_done, h_ok = map(
            s.sem, ["order", "d_ok", "e_ok", "w_ok", "comb_ok", "otr", "ot_a", "ot_d", "out_done", "h_ok"])
        slab_in = [s.sem(f"slab_in{i}") for i in range(3)]
        units = [(0, hh, (j,)) for hh in range(AH) for j in range(J)] + [(gi, hh, tuple(range(J))) for gi in (1, 2) for hh in range(AH)]
        NU = len(units)
        NPROJ = 12 * G
        block = s.enter_context(nc.Block())

        def evacuated(eng, u):
            eng.wait_ge(ev_d if u % 2 else ev_a, u // 2 + 1)

        def projected(u):
            gi, kind, i = u // 12, u % 12 // 4, u % 4
            return (kT, qT, vv)[kind][gi][:, i, :]

        @block.sync
        def _(sp):
            def load(i, src, k, need):
                if need:
                    sp.wait_ge(unit, need)
                sp.dma_start(ring[i][:, :, :] if k == KT else ring[i][:, :, :].rearrange("p a b -> p (a b)").rearrange("p (a b) -> p a b", a=k),
                             src.rearrange("(k p) n -> p k n", p=P)).then_inc(slab_in[i], 16)

            for gi in range(G):
                for i, src in enumerate([io["w_kv"][:, W * gi:W * gi + W], io["attn_w_q"][0, :, W * gi:W * gi + W],
                                         io["w_kv"][:, W * (G + gi):W * (G + gi) + W]]):
                    load(i, src, KT, 12 * (gi - 1) + 4 * (i + 1) if gi else 0)
            load(0, io["attn_w_o"][0], W // P, 12 * (G - 1) + 4)

        @block.gpsimd
        def _(pool):
            ch = Chain(pool, pool_order)
            ch.inc(nc.gpsimd.memset(mask[0][:, :, :], 0.0))
            ch.inc(nc.gpsimd.memset(mask[1][:, :], 0.0))
            ch.inc(nc.gpsimd.memset(mask[2][:, :], 1.0))
            ch.link(nc.gpsimd.memset(residue[:, :], 0.0))

            def keep(m, op, fill, base, pattern, per_partition):
                ch.link(nc.gpsimd.affine_select(out=m, in_=m, compare_op=op, fill=fill, base=base, pattern=pattern, channel_multiplier=per_partition))

            m0 = mask[0][:, :, :].rearrange("p j (i k) -> p j i k", i=J)
            window = P
            keep(m0, ALU.is_ge, FAR, 0, [[1, J], [-1, J], [-J, P]], J)
            keep(m0, ALU.is_ge, FAR, window, [[-1, J], [1, J], [J, P]], -J)
            keep(mask[1][:, :], ALU.is_ge, FAR, 0, [[-1, P]], 1)
            keep(mask[2][:, :], ALU.is_ge, 0.0, 0, [[-1, P]], 1)
            r4 = residue[:, :].rearrange("p (a b) -> p a b", b=4)
            nc.gpsimd.affine_select(out=r4, in_=r4, compare_op=ALU.not_equal, fill=1.0, base=0, pattern=[[0, P // 4], [-1, 4]],
                                    channel_multiplier=1).then_inc(mask_ok, 1)

        @block.scalar
        def _(act):
            for j in range(J):
                nc.scalar.activation(xq[:, 0:2, :].rearrange("p a b -> p (a b)"), h[:, j, :], ACT.Square, accum_out=ss[:, j:j + 1]).then_inc(sumsq, 1)
                act.wait_ge(sumsq, j + 1)
            nc.scalar.activation(ss[:, :], ss[:, :], ACT.Sqrt, scale=1.0 / D, bias=g["eps"][:, 0:1]).then_inc(rms, 1)
            for kt in range(KT):
                act.wait_ge(tr, kt + 1)
                act.wait_ge(xk_ok, kt + 1)
                nc.scalar.activation(xq[:, kt, :], bank[kt][:, :], ACT.Copy, scale=g["par"][:, GMIX + KT + kt:GMIX + KT + kt + 1]).then_inc(xq_ok, 1)
            for u in range(0, NPROJ, 2):
                act.wait_ge(unit, u + 1)
                nc.scalar.activation(projected(u), bank[u % 8][:, :], ACT.Copy).then_inc(ev_a, 1)

            def transposed(u):
                act.wait_ge(t_done, u + 1)
                if u >= 2:
                    act.wait_ge(o_done, u - 1)
                nc.scalar.activation(pT[u % 2], bank[3 + u % 2][:, :], ACT.Copy).then_inc(pt_ok, 1)

            for u, (gi, hh, js) in enumerate(units):
                act.wait_ge(max_ok, u + 1)
                if u >= 2:
                    act.wait_ge(t_done, u - 1)
                n = T // len(js)
                for i, j in enumerate(js):
                    ins = nc.scalar.activation(pr[u % 2][:, n * i:n * i + n], sm[u % 2][:, n * i:n * i + n], ACT.Exp,
                                               bias=negm[:, gi, j, hh:hh + 1], accum_out=lsum[:, gi, j, hh:hh + 1])
                ins.then_inc(p_ok, 1)
                if u >= 1:
                    transposed(u - 1)
            transposed(NU - 1)
            act.wait_ge(d_ok, 1)
            nc.scalar.activation(negm[:, :, :, :], negm[:, :, :, :], ACT.Exp, scale=-1.0).then_inc(e_ok, 1)
            for b in range(0, 4, 2):
                act.wait_ge(otr, b + 1)
                nc.scalar.activation(oT[:, b, :], bank[b][:, :], ACT.Copy).then_inc(ot_a, 1)

        @block.vector
        def _(dve):
            V = nc.vector
            dve.wait_ge(rms, 1)
            V.reciprocal(rstd[:, :], ss[:, :]).then_inc(rstd_ok, 1)
            dve.wait_ge(rstd_ok, 1)
            for j in range(J):
                V.tensor_scalar(xhat[:, j, :], h[:, j, :], rstd[:, j:j + 1], None, ALU.mult).then_inc(xhat_ok, 1)
            for kt in range(KT):
                dve.wait_ge(tr, kt + 1)
                V.tensor_scalar(xk[:, kt, :], bank[kt][:, :], g["par"][:, GKV + kt:GKV + kt + 1], None, ALU.mult).then_inc(xk_ok, 1)
            for u in range(1, NPROJ, 2):
                dve.wait_ge(unit, u + 1)
                V.tensor_copy(projected(u), bank[u % 8][:, :]).then_inc(ev_d, 1)
            ch = Chain(dve, order)
            dve.wait_ge(res_mm, 1)
            ch.link(V.tensor_tensor(mask[2][:, :], bank[7][:, 0:P], mask[2][:, :], ALU.mult))
            ch.link(V.tensor_scalar(mask[2][:, :], mask[2][:, :], 1.0, -FAR, ALU.subtract, ALU.mult))

            def output(u):
                gi, hh, js = units[u]
                dve.wait_ge(o_done, u + 1)
                src = bank[5 + u % 2][:, 0:HD * len(js)].rearrange("p (j v) -> p j v", j=len(js))
                V.tensor_copy(oacc[gi][:, js[0]:js[0] + len(js), HD * hh:HD * hh + HD], src).then_inc(o_ev, 1)

            dve.wait_ge(ev_a, NPROJ // 2)
            for u, (gi, hh, js) in enumerate(units):
                dve.wait_ge(s_done, u + 1)
                if u >= 2:
                    dve.wait_ge(p_ok, u - 1)
                if gi == 0:
                    V.scalar_tensor_tensor(out=sm[u % 2], in0=bank[u % 3][:, :], scalar=SCALE, in1=mask[0][:, js[0], :], op0=ALU.mult, op1=ALU.add).then_inc(sm_ok, 1)
                    dve.wait_ge(sm_ok, u + 1)
                    V.tensor_reduce(out=negm[:, gi, js[0], hh:hh + 1], in_=sm[u % 2], axis=AX.X, op=ALU.max, negate=True).then_inc(max_ok, 1)
                else:
                    v3 = lambda x: x.rearrange("p (j t) -> p j t", j=J)
                    V.scalar_tensor_tensor(out=v3(sm[u % 2]), in0=v3(bank[u % 3][:, :]), scalar=SCALE,
                                           in1=mask[gi][:, :].rearrange("p (x t) -> p x t", x=1).to_broadcast([P, J, P]), op0=ALU.mult, op1=ALU.add).then_inc(sm_ok, 1)
                    dve.wait_ge(sm_ok, u + 1)
                    V.tensor_reduce(out=negm[:, gi, :, hh], in_=v3(sm[u % 2]), axis=AX.X, op=ALU.max, negate=True).then_inc(max_ok, 1)
                if u >= 2:
                    output(u - 2)
            output(NU - 2)
            output(NU - 1)
            dve.wait_ge(p_ok, NU)
            dve.wait_ge(max_ok, NU)
            ch.link(V.tensor_tensor(least[:, :, :], negm[:, 0, :, :], negm[:, 1, :, :], ALU.min))
            ch.link(V.tensor_tensor(least[:, :, :], least[:, :, :], negm[:, 2, :, :], ALU.min))
            for gi in range(G):
                ins = V.tensor_tensor(negm[:, gi, :, :], negm[:, gi, :, :], least[:, :, :], ALU.subtract)
                if gi < G - 1:
                    ch.inc(ins)
                else:
                    ch.wait()
                    ins.then_inc(d_ok, 1)
            dve.wait_ge(e_ok, 1)
            for gi in range(G):
                ch.link(V.tensor_tensor(lsum[:, gi, :, :], lsum[:, gi, :, :], negm[:, gi, :, :], ALU.mult))
            ch.link(V.tensor_tensor(den[:, :, :], lsum[:, 0, :, :], lsum[:, 1, :, :], ALU.add))
            ch.link(V.tensor_tensor(den[:, :, :], den[:, :, :], lsum[:, 2, :, :], ALU.add))
            ch.link(V.reciprocal(den[:, :, :], den[:, :, :]))
            for gi in range(G):
                ch.link(V.tensor_tensor(negm[:, gi, :, :], negm[:, gi, :, :], den[:, :, :], ALU.mult))
            dve.wait_ge(o_ev, NU)
            heads = lambda t, j: t[:, j, :].rearrange("p (h v) -> p h v", h=AH)
            for j in range(J):
                for gi in range(G):
                    ch.link(V.tensor_tensor(heads(oacc[gi], j), heads(oacc[gi], j),
                                            negm[:, gi, j, :].rearrange("p (h x) -> p h x", x=1).to_broadcast([P, AH, HD]), ALU.mult))
                ch.link(V.tensor_tensor(oacc[0][:, j, :], oacc[0][:, j, :], oacc[1][:, j, :], ALU.add))
                V.tensor_tensor(oacc[0][:, j, :], oacc[0][:, j, :], oacc[2][:, j, :], ALU.add).then_inc(comb_ok, 1)
            for b in range(1, 4, 2):
                dve.wait_ge(otr, b + 1)
                V.tensor_copy(oT[:, b, :], bank[b][:, :]).then_inc(ot_d, 1)
            for u in range(2 * J):
                dve.wait_ge(out_done, u + 1)
                hh = h[:, u // 2, 512 * (u % 2):512 * (u % 2) + 512]
                V.tensor_tensor(hh, bank[u][:, :], hh, ALU.add).then_inc(h_ok, 1)

        @block.tensor
        def _(pe):
            pe.wait_ge(xhat_ok, J)
            for kt in range(KT):
                for j in range(J):
                    last = nc.tensor.transpose(bank[kt][:, P * j:P * j + P], xhat[:, j, P * kt:P * kt + P], g["ident"][:, :])
                last.then_inc(tr, 1)
            for u in range(NPROJ):
                gi, kind, i = u // 12, u % 12 // 4, u % 4
                b = bank[u % 8]
                if u >= 8:
                    evacuated(pe, u - 8)
                else:
                    pe.wait_ge(xq_ok, KT)
                if i == 0:
                    pe.wait_ge(slab_in[kind], 16 * (gi + 1))
                x = xq if kind == 1 else xk
                for kt in range(KT):
                    w = ring[kind][:, kt, :]
                    a, c = (x[:, kt, P * i:P * i + P], w) if kind == 2 else (w[:, P * i:P * i + P], x[:, kt, :])
                    last = nc.tensor.matmul(b[:, :], a, c, start=kt == 0, stop=kt == KT - 1)
                last.then_inc(unit, 1)
            pe.wait_ge(mask_ok, 1)
            pe.wait_ge(ev_a, NPROJ // 2)
            pe.wait_ge(ev_d, NPROJ // 2)
            nc.tensor.matmul(bank[7][:, 0:P], residue[:, :], residue[:, :], start=True, stop=True).then_inc(res_mm, 1)

            def scores(u):
                gi, hh, js = units[u]
                rows = slice(HD * (hh % 2), HD * (hh % 2) + HD)
                if u >= 3:
                    pe.wait_ge(sm_ok, u - 2)
                for i, j in enumerate(js):
                    q = qT[gi][rows, hh // 2, P * j:P * j + P]
                    out, k = (bank[u % 3][:, :], kT[gi][rows, hh // 2, :]) if gi == 0 else (bank[u % 3][:, P * i:P * i + P], kT[gi][rows, hh // 2, P * j:P * j + P])
                    ins = nc.tensor.matmul(out, q, k, start=True, stop=True)
                ins.then_inc(s_done, 1)

            def values(u):
                gi, hh, js = units[u]
                pe.wait_ge(pt_ok, u + 1)
                if u >= 2:
                    pe.wait_ge(o_ev, u - 1)
                for i in range(J):
                    out = bank[5 + u % 2][:, 0:HD] if gi == 0 else bank[5 + u % 2][:, HD * i:HD * i + HD]
                    ins = nc.tensor.matmul(out, pT[u % 2][:, P * i:P * i + P], vv[gi][:, i, HD * hh:HD * hh + HD],
                                           start=gi > 0 or i == 0, stop=gi > 0 or i == J - 1)
                ins.then_inc(o_done, 1)

            scores(0)
            scores(1)
            for u in range(NU):
                if u + 2 < NU:
                    scores(u + 2)
                pe.wait_ge(p_ok, u + 1)
                if u >= 2:
                    pe.wait_ge(pt_ok, u - 1)
                for i in range(J):
                    ins = nc.tensor.transpose(bank[3 + u % 2][:, P * i:P * i + P], pr[u % 2][:, P * i:P * i + P], g["ident"][:, :])
                ins.then_inc(t_done, 1)
                if u >= 1:
                    values(u - 1)
            values(NU - 1)
            pe.wait_ge(comb_ok, J)
            for b in range(W // P):
                for j in range(J):
                    ins = nc.tensor.transpose(bank[b][:, P * j:P * j + P], oacc[0][:, j, P * b:P * b + P], g["ident"][:, :])
                ins.then_inc(otr, 1)
            pe.wait_ge(ot_a, 2)
            pe.wait_ge(ot_d, 2)
            pe.wait_ge(slab_in[0], 16 * (G + 1))
            wo = ring[0][:, :, :].rearrange("p a b -> p (a b)").rearrange("p (a b) -> p a b", a=W // P)
            for u in range(2 * J):
                for kt in range(W // P):
                    ins = nc.tensor.matmul(bank[u][:, :], oT[:, kt, P * (u // 2):P * (u // 2) + P], wo[:, kt, 512 * (u % 2):512 * (u % 2) + 512],
                                           start=kt == 0, stop=kt == W // P - 1)
                ins.then_inc(out_done, 1)


def final_norm(nc, io, g, out):
    h = g["h"]
    with Scope(nc, "final") as s:
        gb = s.sb("gb", [P, D])
        junk = s.sb("junk", [P, D])
        ss, rstd = s.sb("ss", [P, J]), s.sb("rstd", [P, J])
        g_in, sumsq, rms, rstd_ok, done, stored = map(s.sem, ["g_in", "sumsq", "rms", "rstd_ok", "done", "stored"])
        block = s.enter_context(nc.Block())

        @block.sync
        def _(sp):
            sp.dma_start(gb[:, :], io["final_norm_g"].rearrange("(a d) -> a d", a=1).to_broadcast([P, D])).then_inc(g_in, 16)
            for j in range(J):
                sp.wait_ge(done, j + 1)
                sp.dma_start(out[0].rearrange("(p j) d -> p j d", j=J)[:, j, :], h[:, j, :]).then_inc(stored, 16)
            sp.wait_ge(stored, 16 * J)

        @block.scalar
        def _(act):
            for j in range(J):
                nc.scalar.activation(junk[:, :], h[:, j, :], ACT.Square, accum_out=ss[:, j:j + 1]).then_inc(sumsq, 1)
                act.wait_ge(sumsq, j + 1)
            nc.scalar.activation(ss[:, :], ss[:, :], ACT.Sqrt, scale=1.0 / D, bias=g["eps"][:, 0:1]).then_inc(rms, 1)

        @block.vector
        def _(dve):
            dve.wait_ge(rms, 1)
            nc.vector.reciprocal(rstd[:, :], ss[:, :]).then_inc(rstd_ok, 1)
            dve.wait_ge(rstd_ok, 1)
            dve.wait_ge(g_in, 16)
            for j in range(J):
                nc.vector.scalar_tensor_tensor(out=h[:, j, :], in0=h[:, j, :], scalar=rstd[:, j:j + 1], in1=gb[:, :], op0=ALU.mult, op1=ALU.mult).then_inc(done, 1)


_EXTRA = 0


def build(nc, io, out):
    top = Scope(nc, "all")
    with top:
        g = {
            "ident": top.sb("ident", [P, P]), "par": top.sb("par", [P, P]), "eps": top.sb("eps", [P, 2]),
            "blockones": top.sb("blockones", [P, P]), "chmask": top.sb("chmask", [P, P]), "upper": top.sb("upper", [P, P]), "ones": top.sb("ones", [P, P]), "h": top.sb("h", [P, J, D]),
            "ident2": top.sb("ident2", [P, C]), "down4": top.sb("down4", [P, 4]), "base16": top.sb("base16", [P, 16]), "tokid": top.sb("tokid", [P, J]), "ints": top.sb("ints", [P, 16], i32), "lowmask": top.sb("lowmask", [C, C]), "bonus": top.sb("bonus", [P, J, H]),
            "bank": [top.ps(f"bank{i}", [P, 512]) for i in range(8)],
            "ready": top.sem("constants_ready"),
        }
        io["g_dram"] = nc.dram_tensor("g_dram", [T, D], fp32).ap()
        for i in range(2):
            io[f"xn_dram{i}"] = nc.dram_tensor(f"xn_dram{i}", [T, D], fp32).ap()
            io[f"tok_dram{i}"] = nc.dram_tensor(f"tok_dram{i}", [16 * T, 1], fp32).ap()
            io[f"out_dram{i}"] = nc.dram_tensor(f"out_dram{i}", [16 * T, D], fp32).ap()
        io["y_dram"] = nc.dram_tensor("y_dram", [T, D], fp32).ap()
        io["v_dram"] = nc.dram_tensor("v_dram", [T, D], fp32).ap()
        with nc.Block() as block:
            @block.gpsimd
            def _(pool):
                ch = Chain(pool, g["ready"])
                ones = lambda name, v=1.0: ch.inc(nc.gpsimd.memset(g[name][:, :], v))
                ones("ident", 0.0)
                ones("blockones", 0.0)
                for name in ["upper", "chmask", "lowmask", "ones"]:
                    ones(name)
                ch.inc(nc.gpsimd.memset(g["eps"][:, 0:1], NORM_EPS))
                ch.link(nc.gpsimd.memset(g["eps"][:, 1:2], GN_EPS))

                def keep(m, fill, op, base, step, per_partition):
                    ch.link(nc.gpsimd.affine_select(out=m, in_=m, compare_op=op, fill=fill, base=base,
                                                    pattern=[[step, m.shape[1]]], channel_multiplier=per_partition))

                for name, n, step, base, per_partition in (("down4", 4, -1, 4, 0), ("base16", 16, P, 0, 0), ("tokid", J, 1, 0, J)):
                    ch.link(nc.gpsimd.iota(g["ints"][:, 0:n], pattern=[[step, n]], base=base, channel_multiplier=per_partition))
                    ch.link(nc.gpsimd.tensor_copy(g[name][:, :], g["ints"][:, 0:n]))
                keep(g["ident"][:, :], 1.0, ALU.not_equal, 0, -1, 1)
                keep(g["upper"][:, :], 0.0, ALU.is_ge, -1, 1, -1)
                for rows, base in ((P, C), (C, 0)):
                    for x in range(2):
                        keep(g["chmask"][0:rows, C * x:C * x + C], 0.0, ALU.is_ge, base - 1 + x, 1, -1)
                keep(g["lowmask"][:, :], 0.0, ALU.is_ge, -1, -1, 1)
                for i in range(2):
                    ch.link(nc.gpsimd.tensor_copy(g["ident2"][HD * i:HD * i + HD, :], g["ident"][HD * i:HD * i + HD, HD * i:HD * i + HD]))
                    ch.link(nc.gpsimd.memset(g["blockones"][HD * i:HD * i + HD, HD * i:HD * i + HD], 1.0))

        with Scope(nc, "rwkv") as s:
            rw = {n: s.sb("rw_" + n, [P, KT, T]) for n in "rkwa"}
            rwkv_project(nc, io, g, rw)
            for x in ["n", "e1", "e2", "tmp"]:
                rw[x] = s.sb("rw_" + x, [P, KT, T])
            rw["pc"] = s.sb("rw_pc", [C, NC, H])
            rwkv_operands(nc, io, g, rw)
            rwkv_chunks(nc, io, g, rw)
            rwkv_finish(nc, io, g, rw)
        if _STAGE >= 2:
            moe(nc, io, g, 0)
        if _STAGE >= 3:
            attention(nc, io, g)
        if _STAGE >= 4:
            moe(nc, io, g, 1)
            final_norm(nc, io, g, out)
            return
        with Scope(nc, "end") as s:
            dump = s.sem("dump")
            with nc.Block() as block:
                @block.sync
                def _(sp):
                    sp.dma_start(out[0].rearrange("(p j) d -> p j d", j=J), g["h"][:, :, :]).then_inc(dump, 16)
                    sp.wait_ge(dump, 16)


_STAGE = 4
_DUMP = "r"
_INS = ["x", "norm_mix_g", "norm_ffn_g", "rwkv_mu", "rwkv_w_r", "rwkv_w_k", "rwkv_w_v", "rwkv_w0", "rwkv_w1", "rwkv_w2",
        "rwkv_a0", "rwkv_a1", "rwkv_a2", "rwkv_g1", "rwkv_g2", "rwkv_k_k", "rwkv_k_a", "rwkv_r_k", "rwkv_ln_w", "rwkv_ln_b",
        "rwkv_w_o", "kv_norm_g", "w_kv", "attn_w_q", "attn_w_o", "moe_w_grp", "moe_b_grp", "moe_w_exp", "moe_b_exp",
        "moe_w_gate", "moe_w_up", "moe_w_down", "final_norm_g"]


def kernel(**inputs):
    import numpy as _np
    import concourse.bacc as _bacc
    from concourse import mybir as _mybir
    from concourse.bass_utils import run_bass_kernel_spmd as _run

    nc = _bacc.Bacc("TRN2", target_bir_lowering=False, num_devices=1)
    arrays, io = {}, {}
    for name in _INS:
        a = _np.ascontiguousarray(inputs[name])
        arrays[f"in_{name}_dram"] = a
        io[name] = nc.dram_tensor(f"in_{name}_dram", a.shape, _mybir.dt.from_np(a.dtype), kind="ExternalInput").ap()
    out = nc.dram_tensor("out_0_dram", (1, T, D), _mybir.dt.float32, kind="ExternalOutput").ap()
    build(nc, io, out)
    r = _run(nc, [arrays], core_ids=[0])
    return r.results[0]["out_0_dram"]
```

```python
import concourse.bass as bass
from concourse import mybir
from contextlib import ExitStack

fp32 = mybir.dt.float32
i32 = mybir.dt.int32
fp32r = mybir.dt.float32r
ALU = mybir.AluOpType
ACT = mybir.ActivationFunctionType
AX = mybir.AxisListType

P = 128
T = 512
D = 1024
J = T // P
KT = D // P
HD = 64
H = D // HD
LORA = 64
GLORA = 160
C = 64
NC = T // C
NORM_EPS = 1e-6
GN_EPS = HD * 1e-5
DECAY = float(-(2.718281828459045 ** -0.5))

MU, W0, A0, KK_, KA_, RK_, GMIX, GFFN, GKV = 0, 48, 56, 64, 72, 80, 88, 104, 120


class Chain:

    def __init__(self, eng, sem):
        self.eng, self.sem, self.base, self.n = eng, sem, 0, 0

    def inc(self, ins):
        ins.then_inc(self.sem, 1)
        self.n += 1
        return ins

    def wait(self):
        self.eng.wait_ge(self.sem, self.base + self.n)

    def link(self, ins):
        self.inc(ins)
        self.wait()

    def enter(self, i, per):
        self.before, self.per = self.base + self.n, per
        self.base, self.n = i * per + self.before, 0

    def leave(self, times):
        assert self.n == self.per, f"{self.n} signals an iteration, not {self.per}"
        self.base, self.n = self.before + times * self.per, 0


def square_tile(nc, act, g, j, junk, done):
    if j:
        act.wait_ge(done, j)
    nc.scalar.activation(junk, g["h"][:, j, :], ACT.Square, accum_out=g["ss"][:, j:j + 1]).then_inc(done, 1)


class Scope(ExitStack):

    def __init__(self, nc, stage):
        super().__init__()
        self.nc, self.stage, self.sems = nc, stage + "_", []
        self.callback(self.clear)

    def clear(self):
        if self.sems:
            self.nc.clear_and_free_semaphores(self.sems)
            self.nc.all_engine_barrier()

    def sb(self, name, shape, dt=fp32):
        return self.enter_context(self.nc.sbuf_tensor(self.stage + name, shape, dt))

    def ps(self, name, shape, dt=fp32):
        return self.enter_context(self.nc.psum_tensor(self.stage + name, shape, dt))

    def sem(self, name):
        self.sems.append(self.nc.alloc_semaphore(self.stage + name))
        return self.sems[-1]


def rwkv_project(nc, io, g, rw):
    with Scope(nc, "project") as s:
        xT = s.sb("xT", [P, KT, T + 1])
        xx = s.sb("xx", [P, KT, T])
        xm = s.sb("xm", [P, KT, T])
        xtemp = s.sb("xtemp", [P, 2, T])
        xhi, xlo = (s.sb(n, [P, KT, T], fp32r) for n in ["xhi", "xlo"])
        raw = [g["h"][:, 2 * i:2 * i + 2, :].rearrange("p a b -> p (a b)").rearrange("p (k n) -> p k n", k=4) for i in range(2)]
        whi = [s.sb(f"whi{i}", [P, 4, 512], fp32r) for i in range(2)]
        wlo = [s.sb(f"wlo{i}", [P, 4, 512], fp32r) for i in range(2)]
        lh = s.sb("lora_hidden", [P, 2, T])
        parrow = s.sb("parrow", [P, P])
        ss = s.sb("ss", [P, J])
        rstd = s.sb("rstd", [P, J])
        r, k, w, a = rw["r"], rw["k"], rw["w"], rw["a"]
        flat = lambda t: t[:, :, :].rearrange("p a b -> p (a b)")
        xtok = r[:, :, :].rearrange("p a b -> p (a b)").rearrange("p (j d) -> p j d", j=J)
        xhat = k[:, :, :].rearrange("p a b -> p (a b)").rearrange("p (j d) -> p j d", j=J)
        kf = flat(k)
        rf = flat(r)
        g1 = kf[:, 0:KT * GLORA].rearrange("p (a b) -> p a b", a=KT)
        g2 = kf[:, 1280:1280 + 2 * D].rearrange("p (a b) -> p a b", a=2)
        w1 = rf[:, 0:512].rearrange("p (a b) -> p a b", a=KT)
        a1 = rf[:, 512:1024].rearrange("p (a b) -> p a b", a=KT)
        w2 = rf[0:LORA, 1024:2048]
        a2 = rf[0:LORA, 2048:3072]
        gout = flat(w).rearrange("p (j d) -> p j d", j=J)
        vout = flat(a).rearrange("p (j d) -> p j d", j=J)
        bank = g["bank"]
        x_in, par_in, lora_g, lora_wa = map(s.sem, ["x_in", "par_in", "lora_g", "lora_wa"])
        piece_in = [s.sem(f"piece_in{i}") for i in range(2)]
        temp_ok, xh_ok, xl_ok, hi_ok, lo_ok, piece_used = map(s.sem, ["temp_ok", "xh_ok", "xl_ok", "hi_ok", "lo_ok", "piece_used"])
        sumsq, rms, rstd_ok, xhat_ok = map(s.sem, ["sumsq", "rms", "rstd_ok", "xhat_ok"])
        par_tr, par_ok, tr, ev_t, xx_ok, zero_ok = map(s.sem, ["par_tr", "par_ok", "tr", "ev_t", "xx_ok", "zero_ok"])
        mixed, unit, ev_act, ev_dve, g_stored, v_stored = map(s.sem, ["mixed", "unit", "ev_act", "ev_dve", "g_stored", "v_stored"])

        order = [("g", 5), ("v", 3), ("w", 1), ("a", 4), ("k", 2), ("r", 0)]
        kinds = {"g": "AA" + "VA" * 4, "v": "VA" * 4, "w": "A" + "A" * 8, "a": "V" + "A" * 8, "k": "VA" * 4, "r": "VA" * 4}
        start, n = {}, 0
        for name, _ in order:
            start[name] = n
            n += len(kinds[name])
        allk = "".join(kinds[name] for name, _ in order)

        def evacuated(eng, u):
            eng.wait_ge(ev_act if allk[u] == "A" else ev_dve, allk[:u + 1].count(allk[u]))


        ORDER = "vkr"

        def after_piece(eng, n):
            if n % 2:
                eng.wait_ge(unit, start[ORDER[n // 4]] + 4 * (n % 4 // 2 + 1))
            else:
                eng.wait_ge(piece_used, n // 2 + 1)

        def split_hi(act, n):
            act.wait_ge(piece_in[n % 2], 16 * (n // 2 + 1))
            if n >= 2:
                after_piece(act, n - 2)
            nc.scalar.activation(whi[n % 2][:, :, :], raw[n % 2], ACT.Copy).then_inc(hi_ok, 1)

        def split_lo(dve, n):
            dve.wait_ge(hi_ok, n + 1)
            nc.vector.tensor_tensor(wlo[n % 2][:, :, :], raw[n % 2], whi[n % 2][:, :, :].bitcast(fp32), ALU.subtract).then_inc(lo_ok, 1)

        def x_hi(act, q, half):
            if q:
                after_piece(act, 4 * (q - 1) + 2 + half)
            for kt in range(4 * half, 4 * half + 4):
                act.wait_ge(temp_ok, KT * q + kt + 1)
                nc.scalar.activation(xhi[:, kt, :], xtemp[:, kt % 2, :], ACT.Copy).then_inc(xh_ok, 1)

        def x_lo(dve, q, half):
            mu = MU + KT * dict(order)[ORDER[q]]

            def mix(kt):
                if KT * q + kt >= 2:
                    dve.wait_ge(xl_ok, KT * q + kt - 1)
                nc.vector.scalar_tensor_tensor(out=xtemp[:, kt % 2, :], in0=xx[:, kt, :], scalar=g["par"][:, mu + kt:mu + kt + 1],
                                               in1=xT[:, kt, 1:T + 1], op0=ALU.mult, op1=ALU.add).then_inc(temp_ok, 1)

            mix(4 * half)
            for kt in range(4 * half, 4 * half + 4):
                if kt < 4 * half + 3:
                    mix(kt + 1)
                dve.wait_ge(xh_ok, KT * q + kt + 1)
                nc.vector.tensor_tensor(xlo[:, kt, :], xtemp[:, kt % 2, :], xhi[:, kt, :].bitcast(fp32), ALU.subtract).then_inc(xl_ok, 1)

        block = s.enter_context(nc.Block())

        @block.sync
        def _(sp):
            sp.dma_start(xtok, io["x"].rearrange("b (j p) d -> p (b j) d", p=P)).then_inc(x_in, 16)
            rows = [(MU, io["rwkv_mu"].rearrange("a m (k c) -> (a m k) c", c=P)), (W0, io["rwkv_w0"].rearrange("a (k c) -> (a k) c", c=P)),
                    (A0, io["rwkv_a0"].rearrange("a (k c) -> (a k) c", c=P)), (KK_, io["rwkv_k_k"].rearrange("a (k c) -> (a k) c", c=P)),
                    (KA_, io["rwkv_k_a"].rearrange("a (k c) -> (a k) c", c=P)),
                    (RK_, io["rwkv_r_k"].rearrange("a (k b) c -> (a k) (b c)", b=2)),
                    (GMIX, io["norm_mix_g"].rearrange("a (k c) -> (a k) c", c=P)),
                    (GFFN, io["norm_ffn_g"].rearrange("a (k c) -> (a k) c", c=P)),
                    (GKV, io["kv_norm_g"].rearrange("(k c) -> k c", c=P))]
            for at, src in rows:
                sp.dma_start(parrow[at:at + src.shape[0], :], src).then_inc(par_in, 16)
            sp.wait_ge(tr, KT)
            sp.dma_start(g1, io["rwkv_g1"][0].rearrange("(k p) n -> p k n", p=P)).then_inc(lora_g, 16)
            sp.dma_start(g2[:, 0, :], io["rwkv_g2"][0, 0:P, :]).then_inc(lora_g, 16)
            sp.dma_start(g2[0:GLORA - P, 1, :], io["rwkv_g2"][0, P:GLORA, :]).then_inc(lora_g, 16)
            sp.dma_start(w1, io["rwkv_w1"][0].rearrange("(k p) n -> p k n", p=P)).then_inc(lora_wa, 16)
            sp.dma_start(a1, io["rwkv_a1"][0].rearrange("(k p) n -> p k n", p=P)).then_inc(lora_wa, 16)
            sp.dma_start(w2, io["rwkv_w2"][0]).then_inc(lora_wa, 16)
            sp.dma_start(a2, io["rwkv_a2"][0]).then_inc(lora_wa, 16)
            def load(n):
                if n >= 2:
                    sp.wait_ge(lo_ok, n - 1)
                rows, cols = 512 * (n % 2), 512 * (n % 4 // 2)
                sp.dma_start(raw[n % 2], io["rwkv_w_" + ORDER[n // 4]][0, rows:rows + 512, cols:cols + 512].rearrange("(k p) n -> p k n", p=P)
                             ).then_inc(piece_in[n % 2], 16)

            for n in range(12):
                load(n)
                if n == 1:
                    evacuated(sp, start["g"] + 9)
                    evacuated(sp, start["g"] + 8)
                    for j in range(J):
                        sp.dma_start(io["g_dram"][P * j:P * j + P, :], gout[:, j, :]).then_inc(g_stored, 16)
                if n == 5:
                    evacuated(sp, start["v"] + 7)
                    evacuated(sp, start["v"] + 6)
                    for j in range(J):
                        sp.dma_start(io["v_dram"][P * j:P * j + P, :], vout[:, j, :]).then_inc(v_stored, 16)
            sp.wait_ge(g_stored, 16 * J)
            sp.wait_ge(v_stored, 16 * J)

        @block.tensor
        def _(pe):
            pe.wait_ge(par_in, 16 * 9)
            nc.tensor.transpose(bank[7][:, 0:P], parrow[:, :], g["ident"][:, :]).then_inc(par_tr, 1)
            pe.wait_ge(par_ok, 1)
            for j in range(J):
                pe.wait_ge(xhat_ok, j + 1)
                for kt in range(KT):
                    ins = nc.tensor.transpose(bank[kt][:, P * j:P * j + P], xhat[:, j, P * kt:P * kt + P], g["ident"][:, :])
                    if j == J - 1:
                        ins.then_inc(tr, 1)

            seen = set()

            def begin(u):
                if u >= 8:
                    evacuated(pe, u - 8)
                elif u == 0:
                    pe.wait_ge(ev_t, KT)
                return bank[u % 8]

            fp32_mixes = [name for name, _ in order if name not in ORDER]
            for i, (name, mu) in enumerate(order):
                x = xm
                u = start[name]

                def mix(kt):
                    if (i, kt) not in seen:
                        seen.add((i, kt))
                        pe.wait_ge(mixed, KT * fp32_mixes.index(name) + kt + 1)

                if name == "g":
                    pe.wait_ge(lora_g, 48)
                    for m, (lo, n) in enumerate([(0, P), (P, GLORA - P)]):
                        b = begin(u)
                        for kt in range(KT):
                            mix(kt)
                            last = nc.tensor.matmul(b[0:n, :], g1[:, kt, lo:lo + n], x[:, kt, :], start=kt == 0, stop=kt == KT - 1)
                        last.then_inc(unit, 1)
                        u += 1
                    evacuated(pe, u - 1)
                    evacuated(pe, u - 2)
                    for j in range(J):
                        for half in range(2):
                            b = begin(u)
                            nc.tensor.matmul(b[:, :], lh[:, 0, P * j:P * j + P], g2[:, 0, 512 * half:512 * half + 512], start=True, stop=False)
                            nc.tensor.matmul(b[:, :], lh[0:GLORA - P, 1, P * j:P * j + P], g2[0:GLORA - P, 1, 512 * half:512 * half + 512],
                                             start=False, stop=True).then_inc(unit, 1)
                            u += 1
                elif name in ORDER:
                    q = ORDER.index(name)
                    for half in range(2):
                        for kh in range(2):
                            n = 4 * q + 2 * half + kh
                            pe.wait_ge(lo_ok, n + 1)
                            if half == 0:
                                pe.wait_ge(xl_ok, KT * q + 4 * kh + 4)
                            for m in range(4):
                                v = u + 4 * half + m
                                b = begin(v) if kh == 0 else bank[v % 8]
                                for kt in range(4):
                                    xs = [z[:, 4 * kh + kt, P * m:P * m + P] if name == "v" else z[:, 4 * kh + kt, :] for z in (xhi, xlo)]
                                    ws = [z[n % 2][:, kt, :] if name == "v" else z[n % 2][:, kt, P * m:P * m + P] for z in (whi, wlo)]
                                    (ah, al), (ch, cl) = (xs, ws) if name == "v" else (ws, xs)
                                    nc.tensor.matmul(b[:, :], ah, ch, start=kh == 0 and kt == 0, stop=False)
                                    nc.tensor.matmul(b[:, :], ah, cl, start=False, stop=False)
                                    last = nc.tensor.matmul(b[:, :], al, ch, start=False, stop=kh == 1 and kt == 3)
                                if kh == 1:
                                    last.then_inc(unit, 1)
                                elif m == 3:
                                    last.then_inc(piece_used, 1)
                elif name in "wa":
                    if name == "w":
                        pe.wait_ge(lora_wa, 64)
                    l1, l2 = (w1, w2) if name == "w" else (a1, a2)
                    b = begin(u)
                    for kt in range(KT):
                        mix(kt)
                        last = nc.tensor.matmul(b[0:LORA, :], l1[:, kt, :], x[:, kt, :], start=kt == 0, stop=kt == KT - 1)
                    last.then_inc(unit, 1)
                    evacuated(pe, u)
                    u += 1
                    hid = lh[0:LORA, 0 if name == "w" else 1, :]
                    for m in range(KT):
                        b = begin(u)
                        nc.tensor.matmul(b[:, :], l2[:, P * m:P * m + P], hid, start=True, stop=True).then_inc(unit, 1)
                        u += 1

        def share(who, name, lo, hi):
            return [(name, i, start[name] + i) for i in range(lo, hi) if kinds[name][i] == who]

        def move(eng, who, name, i, u):
            b = bank[u % 8]
            eng.wait_ge(unit, u + 1)
            if name == "g" and i < 2:
                n = P if i == 0 else GLORA - P
                return nc.scalar.activation(lh[0:n, i, :], b[0:n, :], ACT.Sigmoid)
            if name == "w" and i == 0:
                return nc.scalar.activation(lh[0:LORA, 0, :], b[0:LORA, :], ACT.Tanh)
            if name == "a" and i == 0:
                return nc.vector.tensor_copy(lh[0:LORA, 1, :], b[0:LORA, :])
            if name == "w":
                if i == 1:
                    eng.wait_ge(g_stored, 16 * J)
                return nc.scalar.activation(w[:, i - 1, :], b[:, :], ACT.Sigmoid, bias=g["par"][:, W0 + i - 1:W0 + i])
            if name == "a":
                if i == 1:
                    eng.wait_ge(v_stored, 16 * J)
                return nc.scalar.activation(a[:, i - 1, :], b[:, :], ACT.Sigmoid, bias=g["par"][:, A0 + i - 1:A0 + i])
            if name == "g":
                out = gout[:, (i - 2) // 2, 512 * (i % 2):512 * (i % 2) + 512]
            elif name == "v":
                out = vout[:, i % 4, 512 * (i // 4):512 * (i // 4) + 512]
            else:
                out = (k if name == "k" else r)[:, i, :]
            if who == "A":
                return nc.scalar.activation(out, b[:, :], ACT.Copy)
            return nc.vector.tensor_copy(out, b[:, :])

        @block.scalar
        def _(act):
            act.wait_ge(x_in, 16)
            for j in range(J):
                nc.scalar.activation(xx[:, 0:2, :].rearrange("p a b -> p (a b)"), xtok[:, j, :], ACT.Square, accum_out=ss[:, j:j + 1]).then_inc(sumsq, 1)
                act.wait_ge(sumsq, j + 1)
            nc.scalar.activation(ss[:, :], ss[:, :], ACT.Sqrt, scale=1.0 / D, bias=g["eps"][:, 0:1]).then_inc(rms, 1)
            act.wait_ge(par_ok, 1)
            for kt in range(0, KT, 2):
                act.wait_ge(tr, kt + 1)
                nc.scalar.activation(xT[:, kt, 1:T + 1], bank[kt][:, :], ACT.Copy, scale=g["par"][:, GMIX + kt:GMIX + kt + 1]).then_inc(ev_t, 1)

            def flush(name, lo, hi):
                if name in "kr":
                    act.wait_ge(unit, start[name])
                for item in share("A", name, lo, hi):
                    move(act, "A", *item).then_inc(ev_act, 1)

            x_hi(act, 0, 0)
            split_hi(act, 0)
            x_hi(act, 0, 1)
            split_hi(act, 1)
            flush("g", 0, 10)
            for q, name in enumerate(ORDER):
                n = 4 * q
                split_hi(act, n + 2)
                flush(name, 0, 4)
                split_hi(act, n + 3)
                if name != "r":
                    split_hi(act, n + 4)
                    x_hi(act, q + 1, 0)
                flush(name, 4, 8)
                if name != "r":
                    split_hi(act, n + 5)
                    x_hi(act, q + 1, 1)
                if name == "v":
                    flush("w", 0, 9)
                    flush("a", 0, 9)

        @block.vector
        def _(dve):
            dve.wait_ge(par_tr, 1)
            nc.vector.tensor_copy(g["par"][:, :], bank[7][:, 0:P]).then_inc(par_ok, 1)
            nc.vector.memset(xT[:, :, 0:1], 0.0).then_inc(zero_ok, 1)
            dve.wait_ge(rms, 1)
            nc.vector.reciprocal(rstd[:, :], ss[:, :]).then_inc(rstd_ok, 1)
            dve.wait_ge(rstd_ok, 1)
            for j in range(J):
                nc.vector.tensor_scalar(xhat[:, j, :], xtok[:, j, :], rstd[:, j:j + 1], None, ALU.mult).then_inc(xhat_ok, 1)
            dve.wait_ge(par_ok, 1)
            for kt in range(1, KT, 2):
                dve.wait_ge(tr, kt + 1)
                nc.vector.tensor_scalar(xT[:, kt, 1:T + 1], bank[kt][:, :], g["par"][:, GMIX + kt:GMIX + kt + 1], None, ALU.mult).then_inc(ev_t, 1)
            dve.wait_ge(ev_t, KT)
            dve.wait_ge(zero_ok, 1)
            nc.vector.tensor_tensor(xx[:, :, :], xT[:, :, 0:T], xT[:, :, 1:T + 1], ALU.subtract).then_inc(xx_ok, 1)
            dve.wait_ge(xx_ok, 1)

            def flush(name, lo, hi):
                for item in share("V", name, lo, hi):
                    move(dve, "V", *item).then_inc(ev_dve, 1)

            def mix(name, free):
                if free:
                    dve.wait_ge(unit, free)
                at = MU + KT * dict(order)[name]
                for kt in range(KT):
                    nc.vector.scalar_tensor_tensor(out=xm[:, kt, :], in0=xx[:, kt, :], scalar=g["par"][:, at + kt:at + kt + 1],
                                                   in1=xT[:, kt, 1:T + 1], op0=ALU.mult, op1=ALU.add).then_inc(mixed, 1)

            mix("g", 0)
            x_lo(dve, 0, 0)
            split_lo(dve, 0)
            x_lo(dve, 0, 1)
            split_lo(dve, 1)
            flush("g", 0, 10)
            mix("w", start["g"] + 2)
            for q, name in enumerate(ORDER):
                n = 4 * q
                split_lo(dve, n + 2)
                flush(name, 0, 4)
                split_lo(dve, n + 3)
                if name != "r":
                    split_lo(dve, n + 4)
                    x_lo(dve, q + 1, 0)
                flush(name, 4, 8)
                if name != "r":
                    split_lo(dve, n + 5)
                    x_lo(dve, q + 1, 1)
                if name == "v":
                    mix("a", start["w"] + 1)
                    flush("a", 0, 9)


def rwkv_operands(nc, io, g, rw):
    with Scope(nc, "operands") as s:
        r, k, w, a, n, e1, e2, tmp = (rw[x] for x in ["r", "k", "w", "a", "n", "e1", "e2", "tmp"])
        omk = s.sb("one_minus_ka", [P, KT])
        hsel = s.sb("hsel", [P, KT, 2])
        norms = s.sb("norms", [H, T])
        of_head, to_head = s.sb("of_head", [P, KT, H]), s.sb("to_head", [H, KT, P])
        reset = s.sb("reset", [P, T])
        bank = g["bank"]
        small, n_ok, sq_ok, sum_ok, root_ok, cs_ok, ex_ok = map(s.sem, ["small", "n_ok", "sq_ok", "sum_ok", "root_ok", "cs_ok", "ex_ok"])
        pool_order, sel_ok, rcp_ok, spread_ok, na_ok, nn_ok, rate_ok, k_ok, rk_ok, bonus_mm, order, exp_ok = map(s.sem, ["pool_order", "sel_ok", "rcp_ok", "spread_ok", "na_ok", "nn_ok", "rate_ok", "k_ok", "rk_ok", "bonus_mm", "dve_order", "exp_ok"])
        block = s.enter_context(nc.Block())

        @block.vector
        def _(dve):
            ch = Chain(dve, order)
            par = g["par"]
            ch.inc(nc.vector.memset(reset[:, :], 1.0))
            ch.wait()
            ch.inc(nc.vector.memset(reset[:, 0:T:C], 0.0))
            nc.vector.tensor_scalar(omk[:, :], par[:, KA_:KA_ + KT], -1.0, 1.0, ALU.mult, ALU.add).then_inc(small, 1)
            for i in range(2):
                nc.vector.tensor_scalar(hsel[:, :, i], par[:, RK_:RK_ + KT], g["blockones"][:, HD * i:HD * i + 1], None, ALU.mult).then_inc(small, 1)
            for m in range(KT):
                nc.vector.tensor_scalar(n[:, m, :], k[:, m, :], par[:, KK_ + m:KK_ + m + 1], None, ALU.mult).then_inc(n_ok, 1)
            ch.wait()
            for m in range(KT):
                nc.vector.tensor_tensor_scan(e1[:, m, :], reset[:, :], w[:, m, :], 0.0, ALU.mult, ALU.add).then_inc(cs_ok, 1)
            dve.wait_ge(root_ok, 1)
            ch.link(nc.vector.tensor_scalar(norms[:, :], norms[:, :], 1e-12, None, ALU.max))
            nc.vector.reciprocal(norms[:, :], norms[:, :]).then_inc(rcp_ok, 1)
            for m in range(KT):
                dve.wait_ge(rate_ok, m + 1)
                dve.wait_ge(n_ok, m + 1)
                dve.wait_ge(sq_ok, m + 1)
                nc.vector.tensor_tensor(k[:, m, :], k[:, m, :], tmp[:, m, :], ALU.mult).then_inc(k_ok, 1)
            for m in range(KT):
                dve.wait_ge(spread_ok, m + 1)
                nc.vector.tensor_tensor(n[:, m, :], n[:, m, :], bank[m][:, :], ALU.mult).then_inc(nn_ok, 1)
            for m in range(KT):
                dve.wait_ge(k_ok, m + 1)
                nc.vector.tensor_tensor(tmp[:, m, :], r[:, m, :], k[:, m, :], ALU.mult).then_inc(rk_ok, 1)
            dve.wait_ge(bonus_mm, 1)
            nc.vector.tensor_copy(g["bonus"][:, :, :], bank[0][:, 0:J * H].rearrange("p (j h) -> p j h", j=J))
            dve.wait_ge(exp_ok, 3)
            for i in range(2):
                nc.vector.tensor_copy(rw["pc"][:, :, KT * i:KT * i + KT].rearrange("p c m -> p m c"), e1[HD * i:HD * i + HD, :, C - 1:T:C])

        @block.gpsimd
        def _(pool):
            ch = Chain(pool, pool_order)
            for m, pattern, per_partition in ((of_head[:, :, :], [[P, KT], [-HD, H]], 1), (to_head[:, :, :], [[P, KT], [1, P]], -HD)):
                ch.link(nc.gpsimd.memset(m, 1.0))
                ch.link(nc.gpsimd.affine_select(out=m, in_=m, compare_op=ALU.is_ge, fill=0.0, base=0, pattern=pattern, channel_multiplier=per_partition))
                nc.gpsimd.affine_select(out=m, in_=m, compare_op=ALU.is_ge, fill=0.0, base=HD - 1, pattern=[[-a, b] for a, b in pattern],
                                        channel_multiplier=-per_partition).then_inc(sel_ok, 1)
            for m in range(KT):
                pool.wait_ge(cs_ok, m + 1)
                nc.gpsimd.tensor_tensor(w[:, m, :], e1[:, m, :], w[:, m, :], ALU.subtract).then_inc(ex_ok, 1)
            for m in range(KT):
                pool.wait_ge(rate_ok, m + 1)
                pool.wait_ge(nn_ok, m + 1)
                nc.gpsimd.tensor_tensor(a[:, m, :], n[:, m, :], a[:, m, :], ALU.mult).then_inc(na_ok, 1)
            for m in range(KT):
                pool.wait_ge(na_ok, m + 1)
                nc.gpsimd.tensor_scalar(a[:, m, :], a[:, m, :], -1.0, None, ALU.mult)

        @block.scalar
        def _(act):
            par = g["par"]
            for m in range(KT):
                nc.scalar.activation(tmp[:, m, :], k[:, m, :], ACT.Square, scale=par[:, KK_ + m:KK_ + m + 1]).then_inc(sq_ok, 1)
            act.wait_ge(sum_ok, 1)
            nc.scalar.activation(norms[:, :], bank[0][0:H, :], ACT.Sqrt).then_inc(root_ok, 1)
            act.wait_ge(small, 3)
            for m in range(KT):
                nc.scalar.activation(tmp[:, m, :], a[:, m, :], ACT.Identity, scale=par[:, KA_ + m:KA_ + m + 1], bias=omk[:, m:m + 1]).then_inc(rate_ok, 1)
            act.wait_ge(ex_ok, KT)
            nc.scalar.activation(w[:, :, :], w[:, :, :], ACT.Exp, scale=DECAY).then_inc(exp_ok, 1)
            act.wait_ge(nn_ok, KT)
            nc.scalar.activation(e2[:, :, :], e1[:, :, :], ACT.Exp, scale=-DECAY).then_inc(exp_ok, 1)
            act.wait_ge(exp_ok, 2)
            nc.scalar.activation(e1[:, :, :], e1[:, :, :], ACT.Exp, scale=DECAY).then_inc(exp_ok, 1)

        @block.tensor
        def _(pe):
            pe.wait_ge(sel_ok, 2)
            for m in range(KT):
                pe.wait_ge(sq_ok, m + 1)
                last = nc.tensor.matmul(bank[0][0:H, :], of_head[:, m, :], tmp[:, m, :], start=m == 0, stop=m == KT - 1)
            last.then_inc(sum_ok, 1)
            pe.wait_ge(rcp_ok, 1)
            for m in range(KT):
                nc.tensor.matmul(bank[m][:, :], to_head[:, m, :], norms[:, :], start=True, stop=True).then_inc(spread_ok, 1)
            pe.wait_ge(small, 3)
            pe.wait_ge(nn_ok, 1)
            for m in range(KT):
                pe.wait_ge(rk_ok, m + 1)
                for j in range(J):
                    last = nc.tensor.matmul(bank[0][:, H * j + 2 * m:H * j + 2 * m + 2], tmp[:, m, j:T:J], hsel[:, m, :], start=True, stop=True)
            last.then_inc(bonus_mm, 1)


def rwkv_chunks(nc, io, g, rw):
    PAIRS, GP = H // 2, 4
    with Scope(nc, "chunks") as s:
        r, k, w, a, n, e1, e2, tmp = (rw[x] for x in ["r", "k", "w", "a", "n", "e1", "e2", "tmp"])
        tf = tmp[:, :, :].rearrange("p a b -> p (a b)")
        AR, BK, BKS = (tf[:, 1024 * i:1024 * i + 1024].rearrange("p (m x t) -> p m x t", m=KT, x=2) for i in range(3))
        first = s.sb("first", [P, H, 2 * C])
        second = s.sb("second", [P, H, 2 * C])
        nq = s.sb("nq", [P, PAIRS, 2, C])
        nt = s.sb("nt", [P, PAIRS, C])
        be = s.sb("be", [P, PAIRS, 2, C])
        n_diag, t_diag, q_diag = (s.sb(x, [P, PAIRS, 2 * C]) for x in ["n_diag", "t_diag", "q_diag"])
        sv = s.sb("sv", [P, H, HD])
        zv = s.sb("zv", [P, H, HD])
        decayed = s.sb("decayed", [C, H, HD])
        ybuf = s.sb("ybuf", [P, H, HD])
        bank = g["bank"]
        names = ["ar_ok", "bk_ok", "bks_ok", "lh_ok", "mm_done", "n_done", "t_done", "tm_ok", "me_ok", "ne_ok", "te_ok", "q_ok", "nq_done", "nt_done", "td_ok", "nd_ok",
                 "nq_ev", "nt_ev", "o1_done", "z_ev", "yp_ev", "fe_done", "fe_ev_d", "fe_ev_a", "o2_done", "so_ev", "dec_ok", "v_in", "y_st"]
        sem = {x: s.sem(x) for x in names}
        setup, zeroed, turn = s.sem("setup"), s.sem("zeroed"), s.sem("turn")
        heads = lambda b: slice(b, H, 2)
        half = lambda b: slice(C * b, C * b + C)
        pairs = lambda gr: slice(GP * gr, GP * gr + GP)
        spread = lambda t, m: t.rearrange("p (x t) -> p x t", x=1).to_broadcast([t.shape[0], m, t.shape[1]])
        QUARTERS = [0, 2, 1, 3]
        NW, TW = [1, 2, 2, 2, 1, 2], [3, 3, 3, 3, 2]
        NQ_PER, NT_PER = 2 * sum(NW), 2 * sum(TW)
        nq_after = lambda lv, gr: 2 * sum(NW[:lv]) + (gr + 1) * NW[lv]
        nt_after = lambda lv, gr: 2 * sum(TW[:lv]) + (gr + 1) * TW[lv]
        nt_later = [1, 1, 1, 1, 0]
        ND_PER = 2 + 2 * 8
        nd_after = lambda lv, gr: 2 + 4 * lv + 2 * (gr + 1)
        block = s.enter_context(nc.Block())

        def waiter(eng, c):
            return lambda name, per, k: eng.wait_ge(sem[name], c * per + (k + 1))

        @block.sync
        def _(sp):
            for x in ["v_in", "y_st"]:
                sp.sem_inc(sem[x], 1)
            with sp.Fori(0, NC) as c:
                wait = waiter(sp, c)
                wait("o2_done", 2, 0)
                src = io["v_dram"][bass.ds(c * C, C), :]
                sp.dma_start(sv[C:P, :, :].rearrange("p h v -> p (h v)"), src).then_inc(sem["v_in"], 16)
                sp.dma_start(zv[C:P, :, :].rearrange("p h v -> p (h v)"), src).then_inc(sem["v_in"], 16)
                wait("so_ev", 4, 4)
                sp.dma_start(io["y_dram"][bass.ds(c * C, C), :], ybuf[C:P, :, :].rearrange("p h v -> p (h v)")).then_inc(sem["y_st"], 16)
            sp.wait_ge(sem["y_st"], 16 * NC + 1)

        @block.gpsimd
        def _(pool):
            for x in ["ar_ok", "bk_ok", "bks_ok", "lh_ok", "q_ok", "dec_ok"]:
                pool.sem_inc(sem[x], 1)
            nc.gpsimd.memset(sv[0:C, :, :], 0.0).then_inc(setup, 1)
            pool.wait_ge(setup, 1)
            nc.gpsimd.memset(second[C:P, :, C:2 * C], 0.0).then_inc(setup, 1)
            pool.wait_ge(setup, 2)
            with pool.Fori(0, NC) as c:
                wait = waiter(pool, c)
                wait("t_done", 2, 0)
                wait("n_done", 2, 0)
                pool.sem_inc(turn, 1)
                at = bass.ds(c * C, C)
                nc.gpsimd.tensor_tensor(BK[:, :, 0, :], a[:, :, at], e2[:, :, at], ALU.mult).then_inc(sem["bk_ok"], 1)
                nc.gpsimd.tensor_tensor(BK[:, :, 1, :], k[:, :, at], e2[:, :, at], ALU.mult).then_inc(sem["bk_ok"], 1)
                last_decay = e1[:, :, bass.ds(c * C + (C - 1), 1)].to_broadcast([P, KT, C])
                for i in range(2):
                    wait("bk_ok", 2, i + 1)
                    pool.sem_inc(turn, 1)
                    nc.gpsimd.tensor_tensor(BKS[:, :, i, :], BK[:, :, i, :], last_decay, ALU.mult).then_inc(sem["bks_ok"], 1)
                wait("lh_ok", 2, 0)
                pool.sem_inc(turn, 1)
                nc.gpsimd.tensor_tensor(AR[:, :, 0, :], n[:, :, at], w[:, :, at], ALU.mult).then_inc(sem["ar_ok"], 1)
                nc.gpsimd.tensor_tensor(AR[:, :, 1, :], r[:, :, at], e1[:, :, at], ALU.mult).then_inc(sem["ar_ok"], 1)
                wait("ar_ok", 2, 2)
                wait("o1_done", 2, 0)
                for i in range(2):
                    pool.sem_inc(turn, 1)
                    nc.gpsimd.tensor_copy(first[0:C, 8 * i:8 * i + 8, :], AR[half(i), :, :, :].rearrange("p m x t -> p m (x t)")).then_inc(sem["lh_ok"], 1)
                    wait("lh_ok", 2, i + 1)
                wait("so_ev", 4, 0)
                for i in range(2):
                    pool.sem_inc(turn, 1)
                    nc.gpsimd.tensor_tensor(decayed[:, i::2, :], sv[0:C, i::2, :],
                                            rw["pc"][:, bass.ds(c, 1), KT * i:KT * i + KT].rearrange("p a (m x) -> p (a m) x", x=1).to_broadcast([C, KT, HD]),
                                            ALU.mult).then_inc(sem["dec_ok"], 1)
                    wait("dec_ok", 2, i + 1)
                wait("ne_ok", 2, 2)
                for gr in range(2):
                    nc.gpsimd.tensor_tensor(nq[:, pairs(gr), 1, :], nq[:, pairs(gr), 0, :], spread(g["ident2"][:, :], GP), ALU.add).then_inc(sem["q_ok"], 1)

        @block.scalar
        def _(act):
            for x in ["te_ok", "td_ok", "nd_ok", "nt_ev", "z_ev", "fe_ev_a"]:
                act.sem_inc(sem[x], 1)
            act.wait_ge(zeroed, 3)
            with act.Fori(0, NC) as c:
                wait = waiter(act, c)
                for b in range(2):
                    wait("t_done", 2, b + 1)
                    src = bank[6 + b][:, :].rearrange("p (m r k) -> p m r k", m=GP, r=2)
                    for par in range(2):
                        nc.scalar.activation(be[half(par), pairs(b), 0, :], src[0:C, :, par, :], ACT.Copy).then_inc(sem["te_ok"], 1)
                        nc.scalar.activation(second[C:P, 8 * par + GP * b:8 * par + GP * b + GP, 0:C], src[C:P, :, par, :], ACT.Copy).then_inc(sem["te_ok"], 1)
                for i, q in enumerate(QUARTERS):
                    wait("tm_ok", 4, i + 1)
                    nc.scalar.activation(t_diag[half(q // 2), pairs(q % 2), half(q // 2)], nt[half(q // 2), pairs(q % 2), :], ACT.Copy).then_inc(sem["td_ok"], 1)
                for b in range(2):
                    wait("ne_ok", 2, b + 1)
                    nc.scalar.activation(n_diag[half(b), :, half(b)], nq[half(b), :, 0, :], ACT.Copy).then_inc(sem["nd_ok"], 1)
                for lv in range(5):
                    for gr in range(2):
                        wait("nt_done", 10, 2 * lv + gr + 1)
                        src = bank[4 + gr][:, 0:GP * C].rearrange("p (h t) -> p h t", h=GP)
                        for b in range(2):
                            nc.scalar.activation(t_diag[half(b), pairs(gr), half(b)], src[half(b), :, :], ACT.Copy).then_inc(sem["nt_ev"], 1)
                        if lv < 4:
                            nc.scalar.activation(nt[:, pairs(gr), :], src, ACT.Copy).then_inc(sem["nt_ev"], 1)
                            wait("nq_ev", NQ_PER, nq_after(lv, gr))
                            for b in range(2):
                                nc.scalar.activation(n_diag[half(b), pairs(gr), half(b)], nq[half(b), pairs(gr), 0, :], ACT.Copy).then_inc(sem["nd_ok"], 1)
                for b in range(2):
                    wait("o1_done", 2, b + 1)
                    nc.scalar.activation(zv[0:C, heads(b), :], bank[4 + b][0:C, :].rearrange("p (h v) -> p h v", h=8), ACT.Copy).then_inc(sem["z_ev"], 1)
                for gr in range(2):
                    wait("fe_done", 2, gr + 1)
                    nc.scalar.activation(second[0:C, 8 + GP * gr:8 + GP * gr + GP, :], bank[gr][C:P, :].rearrange("p (h x) -> p h x", h=GP), ACT.Copy).then_inc(sem["fe_ev_a"], 1)

        @block.vector
        def _(dve):
            for x in ["tm_ok", "me_ok", "ne_ok", "nq_ev", "yp_ev", "fe_ev_d", "so_ev"]:
                dve.sem_inc(sem[x], 1)
            mask = g["chmask"]
            for t in (n_diag, t_diag, q_diag):
                nc.vector.memset(t[:, :, :], 0.0).then_inc(zeroed, 1)
            dve.wait_ge(zeroed, 3)
            with dve.Fori(0, NC) as c:
                wait = waiter(dve, c)
                for i, q in enumerate(QUARTERS):
                    wait("mm_done", 4, i + 1)
                    b = bank[q][:, :].rearrange("p (h x) -> p h x", h=GP)
                    nc.vector.tensor_tensor(nt[half(q // 2), pairs(q % 2), :], b[0:C, :, 0:C], spread(mask[0:C, 0:C], GP), ALU.mult).then_inc(sem["tm_ok"], 1)
                for b in range(2):
                    wait("n_done", 2, b + 1)
                    nc.vector.tensor_tensor(nq[half(b), :, 0, :], bank[4 + b][0:C, :].rearrange("p (h t) -> p h t", h=8),
                                            spread(g["lowmask"][:, :], 8), ALU.mult).then_inc(sem["ne_ok"], 1)
                for lv in range(6):
                    for gr in range(2):
                        wait("nq_done", 12, 2 * lv + gr + 1)
                        b = bank[6 + gr][:, :].rearrange("p (h x t) -> p h x t", h=GP, x=2)
                        at = pairs(gr)
                        if lv == 0:
                            wait("q_ok", 2, gr + 1)
                        if 0 < lv < 5:
                            nc.vector.tensor_tensor(nq[:, at, 1, :], b[:, :, 1, :], nq[:, at, 1, :], ALU.add).then_inc(sem["nq_ev"], 1)
                        if lv < 4:
                            wait("nd_ok", ND_PER, nd_after(lv - 1, gr) if lv else 2)
                            nc.vector.tensor_copy(nq[:, at, 0, :], b[:, :, 0, :]).then_inc(sem["nq_ev"], 1)
                        for x in range(2):
                            if lv == 5:
                                nc.vector.tensor_tensor(q_diag[half(x), at, half(x)], b[half(x), :, 1, :], nq[half(x), at, 1, :], ALU.add).then_inc(sem["nq_ev"], 1)
                    if lv < 4:
                        q = QUARTERS[lv]
                        b = bank[q][:, :].rearrange("p (h x) -> p h x", h=GP)
                        nc.vector.tensor_tensor(be[half(q // 2), pairs(q % 2), 1, :], b[0:C, :, C:2 * C], spread(mask[0:C, C:2 * C], GP), ALU.mult).then_inc(sem["me_ok"], 1)
                        nc.vector.tensor_tensor(first[C:P, GP * q:GP * q + GP, :], b[C:P, :, :], spread(mask[C:P, :], GP), ALU.mult).then_inc(sem["me_ok"], 1)
                wait("y_st", 16, 0)
                for b in range(2):
                    wait("o1_done", 2, b + 1)
                    nc.vector.tensor_copy(ybuf[C:P, heads(b), :], bank[4 + b][C:P, :].rearrange("p (h v) -> p h v", h=8)).then_inc(sem["yp_ev"], 1)
                for gr in range(2):
                    wait("fe_done", 2, gr + 1)
                    nc.vector.tensor_copy(second[0:C, GP * gr:GP * gr + GP, :], bank[gr][0:C, :].rearrange("p (h x) -> p h x", h=GP)).then_inc(sem["fe_ev_d"], 1)
                wait("dec_ok", 2, 2)
                wait("yp_ev", 2, 2)
                for b in range(2):
                    wait("o2_done", 2, b + 1)
                    o = bank[4 + b][:, :].rearrange("p (h v) -> p h v", h=8)
                    nc.vector.tensor_tensor(sv[0:C, heads(b), :], o[0:C, :, :], decayed[:, heads(b), :], ALU.add).then_inc(sem["so_ev"], 1)
                    nc.vector.tensor_tensor(ybuf[C:P, heads(b), :], o[C:P, :, :], ybuf[C:P, heads(b), :], ALU.add).then_inc(sem["so_ev"], 1)

        @block.tensor
        def _(pe):
            for x in ["mm_done", "n_done", "t_done", "nq_done", "nt_done", "o1_done", "fe_done", "o2_done"]:
                pe.sem_inc(sem[x], 1)
            pe.wait_ge(setup, 2)
            pe.wait_ge(zeroed, 3)
            head = lambda place: (2 * place, 0) if place < 8 else (2 * (place - 8) + 1, 1)
            flat = lambda t: t.rearrange("p x t -> p (x t)")
            with pe.Fori(0, NC) as c:
                wait = waiter(pe, c)
                wait("bks_ok", 2, 2)
                wait("te_ok", 8, 0)
                for m in range(KT):
                    ins = nc.tensor.transpose(bank[6 + m // 4][:, 128 * (m % 4):128 * (m % 4) + 128], flat(BKS[:, m, :, :]), g["ident"][:, :])
                    if m % 4 == 3:
                        ins.then_inc(sem["t_done"], 1)
                wait("ar_ok", 2, 2)
                wait("bk_ok", 2, 2)
                wait("fe_ev_d", 2, 0)
                wait("fe_ev_a", 2, 0)
                for q in QUARTERS:
                    for place in range(GP * q, GP * q + GP):
                        h, par = head(place)
                        ins = nc.tensor.matmul(bank[q][:, 128 * (place % 4):128 * (place % 4) + 128],
                                               flat(BK[half(par), h // 2, :, :]), flat(AR[half(par), h // 2, :, :]), start=True, stop=True)
                    ins.then_inc(sem["mm_done"], 1)
                wait("so_ev", 4, 0)
                pe.sem_inc(turn, 1)
                for place in range(H):
                    h, par = head(place)
                    ins = nc.tensor.matmul(bank[4 + place // 8][0:C, C * (place % 8):C * (place % 8) + C],
                                           AR[half(par), h // 2, 0, :], BK[half(par), h // 2, 0, :], start=True, stop=True)
                    if place % 8 == 7:
                        ins.then_inc(sem["n_done"], 1)
                for lv in range(6):
                    for gr in range(2):
                        if lv == 0:
                            wait("ne_ok", 2, 2)
                            wait("te_ok", 8, 4 * (gr + 1))
                            wait("td_ok", 4, 2 * (gr + 1))
                        else:
                            wait("nq_ev", NQ_PER, nq_after(lv - 1, gr))
                            wait("nt_ev", NT_PER, nt_after(lv - 1, gr) - nt_later[lv - 1])
                        if lv == 1:
                            wait("q_ok", 2, gr + 1)
                        lo, hi = (0, 1) if lv == 0 else (0, 2) if lv < 4 else (1, 2)
                        for i in range(GP):
                            ins = nc.tensor.matmul(bank[6 + gr][:, 2 * C * i + C * lo:2 * C * i + C * hi], t_diag[:, GP * gr + i, :],
                                                   flat(nq[:, GP * gr + i, lo:hi, :]), start=True, stop=True)
                        ins.then_inc(sem["nq_done"], 1)
                        if lv < 5:
                            if lv == 0:
                                wait("nd_ok", ND_PER, 2)
                            else:
                                wait("nd_ok", ND_PER, nd_after(lv - 1, gr))
                                wait("nt_ev", NT_PER, nt_after(lv - 1, gr))
                            for i in range(GP):
                                ins = nc.tensor.matmul(bank[4 + gr][:, C * i:C * i + C], n_diag[:, GP * gr + i, :], nt[:, GP * gr + i, :], start=True, stop=True)
                            ins.then_inc(sem["nt_done"], 1)
                wait("lh_ok", 2, 2)
                wait("v_in", 32, 32)
                wait("me_ok", 8, 8)
                for b in range(2):
                    for i in range(8):
                        ins = nc.tensor.matmul(bank[4 + b][:, HD * i:HD * i + HD], first[:, 8 * b + i, :], sv[:, 2 * i + b, :], start=True, stop=True)
                    ins.then_inc(sem["o1_done"], 1)
                wait("te_ok", 8, 8)
                for gr in range(2):
                    wait("nq_ev", NQ_PER, nq_after(5, gr))
                    for i in range(GP):
                        ins = nc.tensor.matmul(bank[gr][:, 128 * i:128 * i + 128], q_diag[:, GP * gr + i, :], flat(be[:, GP * gr + i, :, :]), start=True, stop=True)
                    ins.then_inc(sem["fe_done"], 1)
                for b in range(2):
                    wait("z_ev", 2, b + 1)
                    wait("yp_ev", 2, b + 1)
                    wait("fe_ev_a" if b else "fe_ev_d", 2, 2)
                    for i in range(8):
                        ins = nc.tensor.matmul(bank[4 + b][:, HD * i:HD * i + HD], second[:, 8 * b + i, :], zv[:, 2 * i + b, :], start=True, stop=True)
                    ins.then_inc(sem["o2_done"], 1)


def rwkv_finish(nc, io, g, rw):
    h = g["h"]
    with Scope(nc, "finish") as s:
        big = lambda x: rw[x][:, :, :].rearrange("p a b -> p (a b)").rearrange("p (j d) -> p j d", j=J)
        y, v, gate, sq, zT = big("r"), big("k"), big("w"), big("a"), rw["n"]
        ring = [rw[x][:, :, :] for x in ["e1", "e2"]]
        lnw, lnb = (rw["tmp"][:, 2 * i:2 * i + 2, :].rearrange("p a b -> p (a b)") for i in range(2))
        mu = s.sb("mu", [P, J, H])
        var = s.sb("var", [P, J, H])
        bank = g["bank"]
        v_in, g_in, lnw_in, lnb_in, bonus_ok = map(s.sem, ["v_in", "g_in", "lnw_in", "lnb_in", "bonus_ok"])
        squared = s.sem("squared")
        y_in, h_in, wo_in, order, mu_ok, cent_ok, sq_ok, var_ok, root_ok = map(
            s.sem, ["y_in", "h_in", "wo_in", "order", "mu_ok", "cent_ok", "sq_ok", "var_ok", "root_ok"])
        z_ok, tr, ev_a, ev_d, o_done, h_ok, pool_order = map(s.sem, ["z_ok", "tr", "ev_a", "ev_d", "o_done", "h_ok", "pool_order"])
        wide = lambda t, j: t[:, j, :].rearrange("p (h x) -> p h x", x=1).to_broadcast([P, H, HD])
        split = lambda t, j: t[:, j, :].rearrange("p (h x) -> p h x", h=H)
        block = s.enter_context(nc.Block())

        @block.sync
        def _(sp):
            tiles = lambda d: d.rearrange("(p j) d -> p j d", j=J)
            sp.dma_start(y, tiles(io["y_dram"])).then_inc(y_in, 16)
            sp.dma_start(v, tiles(io["v_dram"])).then_inc(v_in, 16)
            sp.dma_start(lnb, io["rwkv_ln_b"].to_broadcast([P, D])).then_inc(lnb_in, 16)
            sp.dma_start(lnw, io["rwkv_ln_w"].to_broadcast([P, D])).then_inc(lnw_in, 16)
            sp.dma_start(gate, tiles(io["g_dram"])).then_inc(g_in, 16)
            for i in range(2):
                sp.dma_start(ring[i], io["rwkv_w_o"][0, :, 512 * i:512 * i + 512].rearrange("(k p) n -> p k n", p=P)).then_inc(wo_in, 16)
            sp.dma_start(h[:, :, :], tiles(io["x"][0])).then_inc(h_in, 16)

        @block.vector
        def _(dve):
            dve.wait_ge(y_in, 16)
            ch = Chain(dve, order)
            for j in range(J):
                nc.vector.tensor_reduce(out=mu[:, j, :], in_=split(y, j), axis=AX.X, op=ALU.add).then_inc(mu_ok, 1)
            for j in range(J):
                dve.wait_ge(mu_ok, j + 1)
                ch.link(nc.vector.tensor_scalar(mu[:, j, :], mu[:, j, :], 1.0 / HD, None, ALU.mult))
                nc.vector.tensor_tensor(split(y, j), split(y, j), wide(mu, j), ALU.subtract).then_inc(cent_ok, 1)
            for j in range(J):
                dve.wait_ge(sq_ok, j + 1)
                nc.vector.tensor_reduce(out=var[:, j, :], in_=split(sq, j), axis=AX.X, op=ALU.add).then_inc(var_ok, 1)
            for j in range(J):
                dve.wait_ge(root_ok, j + 1)
                ch.link(nc.vector.reciprocal(var[:, j, :], var[:, j, :]))
                ch.link(nc.vector.tensor_tensor(split(y, j), split(y, j), wide(var, j), ALU.mult))
                dve.wait_ge(lnw_in, 16)
                ch.link(nc.vector.tensor_tensor(y[:, j, :], y[:, j, :], lnw, ALU.mult))
                dve.wait_ge(bonus_ok, j + 1)
                ch.link(nc.vector.tensor_tensor(y[:, j, :], y[:, j, :], v[:, j, :], ALU.add))
                dve.wait_ge(g_in, 16)
                nc.vector.tensor_tensor(y[:, j, :], y[:, j, :], gate[:, j, :], ALU.mult).then_inc(z_ok, 1)
            for kt in range(1, KT, 2):
                dve.wait_ge(tr, kt + 1)
                nc.vector.tensor_copy(zT[:, kt, :], bank[kt][:, :]).then_inc(ev_d, 1)
            dve.wait_ge(h_in, 16)
            for u in range(2 * J):
                dve.wait_ge(o_done, u + 1)
                hh = h[:, u // 2, 512 * (u % 2):512 * (u % 2) + 512]
                nc.vector.tensor_tensor(hh, bank[u][:, :], hh, ALU.add).then_inc(h_ok, 1)

        @block.gpsimd
        def _(pool):
            ch = Chain(pool, pool_order)
            pool.wait_ge(v_in, 16)
            pool.wait_ge(lnb_in, 16)
            for j in range(J):
                ch.link(nc.gpsimd.tensor_tensor(split(v, j), split(v, j), wide(g["bonus"], j), ALU.mult))
                nc.gpsimd.tensor_tensor(v[:, j, :], v[:, j, :], lnb, ALU.add).then_inc(bonus_ok, 1)

        @block.scalar
        def _(act):
            for j in range(J):
                act.wait_ge(cent_ok, j + 1)
                nc.scalar.activation(sq[:, j, :], y[:, j, :], ACT.Square).then_inc(sq_ok, 1)
            for j in range(J):
                act.wait_ge(var_ok, j + 1)
                nc.scalar.activation(var[:, j, :], var[:, j, :], ACT.Sqrt, scale=1.0 / HD, bias=g["eps"][:, 1:2]).then_inc(root_ok, 1)
            for kt in range(0, KT, 2):
                act.wait_ge(tr, kt + 1)
                nc.scalar.activation(zT[:, kt, :], bank[kt][:, :], ACT.Copy).then_inc(ev_a, 1)
            for j in range(J):
                act.wait_ge(h_ok, 2 * j + 2)
                square_tile(nc, act, g, j, sq[:, 0, :], squared)

        @block.tensor
        def _(pe):
            for j in range(J):
                pe.wait_ge(z_ok, j + 1)
                for kt in range(KT):
                    ins = nc.tensor.transpose(bank[kt][:, P * j:P * j + P], y[:, j, P * kt:P * kt + P], g["ident"][:, :])
                    if j == J - 1:
                        ins.then_inc(tr, 1)
            pe.wait_ge(ev_a, KT // 2)
            pe.wait_ge(ev_d, KT // 2)
            pe.wait_ge(wo_in, 32)
            for u in range(2 * J):
                for kt in range(KT):
                    last = nc.tensor.matmul(bank[u][:, :], zT[:, kt, P * (u // 2):P * (u // 2) + P], ring[u % 2][:, kt, :], start=kt == 0, stop=kt == KT - 1)
                last.then_inc(o_done, 1)


def moe(nc, io, g, layer):
    h, bank = g["h"], g["bank"]
    NE, NG, EG = 16, 4, 4
    FH = D // 2
    SPLITS = 4
    PIECE = 4 * FH
    with Scope(nc, f"moe{layer}") as s:
        xn = s.sb("xn", [P, J, D])
        xnT = s.sb("xnT", [P, KT, T])
        gb = s.sb("gb", [P, D])
        raw = [s.sb(f"raw{i}", [P, PIECE]) for i in range(6)]
        whi = [s.sb(f"whi{i}", [P, PIECE], fp32r) for i in range(SPLITS)]
        wlo = [s.sb(f"wlo{i}", [P, PIECE], fp32r) for i in range(SPLITS)]
        xg = s.sb("xg", [P, D])
        xhi = [s.sb(f"xhi{i}", [P, KT, P], fp32r) for i in range(2)]
        xlo = [s.sb(f"xlo{i}", [P, KT, P], fp32r) for i in range(2)]
        sg = s.sb("sg", [P, FH])
        hid = s.sb("hid", [P, FH])
        hhi = s.sb("hhi", [P, FH // P, P], fp32r)
        hlo = s.sb("hlo", [P, FH // P, P], fp32r)
        yo = s.sb("yo", [P, D])
        wr = s.sb("wr", [P, KT, NG + NE])
        br = s.sb("br", [P, NG + NE])
        ss, rstd = s.sb("ss", [P, J]), s.sb("rstd", [P, J])
        lg = s.sb("logits", [P, J, NG + NE])
        v4 = [s.sb(f"v4_{i}", [P, J]) for i in range(10)]
        v16 = [s.sb(f"v16_{i}", [P, J, 4]) for i in range(7)]
        v64 = [s.sb(f"v64_{i}", [P, J, NG, EG]) for i in range(5)]
        rank = s.sb("rank", [P, J, NE])
        msum = s.sb("msum", [P, NE])
        posf = s.sb("posf", [P, 2, J])
        pos = s.sb("pos", [P, 2, J], i32)
        first_place, later = s.sb("first_place", [P, 2, J]), s.sb("later", [P, 2, J])
        wgt = s.sb("wgt", [P, 2, J])
        zeros = s.sb("zeros", [NE * J, P])
        tokrow = s.sb("tokrow", [NE * J, P])
        idx = s.sb("idx", [P, NE * J], i32)
        idxcol = s.sb("idxcol", [P, 1], i32)
        most = s.sb("most", [P, 2])
        mosti = s.sb("mosti", [P, 1], i32)
        par_in, squared, rms, rstd_ok, xn_ok, xn_st, tr, ev_a, ev_d, lg_done, order = map(
            s.sem, ["par_in", "squared", "rms", "rstd_ok", "xn_ok", "xn_st", "tr", "ev_a", "ev_d", "lg_done", "order"])
        gs_ok, eg_ok, d_ok, e2_ok, ms_ok, rank_done, pos_ok, tok_zero, tok_st, tok_in, tok_tr, idx_ok, zero_ok = map(
            s.sem, ["gs_ok", "eg_ok", "d_ok", "e2_ok", "ms_ok", "rank_done", "pos_ok", "tok_zero", "tok_st", "tok_in", "tok_tr", "idx_ok", "zero_ok"])
        comb_in = [s.sem(f"comb_in{i}") for i in range(J)]
        comb_ok, turn = s.sem("comb_ok"), s.sem("turn")

        def loop_sems(tag):
            r = {x: s.sem(tag + x) for x in ["hi_ok", "split_ok", "piece_used", "xt_done", "xh_ok", "xl_ok", "sg_ok", "hid_ok", "ht_done", "hh_ok", "hl_ok",
                                             "y_ok", "col_ok", "xg_in", "y_st"]}
            r["lead"] = 2 if tag else SPLITS
            r["raw_in"] = [s.sem(f"{tag}raw_in{i}") for i in range(6)]
            return r

        main, more = loop_sems(""), loop_sems("more_")
        xn_dram, tok_dram, out_dram = io[f"xn_dram{layer}"], io[f"tok_dram{layer}"], io[f"out_dram{layer}"]
        block = s.enter_context(nc.Block())

        second_output = xnT[:, :, :].rearrange("p a b -> p (a b)").rearrange("p (j d) -> p j d", j=J)

        def start(eng, m, names):
            for x in names:
                eng.sem_inc(m[x], {"split_ok": 6, "piece_used": m["lead"]}.get(x, 1))

        def load_piece(sp, m, n, slot, kind, e, half):
            sp.wait_ge(m["split_ok"], n + 1)
            w = io["moe_w_" + kind][layer, bass.ds(e, 1), :, :]
            w = w[:, :, 512 * half:512 * half + 512] if kind == "down" else w[:, 512 * half:512 * half + 512, :]
            sp.dma_start(raw[slot % 6][:, :].rearrange("p (k n) -> p k n", k=4),
                         w.rearrange("a (k p) n -> p (a k) n", p=P)).then_inc(m["raw_in"][slot % 6], 16)

        def split_hi(act, m, n, slot, uses):
            act.wait_ge(m["raw_in"][slot % 6], uses * 16)
            act.wait_ge(m["piece_used"], n + 1)
            nc.scalar.activation(whi[slot % SPLITS][:, :], raw[slot % 6][:, :], ACT.Copy).then_inc(m["hi_ok"], 1)

        def split_lo(dve, m, n, slot):
            dve.wait_ge(m["hi_ok"], n + 2)
            nc.vector.tensor_tensor(wlo[slot % SPLITS][:, :], raw[slot % 6][:, :], whi[slot % SPLITS][:, :].bitcast(fp32), ALU.subtract).then_inc(m["split_ok"], 1)

        def product(pe, m, n, slot, b, hi, lo, k0, begin, end):
            pe.wait_ge(m["split_ok"], n + 7)
            wh, wl = (w[slot % SPLITS][:, :].rearrange("p (k n) -> p k n", k=4) for w in (whi, wlo))
            for k in range(4):
                nc.tensor.matmul(bank[b][:, :], hi[:, k0 + k, :], wh[:, k, :], start=begin and k == 0, stop=False)
                nc.tensor.matmul(bank[b][:, :], hi[:, k0 + k, :], wl[:, k, :], start=False, stop=False)
                ins = nc.tensor.matmul(bank[b][:, :], lo[:, k0 + k, :], wh[:, k, :], start=False, stop=end and k == 3)
            ins.then_inc(m["piece_used"], 1)

        def pe_tokens(pe, m, c):
            pe.wait_ge(m["xg_in"], c * 16 + 16)
            pe.wait_ge(m["xl_ok"], c * 2 + 1)
            for kt in range(KT):
                ins = nc.tensor.transpose(bank[kt // 4][:, P * (kt % 4):P * (kt % 4) + P], xg[:, P * kt:P * kt + P], g["ident"][:, :])
            ins.then_inc(m["xt_done"], 1)

        def pe_hidden(pe, m, c):
            pe.wait_ge(m["hid_ok"], c + 2)
            pe.wait_ge(m["hl_ok"], c + 1)
            for kt in range(FH // P):
                ins = nc.tensor.transpose(bank[4][:, P * kt:P * kt + P], hid[:, P * kt:P * kt + P], g["ident"][:, :])
            ins.then_inc(m["ht_done"], 1)

        def pe_gate(pe, m, c, x, half, n, slot):
            if half == 0:
                pe.wait_ge(m["xl_ok"], c * 2 + 3)
                pe.wait_ge(m["sg_ok"], c + 1)
            product(pe, m, n, slot, 2, xhi[x], xlo[x], 4 * half, half == 0, half == 1)

        def pe_up(pe, m, c, x, half, n, slot):
            if half == 0:
                pe.wait_ge(m["hid_ok"], c + 1)
            product(pe, m, n, slot, 3, xhi[x], xlo[x], 4 * half, half == 0, half == 1)

        def pe_down(pe, m, c, half, n, slot):
            pe.wait_ge(m["y_ok"], c * 2 + 1)
            if half == 0:
                pe.wait_ge(m["hl_ok"], c + 2)
            product(pe, m, n, slot, 5 + half, hhi, hlo, 0, True, True)

        def act_tokens(act, m, c, x):
            act.wait_ge(m["xt_done"], c + 2)
            for b in range(2):
                nc.scalar.activation(xhi[x][:, 4 * b:4 * b + 4, :], bank[b][:, :].rearrange("p (k t) -> p k t", k=4), ACT.Copy).then_inc(m["xh_ok"], 1)

        def dve_tokens(dve, m, c, x):
            for b in range(2):
                dve.wait_ge(m["xh_ok"], c * 2 + b + 2)
                nc.vector.tensor_tensor(xlo[x][:, 4 * b:4 * b + 4, :], bank[b][:, :].rearrange("p (k t) -> p k t", k=4),
                                        xhi[x][:, 4 * b:4 * b + 4, :].bitcast(fp32), ALU.subtract).then_inc(m["xl_ok"], 1)

        def act_gate(act, m, c, n):
            act.wait_ge(m["piece_used"], n + m["lead"] + 1)
            act.wait_ge(m["hid_ok"], c + 1)
            nc.scalar.activation(sg[:, :], bank[2][:, :], ACT.Silu).then_inc(m["sg_ok"], 1)

        def dve_up(dve, m, c, n):
            dve.wait_ge(m["piece_used"], n + m["lead"] + 1)
            dve.wait_ge(m["sg_ok"], c + 2)
            dve.wait_ge(m["ht_done"], c + 1)
            nc.vector.tensor_tensor(hid[:, :], bank[3][:, :], sg[:, :], ALU.mult).then_inc(m["hid_ok"], 1)

        def act_hidden(act, m, c):
            act.wait_ge(m["ht_done"], c + 2)
            nc.scalar.activation(hhi[:, :, :], bank[4][:, :].rearrange("p (k t) -> p k t", k=4), ACT.Copy).then_inc(m["hh_ok"], 1)

        def dve_hidden(dve, m, c):
            dve.wait_ge(m["hh_ok"], c + 2)
            nc.vector.tensor_tensor(hlo[:, :, :], bank[4][:, :].rearrange("p (k t) -> p k t", k=4), hhi[:, :, :].bitcast(fp32),
                                    ALU.subtract).then_inc(m["hl_ok"], 1)

        def act_output(act, m, c, half, n):
            act.wait_ge(m["piece_used"], n + m["lead"] + 1)
            if half == 0:
                act.wait_ge(m["y_st"], c * 16 + 1)
            nc.scalar.activation(yo[:, 512 * half:512 * half + 512], bank[5 + half][:, :], ACT.Copy).then_inc(m["y_ok"], 1)

        def store_output(act, m, c, row):
            act.wait_ge(m["y_ok"], c * 2 + 3)
            act.dma_start(out_dram[bass.ds(row, P), :], yo[:, :]).then_inc(m["y_st"], 16)

        def piece(e, x, k):
            if isinstance(e, int) and e == 0:
                return k, k, 1
            return e * 6 + (k - 2), (6 * x + k - 2) % 12, e + (0 if k < 2 else 1)

        def rounds(eng, body):
            body(0, 0)
            with eng.Fori(0, NE // 2 - 1) as i:
                body(i * 2 + 1, 1)
                body(i * 2 + 2, 0)
            body(NE - 1, 1)

        def each_further(eng, body):
            with eng.Fori(0, NE) as e:
                with eng.Fori(1, J) as b:
                    body(e, b, e * (J - 1) + (b - 1))

        def overflow(eng):
            longest = eng.value_load(mosti[0:1, 0:1], min_val=0, max_val=T)
            return eng.If(longest > P)

        def no_overflow(eng):
            return eng.If(eng.value_load(mosti[0:1, 0:1], min_val=0, max_val=T) < P + 1)

        @block.sync
        def _(sp):
            sp.dma_start(gb[:, :], io["norm_ffn_g"][layer:layer + 1, :].to_broadcast([P, D])).then_inc(par_in, 16)
            sp.dma_start(wr[:, :, 0:NG], io["moe_w_grp"][layer].rearrange("(k p) n -> p k n", p=P)).then_inc(par_in, 16)
            sp.dma_start(wr[:, :, NG:], io["moe_w_exp"][layer].rearrange("(k p) n -> p k n", p=P)).then_inc(par_in, 16)
            sp.dma_start(br[:, 0:NG], io["moe_b_grp"][layer:layer + 1, :].to_broadcast([P, NG])).then_inc(par_in, 16)
            sp.dma_start(br[:, NG:], io["moe_b_exp"][layer:layer + 1, :].to_broadcast([P, NE])).then_inc(par_in, 16)
            sp.wait_ge(zero_ok, 1)
            sp.dma_start(tok_dram.rearrange("(a b) x -> a (b x)", b=P), zeros[:, :]).then_inc(tok_zero, 16)
            def load_round(e, x):
                first = isinstance(e, int) and e == 0
                todo = [("gate", 0, e), ("gate", 1, e)] + ([] if first else [("down", 0, e - 1), ("down", 1, e - 1)]) + [("up", 0, e), ("up", 1, e)]
                for k, (kind, half, ee) in enumerate(todo):
                    n, slot, uses = piece(e, x, k)
                    load_piece(sp, main, n, slot, kind, ee, half)

            rounds(sp, load_round)
            for half in range(2):
                n, slot, uses = piece(NE, 0, half)
                load_piece(sp, main, n, slot, "down", NE - 1, half)
            sp.wait_ge(pos_ok, 2)
            with overflow(sp):
                sp.wait_ge(main["split_ok"], 6 + 6 * NE)

                def further_round(e, b, c):
                    for k, (kind, half) in enumerate([("gate", 0), ("gate", 1), ("up", 0), ("up", 1), ("down", 0), ("down", 1)]):
                        load_piece(sp, more, c * 6 + k, k, kind, e, half)

                each_further(sp, further_round)

        @block.gpsimd
        def _(pool):
            nc.gpsimd.memset(zeros[:, :], 0.0).then_inc(zero_ok, 1)
            start(pool, main, ["col_ok"])
            pool.wait_ge(pos_ok, 2)
            pool.wait_ge(tok_zero, 16)
            for k in range(2):
                for j in range(J):
                    pool.indirect_dma_start(tok_dram, bass.IndirectOffsetOnAxis(ap=pos[:, k, j:j + 1], axis=0), g["tokid"][:, j:j + 1], None).then_inc(tok_st, 16)
            pool.wait_ge(tok_st, 16 * 2 * J)
            pool.dma_start(tokrow[:, :], tok_dram.rearrange("(a b) x -> a (b x)", b=P)).then_inc(tok_in, 16)
            pool.wait_ge(idx_ok, 1)
            pool.wait_ge(xn_st, 16)

            def fetch(m, col, c):
                pool.wait_ge(m["xt_done"], c + 1)
                nc.gpsimd.tensor_copy(idxcol[:, :], idx[:, bass.ds(col, 1)]).then_inc(m["col_ok"], 1)
                pool.wait_ge(m["col_ok"], c + 2)
                pool.sem_inc(turn, 1)
                pool.indirect_dma_start(xg[:, :], None, xn_dram, bass.IndirectOffsetOnAxis(ap=idxcol[:, :], axis=0)).then_inc(m["xg_in"], 16)

            with pool.Fori(0, NE) as e:
                fetch(main, e, e)
            with overflow(pool):
                start(pool, more, ["col_ok"])
                pool.wait_ge(main["xt_done"], NE + 1)
                each_further(pool, lambda e, b, c: fetch(more, b * NE + e, c))
            pool.wait_ge(main["y_st"], 16 * NE + 1)
            with overflow(pool):
                pool.wait_ge(more["y_st"], 16 * NE * (J - 1) + 1)

            def outputs(rows):
                for j in range(J):
                    for k in range(2):
                        dst = (xn if k == 0 else second_output)[:, j, :]
                        pool.indirect_dma_start(dst, None, rows, bass.IndirectOffsetOnAxis(ap=pos[:, k, j:j + 1], axis=0)).then_inc(comb_in[j], 16)

            with overflow(pool):
                outputs(out_dram)
            with no_overflow(pool):
                outputs(out_dram[0:NE * P, :])
            for j in range(J):
                pool.wait_ge(comb_in[j], 32)

        @block.scalar
        def _(act):
            start(act, main, ["hi_ok", "xh_ok", "sg_ok", "hh_ok", "y_ok", "y_st"])
            nc.scalar.activation(ss[:, :], g["ss"][:, :], ACT.Sqrt, scale=1.0 / D, bias=g["eps"][:, 0:1]).then_inc(rms, 1)
            act.wait_ge(xn_ok, J)
            act.dma_start(xn_dram.rearrange("(p j) d -> p j d", j=J), xn[:, :, :]).then_inc(xn_st, 16)
            for kt in range(0, KT, 2):
                act.wait_ge(tr, kt + 1)
                nc.scalar.activation(xnT[:, kt, :], bank[kt][:, :], ACT.Copy).then_inc(ev_a, 1)
            act.wait_ge(gs_ok, 1)
            nc.scalar.activation(v16[0][:, :, :], v16[0][:, :, :], ACT.Exp).then_inc(eg_ok, 1)
            act.wait_ge(d_ok, 1)
            nc.scalar.activation(v4[5][:, :], v4[5][:, :], ACT.Exp).then_inc(e2_ok, 1)
            for k in range(SPLITS):
                split_hi(act, main, *piece(0, 0, k))
            act.wait_ge(rank_done, 1)
            act_tokens(act, main, 0, 0)

            def round_(e, x):
                first, last = (isinstance(e, int) and e == v for v in (0, NE - 1))
                todo = ([] if first else [piece(e, x, k) for k in (4, 5)]) + [piece(e + 1, 1 - x, k) for k in range(2 if last else 4)]
                hi = lambda: split_hi(act, main, *todo.pop(0))
                if not first:
                    act_hidden(act, main, e - 1)
                    hi()
                act_gate(act, main, e, piece(e, x, 1)[0])
                hi()
                if not first:
                    act_output(act, main, e - 1, 0, piece(e, x, 2)[0])
                    hi()
                    act_output(act, main, e - 1, 1, piece(e, x, 3)[0])
                    store_output(act, main, e - 1, (e - 1) * P)
                if not last:
                    act_tokens(act, main, e + 1, 1 - x)
                while todo:
                    hi()

            rounds(act, round_)
            act_hidden(act, main, NE - 1)
            for half in range(2):
                act_output(act, main, NE - 1, half, piece(NE, 0, half)[0])
            store_output(act, main, NE - 1, (NE - 1) * P)
            with overflow(act):
                start(act, more, ["hi_ok", "xh_ok", "sg_ok", "hh_ok", "y_ok", "y_st"])
                act.wait_ge(main["y_st"], 16 * NE + 1)

                def further_round(e, b, c):
                    act_tokens(act, more, c, 0)
                    for k in range(6):
                        split_hi(act, more, c * 6 + k, k, c + 1)
                        if k == 3:
                            act_gate(act, more, c, c * 6 + 1)
                    act_hidden(act, more, c)
                    for half in range(2):
                        act_output(act, more, c, half, c * 6 + (4 + half))
                    store_output(act, more, c, b * (NE * P) + e * P)

                each_further(act, further_round)
            for j in range(J):
                act.wait_ge(comb_ok, 2 * j + 2)
                square_tile(nc, act, g, j, raw[0][:, 0:D], squared)

        @block.vector
        def _(dve):
            start(dve, main, ["split_ok", "xl_ok", "hid_ok", "hl_ok"])
            dve.wait_ge(rms, 1)
            nc.vector.reciprocal(rstd[:, :], ss[:, :]).then_inc(rstd_ok, 1)
            dve.wait_ge(rstd_ok, 1)
            dve.wait_ge(par_in, 80)
            for j in range(J):
                nc.vector.scalar_tensor_tensor(out=xn[:, j, :], in0=h[:, j, :], scalar=rstd[:, j:j + 1], in1=gb[:, :], op0=ALU.mult, op1=ALU.mult).then_inc(xn_ok, 1)
            for kt in range(1, KT, 2):
                dve.wait_ge(tr, kt + 1)
                nc.vector.tensor_copy(xnT[:, kt, :], bank[kt][:, :]).then_inc(ev_d, 1)
            ch = Chain(dve, order)
            V = nc.vector
            gl = lg[:, :, 0:NG]
            el = lg[:, :, NG:].rearrange("p j (g e) -> p j g e", g=NG)
            over = lambda t: t[:, :].rearrange("p (j x) -> p j x", x=1).to_broadcast([P, J, 4])
            reduce = lambda out, in_, op: ch.link(V.tensor_reduce(out=out, in_=in_, axis=AX.X, op=op))
            tt = lambda out, a, b, op: ch.link(V.tensor_tensor(out, a, b, op))
            dve.wait_ge(lg_done, 1)
            tt(lg[:, :, :], bank[0][:, 0:J * (NG + NE)].rearrange("p (j n) -> p j n", j=J),
               br[:, :].rearrange("p (x n) -> p x n", x=1).to_broadcast([P, J, NG + NE]), ALU.add)
            gm, psum, m1, m2, top, dd = v4[0], v4[1], v4[2], v4[3], v4[4], v4[5]
            reduce(gm[:, :], gl, ALU.max)
            V.tensor_tensor(v16[0][:, :, :], gl, over(gm), ALU.subtract).then_inc(gs_ok, 1)

            def first_equal(out, vals, m):
                tt(out[:, :, :], vals, over(m), ALU.is_equal)
                tt(out[:, :, :], out[:, :, :], g["down4"][:, :].rearrange("p (x n) -> p x n", x=1).to_broadcast([P, J, 4]), ALU.mult)
                reduce(top[:, :], out[:, :, :], ALU.max)
                tt(out[:, :, :], out[:, :, :], over(top), ALU.is_equal)

            og, sel, o1, sel2, o2 = v16[1], v16[2], v16[3], v16[4], v16[5]
            first_equal(og, gl, gm)
            inner = lambda t: t[:, :, :].rearrange("p j (n x) -> p j n x", x=1).to_broadcast([P, J, NG, EG])
            outer = lambda t: t[:, :, :].rearrange("p j (x n) -> p j x n", x=1).to_broadcast([P, J, NG, EG])
            tt(v64[0][:, :, :, :], el, inner(og), ALU.mult)
            reduce(sel[:, :, :], v64[0][:, :, :, :].rearrange("p j g e -> p j e g"), ALU.add)
            reduce(m1[:, :], sel[:, :, :], ALU.max)
            first_equal(o1, sel[:, :, :], m1)
            ch.link(V.scalar_tensor_tensor(out=sel2[:, :, :], in0=o1[:, :, :], scalar=-3.0e38, in1=sel[:, :, :], op0=ALU.mult, op1=ALU.add))
            reduce(m2[:, :], sel2[:, :, :], ALU.max)
            V.tensor_tensor(dd[:, :], m2[:, :], m1[:, :], ALU.subtract).then_inc(d_ok, 1)
            first_equal(o2, sel2[:, :, :], m2)
            M1, M2, M = v64[1], v64[2], v64[3]
            tt(M1[:, :, :, :], inner(og), outer(o1), ALU.mult)
            tt(M2[:, :, :, :], inner(og), outer(o2), ALU.mult)
            tt(M[:, :, :, :], M1[:, :, :, :], M2[:, :, :, :], ALU.add)
            flat = lambda t: t[:, :, :, :].rearrange("p j g e -> p j (g e)")
            V.tensor_reduce(out=msum[:, :], in_=flat(M).rearrange("p j n -> p n j"), axis=AX.X, op=ALU.add).then_inc(ms_ok, 1)
            dve.wait_ge(eg_ok, 1)
            reduce(psum[:, :], v16[0][:, :, :], ALU.add)
            dve.wait_ge(e2_ok, 1)
            ch.link(V.tensor_scalar(v4[6][:, :], dd[:, :], 1.0, None, ALU.add))
            tt(v4[6][:, :], v4[6][:, :], psum[:, :], ALU.mult)
            ch.link(V.reciprocal(wgt[:, 0, :], v4[6][:, :]))
            tt(wgt[:, 1, :], wgt[:, 0, :], dd[:, :], ALU.mult)
            dve.wait_ge(rank_done, 1)
            ch.link(V.tensor_copy(rank[:, 0, :], bank[1][:, 0:NE]))
            for j in range(1, J):
                tt(rank[:, j, :], rank[:, j - 1, :], flat(M)[:, j - 1, :], ALU.add)
            for k, Mk in enumerate([M1, M2]):
                tt(v64[4][:, :, :, :].rearrange("p j g e -> p j (g e)"), flat(Mk), rank[:, :, :], ALU.mult)
                reduce(posf[:, k, :], flat(v64[4]), ALU.add)
                tt(flat(v64[4]), flat(Mk), g["base16"][:, :].rearrange("p (x n) -> p x n", x=1).to_broadcast([P, J, NE]), ALU.mult)
                reduce(first_place[:, k, :], flat(v64[4]), ALU.add)
            for b in range(1, J):
                ch.link(V.tensor_scalar(later[:, :, :], posf[:, :, :], float(P * b), float(NE * P - P), ALU.is_ge, ALU.mult))
                tt(first_place[:, :, :], first_place[:, :, :], later[:, :, :], ALU.add)
            tt(posf[:, :, :], posf[:, :, :], first_place[:, :, :], ALU.add)
            V.tensor_copy(pos[:, :, :], posf[:, :, :]).then_inc(pos_ok, 1)
            reduce(most[:, 0:1], bank[1][:, NE:2 * NE], ALU.max)
            V.tensor_copy(mosti[:, :], most[:, 0:1]).then_inc(pos_ok, 1)
            for k in range(SPLITS):
                split_lo(dve, main, *piece(0, 0, k)[:2])
            dve.wait_ge(tok_tr, 1)
            V.tensor_copy(idx[:, 0:NE * J], bank[2][:, 0:NE * J]).then_inc(idx_ok, 1)
            dve_tokens(dve, main, 0, 0)

            def round_(e, x):
                first, last = (isinstance(e, int) and e == v for v in (0, NE - 1))
                todo = ([] if first else [piece(e, x, k) for k in (4, 5)]) + [piece(e + 1, 1 - x, k) for k in range(2 if last else 4)]
                lo = lambda: split_lo(dve, main, *todo.pop(0)[:2])
                if not first:
                    dve_hidden(dve, main, e - 1)
                    lo()
                    lo()
                lo()
                if not last:
                    dve_tokens(dve, main, e + 1, 1 - x)
                while len(todo) > 1:
                    lo()
                dve_up(dve, main, e, piece(e, x, 3 if first else 5)[0])
                lo()

            rounds(dve, round_)
            dve_hidden(dve, main, NE - 1)
            with overflow(dve):
                start(dve, more, ["split_ok", "xl_ok", "hid_ok", "hl_ok"])

                def further_round(e, b, c):
                    dve_tokens(dve, more, c, 0)
                    for k in range(6):
                        split_lo(dve, more, c * 6 + k, k)
                    dve_up(dve, more, c, c * 6 + 3)
                    dve_hidden(dve, more, c)

                each_further(dve, further_round)
            for j in range(J):
                dve.wait_ge(comb_in[j], 32)
                for k in range(2):
                    src = (xn if k == 0 else second_output)[:, j, :]
                    V.scalar_tensor_tensor(out=h[:, j, :], in0=src, scalar=wgt[:, k, j:j + 1], in1=h[:, j, :], op0=ALU.mult, op1=ALU.add).then_inc(comb_ok, 1)
                    dve.wait_ge(comb_ok, 2 * j + k + 1)

        @block.tensor
        def _(pe):
            start(pe, main, ["piece_used", "xt_done", "ht_done"])
            for j in range(J):
                pe.wait_ge(xn_ok, j + 1)
                for kt in range(KT):
                    ins = nc.tensor.transpose(bank[kt][:, P * j:P * j + P], xn[:, j, P * kt:P * kt + P], g["ident"][:, :])
                    if j == J - 1:
                        ins.then_inc(tr, 1)
            pe.wait_ge(ev_a, KT // 2)
            pe.wait_ge(ev_d, KT // 2)
            pe.wait_ge(par_in, 80)
            for j in range(J):
                for kt in range(KT):
                    last = nc.tensor.matmul(bank[0][:, (NG + NE) * j:(NG + NE) * (j + 1)], xnT[:, kt, P * j:P * j + P], wr[:, kt, :], start=kt == 0, stop=kt == KT - 1)
            last.then_inc(lg_done, 1)
            pe.wait_ge(ms_ok, 1)
            nc.tensor.matmul(bank[1][:, 0:NE], g["upper"][:, :], msum[:, :], start=True, stop=True)
            nc.tensor.matmul(bank[1][:, NE:2 * NE], g["ones"][:, :], msum[:, :], start=True, stop=True).then_inc(rank_done, 1)
            pe.wait_ge(tok_in, 16)
            nc.tensor.transpose(bank[2][:, 0:NE * J], tokrow[:, :], g["ident"][0:NE * J, 0:NE * J]).then_inc(tok_tr, 1)
            pe.wait_ge(idx_ok, 1)
            pe_tokens(pe, main, 0)

            def round_(e, x):
                first, last = (isinstance(e, int) and e == v for v in (0, NE - 1))
                k = iter(range(6))
                at = lambda: piece(e, x, next(k))[:2]
                pe_gate(pe, main, e, x, 0, *at())
                if not first:
                    pe_hidden(pe, main, e - 1)
                pe_gate(pe, main, e, x, 1, *at())
                if not first:
                    for half in range(2):
                        pe_down(pe, main, e - 1, half, *at())
                if not last:
                    pe_tokens(pe, main, e + 1)
                for half in range(2):
                    pe_up(pe, main, e, x, half, *at())

            rounds(pe, round_)
            pe_hidden(pe, main, NE - 1)
            for half in range(2):
                pe_down(pe, main, NE - 1, half, *piece(NE, 0, half)[:2])
            with overflow(pe):
                start(pe, more, ["piece_used", "xt_done", "ht_done"])
                pe.wait_ge(main["y_ok"], 2 * NE + 1)

                def further_round(e, b, c):
                    pe_tokens(pe, more, c)
                    for k, part in enumerate([pe_gate, pe_up]):
                        for half in range(2):
                            part(pe, more, c, 0, half, c * 6 + (2 * k + half), 2 * k + half)
                    pe_hidden(pe, more, c)
                    for half in range(2):
                        pe_down(pe, more, c, half, c * 6 + (4 + half), 4 + half)

                each_further(pe, further_round)



def attention(nc, io, g):
    h, bank = g["h"], g["bank"]
    G, AH = 3, 8
    W = AH * HD
    SCALE = HD ** -0.5
    FAR = -1.0e30
    with Scope(nc, "attn") as s:
        xhat = s.sb("xhat", [P, J, D])
        whi = [s.sb(f"whi{i}", [P, 4, W], fp32r) for i in range(2)]
        wlo = [s.sb(f"wlo{i}", [P, 4, W], fp32r) for i in range(2)]
        kT = [s.sb(f"kT{i}", [P, AH // 2, T]) for i in range(G)]
        qT = [s.sb(f"qT{i}", [P, AH // 2, T]) for i in range(G)]
        vv = [s.sb(f"v{i}", [P, J, W]) for i in range(G)]
        smb, prb, pTb = (s.sb(x, [P, 2, T]) for x in ["scores", "probs", "pT"])
        sm, pr, pT = ([v[:, i, :] for i in range(2)] for v in (smb, prb, pTb))
        oacc = [s.sb("oacc0", [P, J, W]), kT[0], qT[0]]
        raw = [xhat[:, 2 * i:2 * i + 2, :].rearrange("p a b -> p (a b)").rearrange("p (k n) -> p k n", k=4) for i in range(2)]
        mask = [s.sb("mask0", [P, J, T]), s.sb("mask1", [P, P]), s.sb("mask2", [P, P])]
        residue = s.sb("residue", [P, P])
        ss, rstd = s.sb("ss", [P, J]), s.sb("rstd", [P, J])
        negm = s.sb("negm", [P, G, J, AH])
        lsum = s.sb("lsum", [P, G, J, AH])
        least = s.sb("least", [P, J, AH])
        den = s.sb("den", [P, J, AH])
        squared, rms, rstd_ok, xhat_ok, tr, xh_ok, xl_ok, unit, ev_a, ev_d = map(
            s.sem, ["squared", "rms", "rstd_ok", "xhat_ok", "tr", "xh_ok", "xl_ok", "unit", "ev_a", "ev_d"])
        pool_order, mask_ok, res_mm, s_done, sm_ok, max_ok, p_ok, t_done, pt_ok, o_done, o_ev = map(
            s.sem, ["pool_order", "mask_ok", "res_mm", "s_done", "sm_ok", "max_ok", "p_ok", "t_done", "pt_ok", "o_done", "o_ev"])
        order, d_ok, e_ok, w_ok, comb_ok, otr, out_done, h_ok = map(
            s.sem, ["order", "d_ok", "e_ok", "w_ok", "comb_ok", "otr", "out_done", "h_ok"])
        piece_in = [s.sem(f"piece_in{i}") for i in range(2)]
        hi_ok, lo_ok, piece_used, oh_ok, ol_ok, last_ok = map(s.sem, ["hi_ok", "lo_ok", "piece_used", "oh_ok", "ol_ok", "last_ok"])
        units = [(0, hh, (j,)) for hh in range(AH) for j in range(J)] + [(gi, hh, tuple(range(J))) for gi in (1, 2) for hh in range(AH)]
        NU = len(units)
        BESIDE = 3
        NPROJ = 12 * G
        pieces = [(gi, kind, kh) for gi in range(G) for kind in range(3) for kh in range(2)]
        NP = len(pieces)

        def source(n):
            if n >= NP:
                return io["attn_w_o"][0][:, W * (n - NP):W * (n - NP) + W]
            gi, kind, kh = pieces[n]
            rows = slice(P * 4 * kh, P * 4 * kh + P * 4)
            return (io["w_kv"][rows, W * gi:W * gi + W], io["attn_w_q"][0, rows, W * gi:W * gi + W], io["w_kv"][rows, W * (G + gi):W * (G + gi) + W])[kind]

        def raw_of(n):
            return vv[1 + n][:, :, :] if n < 2 else raw[n % 2]

        def gain(n, k):
            gi, kind, kh = pieces[n]
            at = (GMIX + KT if kind == 1 else GKV) + 4 * kh + k
            return g["par"][:, at:at + 1]

        def split_hi(act, n):
            act.wait_ge(piece_in[n % 2], 16 * (n // 2 + 1))
            if n >= 2:
                if n % 2:
                    act.wait_ge(unit, 4 * ((n - 3) // 2 + 1))
                else:
                    act.wait_ge(piece_used, n // 2)
            for k in range(4):
                ins = nc.scalar.activation(whi[n % 2][:, k, :], raw_of(n)[:, k, :], ACT.Copy, scale=gain(n, k) if n < NP else 1.0)
            ins.then_inc(hi_ok, 1)

        def split_lo(dve, n):
            dve.wait_ge(hi_ok, n + 1)
            for k in range(4):
                ins = nc.vector.scalar_tensor_tensor(out=wlo[n % 2][:, k, :], in0=raw_of(n)[:, k, :], scalar=gain(n, k) if n < NP else 1.0,
                                                     in1=whi[n % 2][:, k, :].bitcast(fp32), op0=ALU.mult, op1=ALU.subtract)
            ins.then_inc(lo_ok, 1)
        with nc.sbuf_tensor("attn_xhi", [P, KT, T], fp32r) as xhi, nc.sbuf_tensor("attn_xlo", [P, KT, T], fp32r) as xlo:
            pass
        oh, ol = (s.sb(x, [P, W // P, T], fp32r) for x in ["oh", "ol"])
        block = s.enter_context(nc.Block())

        def weigh(eng, gi, j):
            heads = oacc[gi][:, j, :].rearrange("p (h v) -> p h v", h=AH)
            return eng.tensor_tensor(heads, heads, negm[:, gi, j, :].rearrange("p (h x) -> p h x", x=1).to_broadcast([P, AH, HD]), ALU.mult)

        def gather(eng, gi, j):
            return eng.tensor_tensor(oacc[0][:, j, :], oacc[0][:, j, :], oacc[gi][:, j, :], ALU.add)

        def bank_of(u):
            return bank[u % 8 if u < 4 * BESIDE else u % 4]

        def beside(sl, kh, i):
            u = 8 * (sl - BESIDE) + 4 * kh + i
            return u if 0 <= u < AH * (J + 1) else None

        def evacuated(eng, u):
            eng.wait_ge(ev_d if u % 2 else ev_a, u // 2 + 1)

        def projected(u):
            gi, kind, i = u // 12, u % 12 // 4, u % 4
            return (kT, qT, vv)[kind][gi][:, i, :]

        @block.sync
        def _(sp):
            for n in range(NP + 2):
                if n in (2, 3):
                    sp.wait_ge(tr, KT)
                if n >= 2:
                    sp.wait_ge(lo_ok, n - 1)
                sp.dma_start(raw_of(n), source(n).rearrange("(k p) n -> p k n", p=P)).then_inc(piece_in[n % 2], 16)

        @block.gpsimd
        def _(pool):
            ch = Chain(pool, pool_order)
            ch.inc(nc.gpsimd.memset(mask[0][:, :, :], 0.0))
            ch.inc(nc.gpsimd.memset(mask[1][:, :], 0.0))
            ch.inc(nc.gpsimd.memset(mask[2][:, :], 1.0))
            ch.link(nc.gpsimd.memset(residue[:, :], 0.0))

            def keep(m, op, fill, base, pattern, per_partition):
                ch.link(nc.gpsimd.affine_select(out=m, in_=m, compare_op=op, fill=fill, base=base, pattern=pattern, channel_multiplier=per_partition))

            m0 = mask[0][:, :, :].rearrange("p j (i k) -> p j i k", i=J)
            window = P
            keep(m0, ALU.is_ge, FAR, 0, [[1, J], [-1, J], [-J, P]], J)
            keep(m0, ALU.is_ge, FAR, window, [[-1, J], [1, J], [J, P]], -J)
            keep(mask[1][:, :], ALU.is_ge, FAR, 0, [[-1, P]], 1)
            keep(mask[2][:, :], ALU.is_ge, 0.0, 0, [[-1, P]], 1)
            r4 = residue[:, :].rearrange("p (a b) -> p a b", b=4)
            nc.gpsimd.affine_select(out=r4, in_=r4, compare_op=ALU.not_equal, fill=1.0, base=0, pattern=[[0, P // 4], [-1, 4]],
                                    channel_multiplier=1).then_inc(mask_ok, 1)
            pool.wait_ge(w_ok, 1)
            for gi in range(G):
                ch.inc(weigh(nc.gpsimd, gi, J - 1))
            ch.wait()
            ch.link(gather(nc.gpsimd, 1, J - 1))
            gather(nc.gpsimd, 2, J - 1).then_inc(last_ok, 1)

        @block.scalar
        def _(act):
            nc.scalar.activation(ss[:, :], g["ss"][:, :], ACT.Sqrt, scale=1.0 / D, bias=g["eps"][:, 0:1]).then_inc(rms, 1)
            split_hi(act, 0)
            for kt in range(KT):
                act.wait_ge(tr, kt + 1)
                nc.scalar.activation(xhi[:, kt, :], bank[kt][:, :], ACT.Copy).then_inc(xh_ok, 1)
            split_hi(act, 1)

            def transposed(u):
                act.wait_ge(t_done, u + 1)
                if u >= 2:
                    act.wait_ge(o_done, u - 1)
                nc.scalar.activation(pT[u % 2], bank[6][:, :], ACT.Copy).then_inc(pt_ok, 1)

            def attend(u):
                gi, hh, js = units[u]
                if u >= 1:
                    transposed(u - 1)
                act.wait_ge(max_ok, u + 1)
                if u >= 2:
                    act.wait_ge(t_done, u - 1)
                n = T // len(js)
                for i, j in enumerate(js):
                    ins = nc.scalar.activation(pr[u % 2][:, n * i:n * i + n], sm[u % 2][:, n * i:n * i + n], ACT.Exp,
                                               bias=negm[:, gi, j, hh:hh + 1], accum_out=lsum[:, gi, j, hh:hh + 1])
                ins.then_inc(p_ok, 1)

            for sl in range(NPROJ // 4):
                for kh in range(2):
                    for i in range(4):
                        if i == 1 and 1 <= 2 * sl + kh:
                            split_hi(act, 2 * sl + kh + 1)
                        u = 4 * sl + i
                        if kh == 1 and u % 2 == 0:
                            act.wait_ge(unit, u + 1)
                            nc.scalar.activation(projected(u), bank_of(u)[:, :], ACT.Copy).then_inc(ev_a, 1)
                        if beside(sl, kh, i) is not None:
                            attend(beside(sl, kh, i))
            for u in range(AH * (J + 1), NU):
                attend(u)
                if u == AH * (J + 1) + 1:
                    split_hi(act, NP + 1)
            transposed(NU - 1)
            act.wait_ge(d_ok, 1)
            nc.scalar.activation(negm[:, :, :, :], negm[:, :, :, :], ACT.Exp, scale=-1.0).then_inc(e_ok, 1)
            for b in range(4):
                act.wait_ge(otr, b + 1)
                nc.scalar.activation(oh[:, b, :], bank[b][:, :], ACT.Copy).then_inc(oh_ok, 1)
            for j in range(J):
                act.wait_ge(h_ok, J + j + 1)
                square_tile(nc, act, g, j, xhat[:, 0, :], squared)

        @block.vector
        def _(dve):
            V = nc.vector
            dve.wait_ge(rms, 1)
            V.reciprocal(rstd[:, :], ss[:, :]).then_inc(rstd_ok, 1)
            dve.wait_ge(rstd_ok, 1)
            for j in range(J):
                V.tensor_scalar(xhat[:, j, :], h[:, j, :], rstd[:, j:j + 1], None, ALU.mult).then_inc(xhat_ok, 1)
            split_lo(dve, 0)
            for kt in range(KT):
                dve.wait_ge(xh_ok, kt + 1)
                V.tensor_tensor(xlo[:, kt, :], bank[kt][:, :], xhi[:, kt, :].bitcast(fp32), ALU.subtract).then_inc(xl_ok, 1)
            split_lo(dve, 1)

            def output(u):
                gi, hh, js = units[u]
                dve.wait_ge(o_done, u + 1)
                src = bank[7][:, 0:HD * len(js)].rearrange("p (j v) -> p j v", j=len(js))
                V.tensor_copy(oacc[gi][:, js[0]:js[0] + len(js), HD * hh:HD * hh + HD], src).then_inc(o_ev, 1)

            def attend(u):
                gi, hh, js = units[u]
                dve.wait_ge(s_done, u + 1)
                if u >= 2:
                    dve.wait_ge(p_ok, u - 1)
                scores = bank[4 + u % 2]
                if gi == 0:
                    V.scalar_tensor_tensor(out=sm[u % 2], in0=scores[:, :], scalar=SCALE, in1=mask[0][:, js[0], :], op0=ALU.mult, op1=ALU.add).then_inc(sm_ok, 1)
                    dve.wait_ge(sm_ok, u + 1)
                    V.tensor_reduce(out=negm[:, gi, js[0], hh:hh + 1], in_=sm[u % 2], axis=AX.X, op=ALU.max, negate=True).then_inc(max_ok, 1)
                else:
                    v3 = lambda x: x.rearrange("p (j t) -> p j t", j=J)
                    V.scalar_tensor_tensor(out=v3(sm[u % 2]), in0=v3(scores[:, :]), scalar=SCALE,
                                           in1=mask[gi][:, :].rearrange("p (x t) -> p x t", x=1).to_broadcast([P, J, P]), op0=ALU.mult, op1=ALU.add).then_inc(sm_ok, 1)
                    dve.wait_ge(sm_ok, u + 1)
                    V.tensor_reduce(out=negm[:, gi, :, hh], in_=v3(sm[u % 2]), axis=AX.X, op=ALU.max, negate=True).then_inc(max_ok, 1)
                if u >= 2:
                    output(u - 2)

            dve.wait_ge(mask_ok, 1)
            for sl in range(NPROJ // 4):
                for kh in range(2):
                    for i in range(4):
                        if i == 1 and 1 <= 2 * sl + kh:
                            split_lo(dve, 2 * sl + kh + 1)
                        u = 4 * sl + i
                        if kh == 1 and u % 2:
                            dve.wait_ge(unit, u + 1)
                            V.tensor_copy(projected(u), bank_of(u)[:, :]).then_inc(ev_d, 1)
                        if beside(sl, kh, i) is not None:
                            attend(beside(sl, kh, i))
            ch = Chain(dve, order)
            dve.wait_ge(res_mm, 1)
            ch.link(V.tensor_tensor(mask[2][:, :], bank[0][:, 0:P], mask[2][:, :], ALU.mult))
            ch.link(V.tensor_scalar(mask[2][:, :], mask[2][:, :], 1.0, -FAR, ALU.subtract, ALU.mult))
            for u in range(AH * (J + 1), NU):
                attend(u)
                if u == AH * (J + 1) + 1:
                    split_lo(dve, NP + 1)
            output(NU - 2)
            output(NU - 1)
            dve.wait_ge(p_ok, NU)
            dve.wait_ge(max_ok, NU)
            ch.link(V.tensor_tensor(least[:, :, :], negm[:, 0, :, :], negm[:, 1, :, :], ALU.min))
            ch.link(V.tensor_tensor(least[:, :, :], least[:, :, :], negm[:, 2, :, :], ALU.min))
            for gi in range(G):
                ins = V.tensor_tensor(negm[:, gi, :, :], negm[:, gi, :, :], least[:, :, :], ALU.subtract)
                if gi < G - 1:
                    ch.inc(ins)
                else:
                    ch.wait()
                    ins.then_inc(d_ok, 1)
            dve.wait_ge(e_ok, 1)
            for gi in range(G):
                ch.link(V.tensor_tensor(lsum[:, gi, :, :], lsum[:, gi, :, :], negm[:, gi, :, :], ALU.mult))
            ch.link(V.tensor_tensor(den[:, :, :], lsum[:, 0, :, :], lsum[:, 1, :, :], ALU.add))
            ch.link(V.tensor_tensor(den[:, :, :], den[:, :, :], lsum[:, 2, :, :], ALU.add))
            ch.link(V.reciprocal(den[:, :, :], den[:, :, :]))
            for gi in range(G):
                ch.link(V.tensor_tensor(negm[:, gi, :, :], negm[:, gi, :, :], den[:, :, :], ALU.mult))
            dve.wait_ge(o_ev, NU)
            ch.wait()
            V.memset(residue[:, 0:1], 0.0).then_inc(w_ok, 1)
            for gi in range(G):
                for j in range(J - 1):
                    ch.inc(weigh(nc.vector, gi, j))
            for gi in range(1, G):
                ch.wait()
                for j in range(J - 1):
                    ins = gather(nc.vector, gi, j)
                    ins.then_inc(comb_ok, 1) if gi == G - 1 else ch.inc(ins)
            for b in range(4):
                dve.wait_ge(oh_ok, b + 1)
                V.tensor_tensor(ol[:, b, :], bank[b][:, :], oh[:, b, :].bitcast(fp32), ALU.subtract).then_inc(ol_ok, 1)
            for u in range(2 * J):
                dve.wait_ge(out_done, u + 1)
                hh = h[:, u % J, 512 * (u // J):512 * (u // J) + 512]
                V.tensor_tensor(hh, bank[u][:, :], hh, ALU.add).then_inc(h_ok, 1)

        @block.tensor
        def _(pe):
            for j in range(J):
                pe.wait_ge(xhat_ok, j + 1)
                for kt in range(KT):
                    ins = nc.tensor.transpose(bank[kt][:, P * j:P * j + P], xhat[:, j, P * kt:P * kt + P], g["ident"][:, :])
                    if j == J - 1:
                        ins.then_inc(tr, 1)
            def three_passes(out, a, b, begin, end):
                nc.tensor.matmul(out, a[0], b[0], start=begin, stop=False)
                nc.tensor.matmul(out, a[0], b[1], start=False, stop=False)
                return nc.tensor.matmul(out, a[1], b[0], start=False, stop=end)

            def scores(u):
                gi, hh, js = units[u]
                rows = slice(HD * (hh % 2), HD * (hh % 2) + HD)
                if u >= 2:
                    pe.wait_ge(sm_ok, u - 1)
                b = bank[4 + u % 2]
                for i, j in enumerate(js):
                    q = qT[gi][rows, hh // 2, P * j:P * j + P]
                    out, k = (b[:, :], kT[gi][rows, hh // 2, :]) if gi == 0 else (b[:, P * i:P * i + P], kT[gi][rows, hh // 2, P * j:P * j + P])
                    ins = nc.tensor.matmul(out, q, k, start=True, stop=True)
                ins.then_inc(s_done, 1)

            def transposes(u):
                pe.wait_ge(p_ok, u + 1)
                if u >= 1:
                    pe.wait_ge(pt_ok, u)
                for i in range(J):
                    ins = nc.tensor.transpose(bank[6][:, P * i:P * i + P], pr[u % 2][:, P * i:P * i + P], g["ident"][:, :])
                ins.then_inc(t_done, 1)

            def values(u):
                gi, hh, js = units[u]
                pe.wait_ge(pt_ok, u + 1)
                if u >= 1:
                    pe.wait_ge(o_ev, u)
                for i in range(J):
                    out = bank[7][:, 0:HD] if gi == 0 else bank[7][:, HD * i:HD * i + HD]
                    ins = nc.tensor.matmul(out, pT[u % 2][:, P * i:P * i + P], vv[gi][:, i, HD * hh:HD * hh + HD],
                                           start=gi > 0 or i == 0, stop=gi > 0 or i == J - 1)
                ins.then_inc(o_done, 1)

            def attend(u):
                scores(u)
                if u >= 2:
                    values(u - 2)
                if u >= 1:
                    transposes(u - 1)

            for n, (gi, kind, kh) in enumerate(pieces):
                pe.wait_ge(lo_ok, n + 1)
                for i in range(4):
                    sl = n // 2
                    u = sl * 4 + i
                    if kh == 0:
                        if u >= 8:
                            evacuated(pe, u - 8 if u < 4 * BESIDE else u - 4)
                        elif u == 0:
                            pe.wait_ge(xl_ok, KT)
                    for k in range(4):
                        x = [v[:, 4 * kh + k, P * i:P * i + P] if kind == 2 else v[:, 4 * kh + k, :] for v in (xhi, xlo)]
                        w = [v[n % 2][:, k, :] if kind == 2 else v[n % 2][:, k, P * i:P * i + P] for v in (whi, wlo)]
                        a, c = (x, w) if kind == 2 else (w, x)
                        last = three_passes(bank_of(u)[:, :], a, c, kh == 0 and k == 0, kh == 1 and k == 3)
                    if kh == 1:
                        last.then_inc(unit, 1)
                    elif i == 3:
                        last.then_inc(piece_used, 1)
                    v = beside(sl, kh, i)
                    if v is not None:
                        if v in (0, AH * J):
                            for w in (2, 1):
                                evacuated(pe, 12 * (v // (AH * J) + 1) - w)
                        attend(v)
            pe.wait_ge(mask_ok, 1)
            pe.wait_ge(ev_a, NPROJ // 2)
            pe.wait_ge(ev_d, NPROJ // 2)
            nc.tensor.matmul(bank[0][:, 0:P], residue[:, :], residue[:, :], start=True, stop=True).then_inc(res_mm, 1)
            for u in range(AH * (J + 1), NU):
                attend(u)
            values(NU - 2)
            transposes(NU - 1)
            values(NU - 1)
            for j in range(J):
                if j < J - 1:
                    pe.wait_ge(comb_ok, j + 1)
                else:
                    pe.wait_ge(last_ok, 1)
                for b in range(W // P):
                    ins = nc.tensor.transpose(bank[b][:, P * j:P * j + P], oacc[0][:, j, P * b:P * b + P], g["ident"][:, :])
                    if j == J - 1:
                        ins.then_inc(otr, 1)
            pe.wait_ge(oh_ok, W // P)
            pe.wait_ge(ol_ok, W // P)
            pe.wait_ge(lo_ok, NP + 2)
            for u in range(2 * J):
                half, j = u // J, u % J
                for kt in range(W // P):
                    ins = three_passes(bank[u][:, :], [v[:, kt, P * j:P * j + P] for v in (oh, ol)], [v[half][:, kt, :] for v in (whi, wlo)], kt == 0, kt == W // P - 1)
                ins.then_inc(out_done, 1)


def final_norm(nc, io, g, out):
    h = g["h"]
    with Scope(nc, "final") as s:
        gb = s.sb("gb", [P, D])
        ss, rstd = s.sb("ss", [P, J]), s.sb("rstd", [P, J])
        g_in, rms, rstd_ok, done, stored = map(s.sem, ["g_in", "rms", "rstd_ok", "done", "stored"])
        block = s.enter_context(nc.Block())

        @block.sync
        def _(sp):
            sp.dma_start(gb[:, :], io["final_norm_g"].rearrange("(a d) -> a d", a=1).to_broadcast([P, D])).then_inc(g_in, 16)
            for j in range(J):
                sp.wait_ge(done, j + 1)
                sp.dma_start(out[0].rearrange("(p j) d -> p j d", j=J)[:, j, :], h[:, j, :]).then_inc(stored, 16)
            sp.wait_ge(stored, 16 * J)

        @block.scalar
        def _(act):
            nc.scalar.activation(ss[:, :], g["ss"][:, :], ACT.Sqrt, scale=1.0 / D, bias=g["eps"][:, 0:1]).then_inc(rms, 1)

        @block.vector
        def _(dve):
            dve.wait_ge(rms, 1)
            nc.vector.reciprocal(rstd[:, :], ss[:, :]).then_inc(rstd_ok, 1)
            dve.wait_ge(rstd_ok, 1)
            dve.wait_ge(g_in, 16)
            for j in range(J):
                nc.vector.scalar_tensor_tensor(out=h[:, j, :], in0=h[:, j, :], scalar=rstd[:, j:j + 1], in1=gb[:, :], op0=ALU.mult, op1=ALU.mult).then_inc(done, 1)


def build(nc, io, out):
    top = Scope(nc, "all")
    with top:
        g = {
            "ident": top.sb("ident", [P, P]), "par": top.sb("par", [P, P]), "eps": top.sb("eps", [P, 2]),
            "blockones": top.sb("blockones", [P, P]), "chmask": top.sb("chmask", [P, P]), "upper": top.sb("upper", [P, P]), "ones": top.sb("ones", [P, P]), "h": top.sb("h", [P, J, D]),
            "ident2": top.sb("ident2", [P, C]), "down4": top.sb("down4", [P, 4]), "base16": top.sb("base16", [P, 16]), "tokid": top.sb("tokid", [P, J]), "ints": top.sb("ints", [P, 16], i32), "lowmask": top.sb("lowmask", [C, C]), "bonus": top.sb("bonus", [P, J, H]), "ss": top.sb("ss", [P, J]),
            "bank": [top.ps(f"bank{i}", [P, 512]) for i in range(8)],
            "ready": top.sem("constants_ready"),
        }
        io["g_dram"] = nc.dram_tensor("g_dram", [T, D], fp32).ap()
        for i in range(2):
            io[f"xn_dram{i}"] = nc.dram_tensor(f"xn_dram{i}", [T, D], fp32).ap()
            io[f"tok_dram{i}"] = nc.dram_tensor(f"tok_dram{i}", [16 * T, 1], fp32).ap()
            io[f"out_dram{i}"] = nc.dram_tensor(f"out_dram{i}", [16 * T, D], fp32).ap()
        io["y_dram"] = nc.dram_tensor("y_dram", [T, D], fp32).ap()
        io["v_dram"] = nc.dram_tensor("v_dram", [T, D], fp32).ap()
        with nc.Block() as block:
            @block.gpsimd
            def _(pool):
                ch = Chain(pool, g["ready"])
                ones = lambda name, v=1.0: ch.inc(nc.gpsimd.memset(g[name][:, :], v))
                ones("ident", 0.0)
                ones("blockones", 0.0)
                for name in ["upper", "chmask", "lowmask", "ones"]:
                    ones(name)
                ch.inc(nc.gpsimd.memset(g["eps"][:, 0:1], NORM_EPS))
                ch.link(nc.gpsimd.memset(g["eps"][:, 1:2], GN_EPS))

                def keep(m, fill, op, base, step, per_partition):
                    ch.link(nc.gpsimd.affine_select(out=m, in_=m, compare_op=op, fill=fill, base=base,
                                                    pattern=[[step, m.shape[1]]], channel_multiplier=per_partition))

                for name, n, step, base, per_partition in (("down4", 4, -1, 4, 0), ("base16", 16, P, 0, 0), ("tokid", J, 1, 0, J)):
                    ch.link(nc.gpsimd.iota(g["ints"][:, 0:n], pattern=[[step, n]], base=base, channel_multiplier=per_partition))
                    ch.link(nc.gpsimd.tensor_copy(g[name][:, :], g["ints"][:, 0:n]))
                keep(g["ident"][:, :], 1.0, ALU.not_equal, 0, -1, 1)
                keep(g["upper"][:, :], 0.0, ALU.is_ge, -1, 1, -1)
                for rows, base in ((P, C), (C, 0)):
                    for x in range(2):
                        keep(g["chmask"][0:rows, C * x:C * x + C], 0.0, ALU.is_ge, base - 1 + x, 1, -1)
                keep(g["lowmask"][:, :], 0.0, ALU.is_ge, -1, -1, 1)
                for i in range(2):
                    ch.link(nc.gpsimd.tensor_copy(g["ident2"][HD * i:HD * i + HD, :], g["ident"][HD * i:HD * i + HD, HD * i:HD * i + HD]))
                    ch.link(nc.gpsimd.memset(g["blockones"][HD * i:HD * i + HD, HD * i:HD * i + HD], 1.0))

        with Scope(nc, "rwkv") as s:
            rw = {n: s.sb("rw_" + n, [P, KT, T]) for n in "rkwa"}
            rwkv_project(nc, io, g, rw)
            for x in ["n", "e1", "e2", "tmp"]:
                rw[x] = s.sb("rw_" + x, [P, KT, T])
            rw["pc"] = s.sb("rw_pc", [C, NC, H])
            rwkv_operands(nc, io, g, rw)
            rwkv_chunks(nc, io, g, rw)
            rwkv_finish(nc, io, g, rw)
        moe(nc, io, g, 0)
        attention(nc, io, g)
        moe(nc, io, g, 1)
        final_norm(nc, io, g, out)


_INS = ["x", "norm_mix_g", "norm_ffn_g", "rwkv_mu", "rwkv_w_r", "rwkv_w_k", "rwkv_w_v", "rwkv_w0", "rwkv_w1", "rwkv_w2",
        "rwkv_a0", "rwkv_a1", "rwkv_a2", "rwkv_g1", "rwkv_g2", "rwkv_k_k", "rwkv_k_a", "rwkv_r_k", "rwkv_ln_w", "rwkv_ln_b",
        "rwkv_w_o", "kv_norm_g", "w_kv", "attn_w_q", "attn_w_o", "moe_w_grp", "moe_b_grp", "moe_w_exp", "moe_b_exp",
        "moe_w_gate", "moe_w_up", "moe_w_down", "final_norm_g"]


def kernel(**inputs):
    import numpy as _np
    import concourse.bacc as _bacc
    from concourse import mybir as _mybir
    from concourse.bass_utils import run_bass_kernel_spmd as _run

    nc = _bacc.Bacc("TRN2", target_bir_lowering=False, num_devices=1)
    arrays, io = {}, {}
    for name in _INS:
        a = _np.ascontiguousarray(inputs[name])
        arrays[f"in_{name}_dram"] = a
        io[name] = nc.dram_tensor(f"in_{name}_dram", a.shape, _mybir.dt.from_np(a.dtype), kind="ExternalInput").ap()
    out = nc.dram_tensor("out_0_dram", (1, T, D), _mybir.dt.float32, kind="ExternalOutput").ap()
    build(nc, io, out)
    r = _run(nc, [arrays], core_ids=[0])
    return r.results[0]["out_0_dram"]
```
